# Optimizing a Trainium2 kernel written in Bass

```python
import jax
import jax.numpy as jnp
from jax import lax
import numpy as np
import math
import jax, jax.numpy as jnp

D_MODEL = 1024
BATCH = 1
SEQ = 512
DEPTH = 2

N_META = 16
NORM_EPS = 1e-6
SSM_D_INNER = 2 * D_MODEL
SSM_HEAD_DIM = 64
SSM_HEADS = SSM_D_INNER // SSM_HEAD_DIM
SSM_GROUPS = 4
SSM_HEADS_PER_GROUP = SSM_HEADS // SSM_GROUPS
SSM_STATE = 128
SSM_CONV = 4
SSM_CHUNK = 256
SSM_CONV_DIM = SSM_D_INNER + 2 * SSM_GROUPS * SSM_STATE
SSM_IN_DIM = SSM_D_INNER + SSM_CONV_DIM + SSM_HEADS
SB_HEAD_DIM = 64
SB_HEADS = D_MODEL // SB_HEAD_DIM
SB_WIDTH = SB_HEADS * SB_HEAD_DIM
SB_Q_BLOCK = 128
D_FF = 256 * ((8 * D_MODEL // 3 + 255) // 256)
FFN_CONV = 3


def _rmsnorm(x, g):
    x32 = x.astype(jnp.float32)
    y = x32 * lax.rsqrt(jnp.mean(x32 * x32, axis=-1, keepdims=True) + NORM_EPS)
    return (y * g.astype(jnp.float32)).astype(x.dtype)

def _causal_dwconv(x, w, bias):
    width = w.shape[0]
    L = x.shape[1]
    xp = jnp.pad(x, ((0, 0), (width - 1, 0), (0, 0)))
    y = xp[:, 0:L] * w[0] + bias
    for k in range(1, width):
        y = y + xp[:, k:k + L] * w[k]
    return y

def _ssd_mixer(u, w_in, conv_w, conv_b, dt_bias, a_log, d_skip, gate_g, w_out):
    b, L, _ = u.shape
    G, E, P, N, Q = SSM_GROUPS, SSM_HEADS_PER_GROUP, SSM_HEAD_DIM, SSM_STATE, SSM_CHUNK
    f32 = jnp.float32
    z, xbc, dt_raw = jnp.split(u @ w_in, [SSM_D_INNER, SSM_D_INNER + SSM_CONV_DIM], axis=-1)
    xbc = jax.nn.silu(_causal_dwconv(xbc, conv_w, conv_b))
    xs, b_in, c_in = jnp.split(xbc, [SSM_D_INNER, SSM_D_INNER + G * N], axis=-1)
    dt = jax.nn.softplus(dt_raw.astype(f32) + dt_bias.astype(f32))
    a = -jnp.exp(a_log.astype(f32))
    pf = (-N_META) % Q
    pe = (-(pf + L)) % Q
    nc = (pf + L + pe) // Q

    def to_chunks(t, tail):
        return jnp.pad(t, ((0, 0), (pf, pe), (0, 0))).reshape((b, nc, Q) + tail)

    x_c = to_chunks(xs, (G, E, P)).astype(f32)
    b_c = to_chunks(b_in, (G, N)).astype(f32)
    c_c = to_chunks(c_in, (G, N)).astype(f32)
    dt_c = to_chunks(dt, (G, E))
    xdt = x_c * dt_c[..., None]
    a_cs = jnp.cumsum(jnp.transpose(dt_c * a.reshape(G, E), (0, 3, 4, 1, 2)), axis=-1)
    causal = jnp.tril(jnp.ones((Q, Q), dtype=bool))
    decay_in = jnp.exp(jnp.where(causal, a_cs[..., :, None] - a_cs[..., None, :], -jnp.inf))
    cb = jnp.einsum('bclgn,bcsgn->bgcls', c_c, b_c)
    y_diag = jnp.einsum('bgcls,bgecls,bcsgep->bclgep', cb, decay_in, xdt)
    decay_to_end = jnp.exp(a_cs[..., -1:] - a_cs)
    chunk_states = jnp.einsum('bclgn,bgecl,bclgep->cbgepn', b_c, decay_to_end, xdt)
    chunk_decay = jnp.moveaxis(jnp.exp(a_cs[..., -1]), -1, 0)

    def step(state, inp):
        s_new, d = inp
        return state * d[..., None, None] + s_new, state

    _, prev_states = lax.scan(step, jnp.zeros((b, G, E, P, N), f32), (chunk_states, chunk_decay))
    y_off = jnp.einsum('bclgn,cbgepn,bgecl->bclgep', c_c, prev_states, jnp.exp(a_cs))
    y = (y_diag + y_off).reshape(b, nc * Q, SSM_D_INNER)[:, pf:pf + L]
    y = y + (xs.reshape(b, L, SSM_HEADS, P).astype(f32) * d_skip.astype(f32)[:, None]).reshape(b, L, SSM_D_INNER)
    hg = (y * jax.nn.silu(z.astype(f32))).reshape(b, L, G, SSM_D_INNER // G)
    hg = hg * lax.rsqrt(jnp.mean(hg * hg, axis=-1, keepdims=True) + NORM_EPS)
    hg = hg.reshape(b, L, SSM_D_INNER) * gate_g.astype(f32)
    return hg.astype(u.dtype) @ w_out

def _stick_breaking_attention(q, k, v):
    b, L, H, Dh = q.shape
    lp = -(-L // SB_Q_BLOCK) * SB_Q_BLOCK
    pad = ((0, 0), (0, lp - L), (0, 0), (0, 0))
    q, k, v = jnp.pad(q, pad), jnp.pad(k, pad), jnp.pad(v, pad)
    scale = Dh ** -0.5
    outs = []
    for i in range(lp // SB_Q_BLOCK):
        t0, t1 = i * SB_Q_BLOCK, (i + 1) * SB_Q_BLOCK
        logits = jnp.einsum('bthd,bshd->bhts', q[:, t0:t1], k[:, :t1]).astype(jnp.float32) * scale
        t_idx = t0 + jnp.arange(SB_Q_BLOCK)[:, None]
        s_idx = jnp.arange(t1)[None, :]
        visible = s_idx < t_idx
        log_keep = jnp.where(visible, jax.nn.log_sigmoid(-logits), 0.0)
        later = lax.cumsum(log_keep, axis=3, reverse=True) - log_keep
        log_w = jnp.where(visible, jax.nn.log_sigmoid(logits) + later, -jnp.inf)
        w = jnp.exp(log_w).astype(v.dtype)
        outs.append(jnp.einsum('bhts,bshd->bthd', w, v[:, :t1]))
    return jnp.concatenate(outs, axis=1)[:, :L]

def _conv_ffn(u, w_up, conv_w, conv_b, w_down):
    h = _causal_dwconv(u @ w_up, conv_w, conv_b)
    g, val = jnp.split(h, 2, axis=-1)
    return (jax.nn.silu(g) * val) @ w_down

def first_inputs(seed: int = 0) -> dict:
    key = jax.random.key(seed)
    ks = jax.random.split(key, 32)
    n_a = DEPTH // 2
    n_b = DEPTH - n_a
    f32 = jnp.float32

    def nrm(k, shape, scale):
        return jax.random.normal(k, shape, f32) * scale

    def gain(k, shape):
        return 1.0 + 0.02 * jax.random.normal(k, shape, f32)

    dt0 = jnp.exp(jax.random.uniform(ks[6], (n_a, SSM_HEADS), f32, np.log(1e-3), np.log(1e-1)))
    dt_bias = dt0 + jnp.log(-jnp.expm1(-dt0))
    return {
        'x': jax.random.normal(ks[0], (BATCH, SEQ, D_MODEL), f32),
        'meta_tokens': nrm(ks[1], (N_META, D_MODEL), 1.0),
        'ssd_norm': gain(ks[2], (n_a, D_MODEL)),
        'ssd_w_in': nrm(ks[3], (n_a, D_MODEL, SSM_IN_DIM), D_MODEL ** -0.5),
        'ssd_conv_w': nrm(ks[4], (n_a, SSM_CONV, SSM_CONV_DIM), SSM_CONV ** -0.5),
        'ssd_conv_b': nrm(ks[5], (n_a, SSM_CONV_DIM), 0.02),
        'ssd_dt_bias': dt_bias,
        'ssd_a_log': jnp.log(jax.random.uniform(ks[7], (n_a, SSM_HEADS), f32, 1.0, 16.0)),
        'ssd_d_skip': jax.random.uniform(ks[8], (n_a, SSM_HEADS), f32, 0.5, 1.5),
        'ssd_gate_norm': gain(ks[9], (n_a, SSM_D_INNER)),
        'ssd_w_out': nrm(ks[10], (n_a, SSM_D_INNER, D_MODEL), SSM_D_INNER ** -0.5),
        'kv_norm': gain(ks[11], (D_MODEL,)),
        'w_kv': nrm(ks[12], (D_MODEL, 2 * SB_WIDTH), D_MODEL ** -0.5),
        'sb_norm': gain(ks[13], (n_b, D_MODEL)),
        'sb_w_q': nrm(ks[14], (n_b, D_MODEL, SB_WIDTH), D_MODEL ** -0.5),
        'sb_w_o': nrm(ks[15], (n_b, SB_WIDTH, D_MODEL), SB_WIDTH ** -0.5),
        'ffn_norm': gain(ks[16], (DEPTH, D_MODEL)),
        'ffn_w_up': nrm(ks[17], (DEPTH, D_MODEL, 2 * D_FF), D_MODEL ** -0.5),
        'ffn_conv_w': nrm(ks[18], (DEPTH, FFN_CONV, 2 * D_FF), FFN_CONV ** -0.5),
        'ffn_conv_b': nrm(ks[19], (DEPTH, 2 * D_FF), 0.02),
        'ffn_w_down': nrm(ks[20], (DEPTH, D_FF, D_MODEL), D_FF ** -0.5),
        'final_norm': gain(ks[21], (D_MODEL,)),
    }

def first_block(x, meta_tokens, ssd_norm, ssd_w_in, ssd_conv_w, ssd_conv_b, ssd_dt_bias, ssd_a_log,
              ssd_d_skip, ssd_gate_norm, ssd_w_out, kv_norm, w_kv, sb_norm, sb_w_q, sb_w_o,
              ffn_norm, ffn_w_up, ffn_conv_w, ffn_conv_b, ffn_w_down, final_norm):
    b = x.shape[0]
    n_a = DEPTH // 2
    h = jnp.concatenate([jnp.broadcast_to(meta_tokens[None], (b, N_META, D_MODEL)).astype(x.dtype), x], axis=1)
    L = h.shape[1]
    k_shared = None
    v_shared = None
    for layer in range(DEPTH):
        if layer < n_a:
            h = h + _ssd_mixer(_rmsnorm(h, ssd_norm[layer]), ssd_w_in[layer], ssd_conv_w[layer],
                               ssd_conv_b[layer], ssd_dt_bias[layer], ssd_a_log[layer],
                               ssd_d_skip[layer], ssd_gate_norm[layer], ssd_w_out[layer])
        else:
            if layer == n_a:
                kv = _rmsnorm(h, kv_norm) @ w_kv
                k_shared, v_shared = jnp.split(kv.reshape(b, L, 2, SB_HEADS, SB_HEAD_DIM), 2, axis=2)
                k_shared, v_shared = k_shared[:, :, 0], v_shared[:, :, 0]
            j = layer - n_a
            q = (_rmsnorm(h, sb_norm[j]) @ sb_w_q[j]).reshape(b, L, SB_HEADS, SB_HEAD_DIM)
            o = _stick_breaking_attention(q, k_shared, v_shared).reshape(b, L, SB_WIDTH)
            h = h + o @ sb_w_o[j]
        h = h + _conv_ffn(_rmsnorm(h, ffn_norm[layer]), ffn_w_up[layer], ffn_conv_w[layer],
                          ffn_conv_b[layer], ffn_w_down[layer])
    return _rmsnorm(h, final_norm)[:, N_META:]


HEAD_DIM = 64
FOX_HEADS = 8
RET_HEADS = 8
FOX_WIDTH = FOX_HEADS * HEAD_DIM
RET_WIDTH = RET_HEADS * HEAD_DIM
EVEN_MIX_WIDTH = FOX_WIDTH + RET_WIDTH
FOX_Q_BLOCK = 128
RET_CHUNK = 128
EVEN_SIZES = (FOX_WIDTH, FOX_WIDTH, FOX_WIDTH, FOX_HEADS, RET_WIDTH, RET_WIDTH, RET_WIDTH, EVEN_MIX_WIDTH)
EVEN_IN = sum(EVEN_SIZES)
EVEN_SPLITS = tuple(int(v) for v in np.cumsum(EVEN_SIZES)[:-1])
NSA_HEADS = 16
NSA_KV_GROUPS = 4
NSA_HEADS_PER_GROUP = NSA_HEADS // NSA_KV_GROUPS
NSA_WIDTH = NSA_HEADS * HEAD_DIM
NSA_KV_WIDTH = NSA_KV_GROUPS * HEAD_DIM
N_BRANCH = 3
CMP_BLOCK = 32
CMP_STRIDE = 16
CMP_HIDDEN = 256
SLC_BLOCK = 64
SLC_TOPK = 16
WINDOW = 512
NSA_Q_BLOCK = 64
ODD_SIZES = (NSA_WIDTH,) + (NSA_KV_WIDTH,) * 6 + (NSA_HEADS * N_BRANCH, NSA_WIDTH)
ODD_IN = sum(ODD_SIZES)
ODD_SPLITS = tuple(int(v) for v in np.cumsum(ODD_SIZES)[:-1])

RMS_EPS = 1e-6
GN_EPS = 1e-5
NEG = -1e30
FORCE_BONUS = 1e6


def rms_norm(x, g):
    xf = x.astype(jnp.float32)
    y = xf * lax.rsqrt(jnp.mean(xf * xf, axis=-1, keepdims=True) + RMS_EPS)
    return (y * g.astype(jnp.float32)).astype(x.dtype)

def masked_softmax(s, mask):
    s = jnp.where(mask, s, NEG)
    p = jax.nn.softmax(s, axis=-1)
    return jnp.where(mask, p, 0.0)

def alibi_slopes(n):
    return jnp.asarray(2.0 ** (-8.0 * (np.arange(n) + 1) / n), jnp.float32)

def fox_attention(q, k, v, f_logit):
    B, S, H, d = q.shape
    nb = S // FOX_Q_BLOCK
    scale = d ** -0.5
    c = jnp.cumsum(jax.nn.log_sigmoid(f_logit.astype(jnp.float32)), axis=1)
    c_h = c.transpose(0, 2, 1)
    kh = k.transpose(0, 2, 1, 3)
    vh = v.transpose(0, 2, 1, 3)
    qb = q.reshape(B, nb, FOX_Q_BLOCK, H, d).transpose(1, 0, 3, 2, 4)
    cb = c.reshape(B, nb, FOX_Q_BLOCK, H).transpose(1, 0, 3, 2)
    key_pos = jnp.arange(S)

    def block(args):
        qi, ci, bi = args
        t = bi * FOX_Q_BLOCK + jnp.arange(FOX_Q_BLOCK)
        s = jnp.einsum('bhqd,bhkd->bhqk', qi, kh).astype(jnp.float32) * scale
        s = s + ci[..., None] - c_h[:, :, None, :]
        p = masked_softmax(s, key_pos[None, :] <= t[:, None])
        return jnp.einsum('bhqk,bhkd->bhqd', p.astype(vh.dtype), vh)

    o = lax.map(block, (qb, cb, jnp.arange(nb)))
    return o.transpose(1, 0, 3, 2, 4).reshape(B, S, H, d)

def retention_decays(n_heads, chunk):
    lg = np.log(1.0 - 2.0 ** (-5.0 - np.arange(n_heads)))
    i = np.arange(chunk)
    diff = i[:, None] - i[None, :]
    inner = np.where(diff[None] >= 0, np.exp(lg[:, None, None] * np.maximum(diff, 0)[None]), 0.0)
    cross = np.exp(lg[:, None] * (i[None, :] + 1))
    kdec = np.exp(lg[:, None] * (chunk - 1 - i)[None, :])
    cdec = np.exp(lg * chunk)
    return (jnp.asarray(inner, jnp.float32), jnp.asarray(cross, jnp.float32),
            jnp.asarray(kdec, jnp.float32), jnp.asarray(cdec, jnp.float32))

def retention(q, k, v):
    B, S, H, d = q.shape
    n = S // RET_CHUNK
    inner, cross, kdec, cdec = retention_decays(H, RET_CHUNK)

    def chunks(a):
        return a.astype(jnp.float32).reshape(B, n, RET_CHUNK, H, d).transpose(1, 0, 3, 2, 4)

    qc, kc, vc = chunks(q), chunks(k) * (d ** -0.5), chunks(v)

    def step(state, xs):
        qi, ki, vi = xs
        a = jnp.einsum('bhid,bhjd->bhij', qi, ki) * inner
        o = jnp.einsum('bhij,bhje->bhie', a, vi) + jnp.einsum('bhid,bhde->bhie', qi, state) * cross[None, :, :, None]
        state = state * cdec[None, :, None, None] + jnp.einsum('bhjd,bhje->bhde', ki * kdec[None, :, :, None], vi)
        return state, o

    _, o = lax.scan(step, jnp.zeros((B, H, d, d), jnp.float32), (qc, kc, vc))
    o = o.transpose(1, 0, 3, 2, 4).reshape(B, S, H, d)
    mu = jnp.mean(o, axis=-1, keepdims=True)
    var = jnp.mean(jnp.square(o - mu), axis=-1, keepdims=True)
    return ((o - mu) * lax.rsqrt(var + GN_EPS)).reshape(B, S, H * d)

def even_layer(x, norm_g, w_in, b_f, gn_g, w_out):
    B, S, _ = x.shape
    h = rms_norm(x, norm_g)
    u = h @ w_in
    q_f, k_f, v_f, f_l, q_r, k_r, v_r, z = jnp.split(u, EVEN_SPLITS, axis=-1)
    hd = lambda a, n: a.reshape(B, S, n, HEAD_DIM)
    o_f = fox_attention(hd(q_f, FOX_HEADS), hd(k_f, FOX_HEADS), hd(v_f, FOX_HEADS), f_l + b_f)
    o_f = o_f.reshape(B, S, FOX_WIDTH)
    o_r = (retention(hd(q_r, RET_HEADS), hd(k_r, RET_HEADS), hd(v_r, RET_HEADS)) * gn_g).astype(x.dtype)
    y = jnp.concatenate([o_f, o_r], axis=-1) * jax.nn.silu(z)
    return x + y @ w_out

def compress_blocks(a, idx, pe, w1, w2):
    B = a.shape[0]
    nc, l = idx.shape
    ab = a[:, idx] + pe[None, None, :, None, :]
    ab = ab.transpose(0, 1, 3, 2, 4).reshape(B, nc, NSA_KV_GROUPS, l * HEAD_DIM)
    return jax.nn.silu(ab @ w1) @ w2

def nsa_attention(q, kc, vc, ks, vs, kw, vw, gate_logit, pe_k, pe_v, wk1, wk2, wv1, wv2):
    B, S, H, d = q.shape
    G, Hg, QB = NSA_KV_GROUPS, NSA_HEADS_PER_GROUP, NSA_Q_BLOCK
    scale = d ** -0.5
    dtype = q.dtype
    nc = (S - CMP_BLOCK) // CMP_STRIDE + 1
    idx = np.arange(nc)[:, None] * CMP_STRIDE + np.arange(CMP_BLOCK)[None, :]
    cmp_end = jnp.asarray(idx[:, -1], jnp.int32)
    k_cmp = compress_blocks(kc, idx, pe_k, wk1, wk2)
    v_cmp = compress_blocks(vc, idx, pe_v, wv1, wv2)
    ns = S // SLC_BLOCK
    topk = min(SLC_TOPK, ns)
    c0 = np.arange(nc)[:, None] * CMP_STRIDE
    s0 = np.arange(ns)[None, :] * SLC_BLOCK
    overlap = np.clip(np.minimum(c0 + CMP_BLOCK, s0 + SLC_BLOCK) - np.maximum(c0, s0), 0, None)
    cmp_to_slc = jnp.asarray(overlap / CMP_STRIDE, jnp.float32)
    slopes = alibi_slopes(H).reshape(G, Hg)[None, :, :, None, None]
    ks_g = ks.transpose(0, 2, 1, 3)
    vs_g = vs.transpose(0, 2, 1, 3)
    kw_pad = jnp.pad(kw, ((0, 0), (WINDOW, 0), (0, 0), (0, 0)))
    vw_pad = jnp.pad(vw, ((0, 0), (WINDOW, 0), (0, 0), (0, 0)))
    nqb = S // QB
    qb = q.reshape(B, nqb, QB, G, Hg, d).transpose(1, 0, 2, 3, 4, 5)
    gb = gate_logit.reshape(B, nqb, QB, G, Hg, N_BRANCH).transpose(1, 0, 2, 3, 4, 5)
    b_idx = jnp.arange(B)[:, None, None, None]
    g_idx = jnp.arange(G)[None, :, None, None]
    blk = jnp.arange(ns)

    def block(args):
        qi, gi, bi = args
        t = bi * QB + jnp.arange(QB)
        s = jnp.einsum('bqghd,bcgd->bghqc', qi, k_cmp).astype(jnp.float32) * scale
        s = s - slopes * (t[:, None] - cmp_end[None, :]).astype(jnp.float32)
        p_cmp = masked_softmax(s, cmp_end[None, :] <= t[:, None])
        o_cmp = jnp.einsum('bghqc,bcgd->bqghd', p_cmp.astype(dtype), v_cmp)
        imp = p_cmp.sum(axis=2) @ cmp_to_slc
        cur = t // SLC_BLOCK
        valid = blk[None, :] * SLC_BLOCK <= t[:, None]
        forced = (blk[None, :] == 0) | (blk[None, :] == cur[:, None]) | (blk[None, :] == cur[:, None] - 1)
        score = jnp.where(valid, imp + jnp.where(forced, FORCE_BONUS, 0.0), NEG)
        _, sel = lax.top_k(score, topk)
        tok = (sel[..., None] * SLC_BLOCK + jnp.arange(SLC_BLOCK)).reshape(B, G, QB, topk * SLC_BLOCK)
        k_sel = ks_g[b_idx, g_idx, tok]
        v_sel = vs_g[b_idx, g_idx, tok]
        s = jnp.einsum('bqghd,bgqld->bghql', qi, k_sel).astype(jnp.float32) * scale
        s = s - slopes * (t[None, None, :, None] - tok).astype(jnp.float32)[:, :, None]
        p = masked_softmax(s, (tok <= t[None, None, :, None])[:, :, None])
        o_slc = jnp.einsum('bghql,bgqld->bqghd', p.astype(dtype), v_sel)
        start = bi * QB
        k_win = lax.dynamic_slice_in_dim(kw_pad, start, QB + WINDOW, axis=1)
        v_win = lax.dynamic_slice_in_dim(vw_pad, start, QB + WINDOW, axis=1)
        sp = start - WINDOW + jnp.arange(QB + WINDOW)
        wmask = (sp[None, :] <= t[:, None]) & (sp[None, :] > t[:, None] - WINDOW) & (sp[None, :] >= 0)
        s = jnp.einsum('bqghd,bkgd->bghqk', qi, k_win).astype(jnp.float32) * scale
        s = s - slopes * (t[:, None] - sp[None, :]).astype(jnp.float32)
        p = masked_softmax(s, wmask)
        o_win = jnp.einsum('bghqk,bkgd->bqghd', p.astype(dtype), v_win)
        g = jax.nn.sigmoid(gi.astype(jnp.float32)).astype(dtype)
        return g[..., 0:1] * o_cmp + g[..., 1:2] * o_slc + g[..., 2:3] * o_win

    o = lax.map(block, (qb, gb, jnp.arange(nqb)))
    return o.transpose(1, 0, 2, 3, 4, 5).reshape(B, S, H * d)

def odd_layer(x, norm_g, w_in, b_gate, pe_k, pe_v, wk1, wk2, wv1, wv2, w_out):
    B, S, _ = x.shape
    h = rms_norm(x, norm_g)
    u = h @ w_in
    q, kc, vc, ks, vs, kw, vw, gl, z = jnp.split(u, ODD_SPLITS, axis=-1)
    kv = lambda a: a.reshape(B, S, NSA_KV_GROUPS, HEAD_DIM)
    gl = (gl + b_gate).reshape(B, S, NSA_HEADS, N_BRANCH)
    o = nsa_attention(q.reshape(B, S, NSA_HEADS, HEAD_DIM), kv(kc), kv(vc), kv(ks), kv(vs), kv(kw), kv(vw),
                      gl, pe_k, pe_v, wk1, wk2, wv1, wv2)
    return x + (o * jax.nn.silu(z)) @ w_out

def second_inputs(seed: int = 0) -> dict:
    key = jax.random.key(seed)
    ks = jax.random.split(key, 24)
    ne = (DEPTH + 1) // 2
    no = DEPTH // 2
    nrm = lambda k, shape, sc: jax.random.normal(k, shape, jnp.float32) * sc
    fan_cmp = CMP_BLOCK * HEAD_DIM
    return {
        "x": nrm(ks[0], (BATCH, SEQ, D_MODEL), 1.0),
        "even_norm_g": 1.0 + nrm(ks[1], (ne, D_MODEL), 0.05),
        "even_w_in": nrm(ks[2], (ne, D_MODEL, EVEN_IN), D_MODEL ** -0.5),
        "even_b_f": 1.0 + nrm(ks[3], (ne, FOX_HEADS), 0.1),
        "even_gn_g": 1.0 + nrm(ks[4], (ne, RET_WIDTH), 0.05),
        "even_w_out": nrm(ks[5], (ne, EVEN_MIX_WIDTH, D_MODEL), EVEN_MIX_WIDTH ** -0.5),
        "odd_norm_g": 1.0 + nrm(ks[6], (no, D_MODEL), 0.05),
        "odd_w_in": nrm(ks[7], (no, D_MODEL, ODD_IN), D_MODEL ** -0.5),
        "odd_b_gate": nrm(ks[8], (no, NSA_HEADS * N_BRANCH), 0.1),
        "odd_pe_k": nrm(ks[9], (no, CMP_BLOCK, HEAD_DIM), 0.1),
        "odd_pe_v": nrm(ks[10], (no, CMP_BLOCK, HEAD_DIM), 0.1),
        "odd_wk1": nrm(ks[11], (no, fan_cmp, CMP_HIDDEN), fan_cmp ** -0.5),
        "odd_wk2": nrm(ks[12], (no, CMP_HIDDEN, HEAD_DIM), CMP_HIDDEN ** -0.5),
        "odd_wv1": nrm(ks[13], (no, fan_cmp, CMP_HIDDEN), fan_cmp ** -0.5),
        "odd_wv2": nrm(ks[14], (no, CMP_HIDDEN, HEAD_DIM), CMP_HIDDEN ** -0.5),
        "odd_w_out": nrm(ks[15], (no, NSA_WIDTH, D_MODEL), NSA_WIDTH ** -0.5),
        "final_g": 1.0 + nrm(ks[16], (D_MODEL,), 0.05),
    }

def second_block(x, even_norm_g, even_w_in, even_b_f, even_gn_g, even_w_out,
              odd_norm_g, odd_w_in, odd_b_gate, odd_pe_k, odd_pe_v, odd_wk1, odd_wk2, odd_wv1, odd_wv2, odd_w_out,
              final_g):
    for layer in range(DEPTH):
        i = layer // 2
        if layer % 2 == 0:
            x = even_layer(x, even_norm_g[i], even_w_in[i], even_b_f[i], even_gn_g[i], even_w_out[i])
        else:
            x = odd_layer(x, odd_norm_g[i], odd_w_in[i], odd_b_gate[i], odd_pe_k[i], odd_pe_v[i],
                          odd_wk1[i], odd_wk2[i], odd_wv1[i], odd_wv2[i], odd_w_out[i])
    return rms_norm(x, final_g)


def setup_inputs(seed=0):
    out = dict(first_inputs(seed))
    for name, value in second_inputs(seed + 1).items():
        if name != "x":
            out[name + "_2"] = value
    return out


def reference(
    x, meta_tokens, ssd_norm, ssd_w_in, ssd_conv_w, ssd_conv_b, ssd_dt_bias, ssd_a_log,
    ssd_d_skip, ssd_gate_norm, ssd_w_out, kv_norm, w_kv, sb_norm, sb_w_q, sb_w_o, ffn_norm,
    ffn_w_up, ffn_conv_w, ffn_conv_b, ffn_w_down, final_norm, even_norm_g_2, even_w_in_2,
    even_b_f_2, even_gn_g_2, even_w_out_2, odd_norm_g_2, odd_w_in_2, odd_b_gate_2, odd_pe_k_2,
    odd_pe_v_2, odd_wk1_2, odd_wk2_2, odd_wv1_2, odd_wv2_2, odd_w_out_2, final_g_2,
):
    x = first_block(
        x, meta_tokens, ssd_norm, ssd_w_in, ssd_conv_w, ssd_conv_b, ssd_dt_bias, ssd_a_log,
        ssd_d_skip, ssd_gate_norm, ssd_w_out, kv_norm, w_kv, sb_norm, sb_w_q, sb_w_o, ffn_norm,
        ffn_w_up, ffn_conv_w, ffn_conv_b, ffn_w_down, final_norm,
    )
    return second_block(
        x, even_norm_g_2, even_w_in_2, even_b_f_2, even_gn_g_2, even_w_out_2, odd_norm_g_2,
        odd_w_in_2, odd_b_gate_2, odd_pe_k_2, odd_pe_v_2, odd_wk1_2, odd_wk2_2, odd_wv1_2,
        odd_wv2_2, odd_w_out_2, final_g_2,
    )


_drawn_inputs = setup_inputs


def setup_inputs(seed=0):
    import zlib

    import numpy as np

    out = dict(_drawn_inputs(seed))
    spreads = {}
    factors = {'kv_norm': 4.857,
     'sb_norm': 8.0,
     'ffn_norm': 2.926,
     'ffn_conv_b': 2.876,
     'even_b_f_2': 42.352,
     'even_gn_g_2': 2.894,
     'odd_norm_g_2': 3.478,
     'odd_b_gate_2': 7.019,
     'odd_pe_k_2': 8.0,
     'odd_pe_v_2': 3.523}
    for name, (base, spread) in spreads.items():
        noise = np.random.default_rng([zlib.crc32(name.encode()), seed]).standard_normal(out[name].shape)
        drawn = base * np.exp(spread * noise) if base else spread * noise
        out[name] = jnp.asarray(drawn.astype(out[name].dtype))
    for name, factor in factors.items():
        out[name] = (out[name] * factor).astype(out[name].dtype)
    return out
```

```python
from contextlib import ExitStack

import numpy as np

import concourse.bass as bass
from concourse import mybir

F32 = mybir.dt.float32
ACT = mybir.ActivationFunctionType
ALU = mybir.AluOpType
AX = mybir.AxisListType

P = 128
D = 1024
KD = D // P
META = 16
S = 512
L = META + S
LH = L // 2
BANK = 512
EPS = 1e-6
GN_EPS = 1e-5
BIG = 1e30

GROUPS = 4
HPG = 8
HEADS = 32
DI = 2048
CHUNKS = [(0, META)] + [(META + P * c, P) for c in range(4)]
CONV = 4
FT = 22
FCONV = 3
SBH = 16
DH = 64
FOXH = 8
RETH = 8
NH = 16
NG = 4
CB = 32
N_CMP = 31

R = 4
SLOT = 2048
DK = FT // 2


def layout(fields):
    at, out = 0, {}
    for name, width in fields:
        out[name] = (at, width)
        at += width
    return out, at


PARAMS, N_PARAMS = layout([
    ("ssd_norm", 8), ("kv_norm", 8), ("sb_norm", 8), ("ffn_norm0", 8), ("ffn_norm1", 8),
    ("final_norm", 8), ("even_norm", 8), ("odd_norm", 8), ("final_g", 8), ("gate_norm", 16),
    ("conv_w", 24 * CONV), ("conv_b", 24), ("fconv_w0", 2 * FT * FCONV), ("fconv_b0", 2 * FT),
    ("fconv_w1", 2 * FT * FCONV), ("fconv_b1", 2 * FT), ("d_skip", 16), ("dt_bias", 1), ("a_log", 1),
    ("w_dt", 8 * 32), ("w_f", 8 * 8), ("w_gate", 8 * 48), ("b_f", 1), ("b_gate", 48), ("gn_g", 4),
    ("pe_k", 16), ("pe_v", 16), ("wk2", 256), ("wv2", 128),
    ("ident", P), ("ones", P), ("neg_tri", P), ("neg_ones", P), ("pick127", P), ("pick15", P),
    ("mask_sl", P), ("hidden", P), ("eps", 1), ("gn_eps", 1), ("slopes", NH), ("alibi", 512), ("causal", 512),
    ("cmp_seen", 4 * CB),
])
TABLES, N_TABLES = layout([("decay", RETH * 512), ("cmp_bias", NH * 4 * CB)])

STREAM = [("bc", 4), ("grp", 16), ("sout", 8), ("ffn0", 22), ("down0", 16),
          ("sbk", 4), ("sbv", 4), ("sbq", 4), ("wo", 4), ("ffn1", 22), ("down1", 16),
          ("ev_qf", 2), ("ev_kf", 2), ("ev_vf", 2), ("ev_qr", 2), ("ev_kr", 2), ("ev_vr", 2),
          ("ev_z", 4), ("eout", 4),
          ("od_q", 4), ("od_kc", 1), ("od_vc", 1), ("od_ks", 1), ("od_kw", 1), ("od_vs", 1),
          ("od_vw", 1), ("ck", 2), ("cv", 2), ("od_z", 4), ("oout", 4)]
GT = 26
TILES = [("dt", 1), ("bc", 8), ("dtt", 1), ("end", 1), ("grp", 4 * GT), ("sout", 8),
         ("ffn0", 44), ("down0", 8),
         ("sbk", 8), ("sbv", 20), ("sbq", 8), ("oT", 8), ("wo", 8), ("ffn1", 44), ("down1", 8),
         ("ev_f", 1), ("ev_qf", 4), ("ev_kf", 4), ("ev_vf", 8), ("ev_qr", 4), ("ev_kr", 4), ("ev_vr", 8),
         ("ev_z", 8), ("ev_y", 8), ("eout", 8),
         ("od_g", 1), ("od_q", 8), ("od_kc", 2), ("od_vc", 2), ("od_ks", 2), ("od_kw", 2),
         ("od_vs", 4), ("od_vw", 4), ("ck", 2), ("ck2", 1), ("cv", 2), ("cv2", 1),
         ("od_z", 8), ("od_y", 8), ("oout", 8)]


def bases(pairs):
    at, out = 0, {}
    for name, n in pairs:
        out[name] = at
        at += n
    return out, at


U0, N_UNITS = bases(STREAM)
M0, N_TILES = bases(TILES)


def build(nc, x_in, stream, down, params_in, tables_in, out):
    ctx = ExitStack()
    with ctx:
        def sb(name, shape):
            return ctx.enter_context(nc.sbuf_tensor(name, shape, F32))

        sems = {}

        def sem(name):
            if name not in sems:
                sems[name] = ctx.enter_context(nc.semaphore(name))
            return sems[name]

        ring = sb("ring", [P, R, SLOT])
        par = sb("par", [P, N_PARAMS])
        hT = sb("hT", [P, KD, L])
        uT = sb("uT", [P, KD, L])
        sq = sb("sq", [P, 2, L])
        sd = sb("sd", [P, L])
        rstd = sd
        ARENA = 30860
        arena = sb("arena", [P, ARENA])
        ident_b = ctx.enter_context(nc.sbuf_tensor("ident_b", [P, P], mybir.dt.bfloat16))
        hidden_b = ctx.enter_context(nc.sbuf_tensor("hidden_b", [P, P], mybir.dt.bfloat16))
        PS = [ctx.enter_context(nc.psum_tensor(f"PS{i}", [P, 2 * BANK], F32)) for i in range(2)]
        PC = ctx.enter_context(nc.psum_tensor("PC", [P, 2, BANK], F32))
        PD = ctx.enter_context(nc.psum_tensor("PD", [P, 2, BANK], F32))

        def prm(name, rows=P):
            at, n = PARAMS[name]
            return par[0:rows, at:at + n]

        def carve(fields):
            at, views = 0, {}
            for name, *dims in fields:
                n = int(np.prod(dims))
                v = arena[:, at:at + n]
                if len(dims) == 2:
                    v = v.rearrange("p (a b) -> p a b", a=dims[0])
                elif len(dims) == 3:
                    v = v.rearrange("p (a b c) -> p a b c", a=dims[0], b=dims[1])
                elif len(dims) == 4:
                    v = v.rearrange("p (a b c d) -> p a b c d", a=dims[0], b=dims[1], c=dims[2])
                views[name] = v
                at += n
            assert at <= ARENA, at
            return views

        ident, ones = prm("ident"), prm("ones")
        V0 = BANK - LH

        def wide(M):
            return PS[M % 2][:, V0:V0 + L]

        loaded = sem("loaded")
        w_ready = [sem(f"w_ready{r}") for r in range(R)]
        ps_full = sem("ps_full")
        ps_free = [sem(f"ps_free{b}") for b in range(2)]
        sq_full, sq_free = sem("sq_full"), sem("sq_free")
        sd_full = sem("sd_full")
        u_full = sem("u_full")
        h_upd = sem("h_upd")
        raw_full, conv_full = sem("raw_full"), sem("conv_full")
        stored = sem("stored")

        def steps(eng, n, per, body):
            full = n // per
            if full > 1:
                with eng.Fori(0, full) as it:
                    body(it, per)
            elif full:
                body(0, per)
            if n % per:
                body(full, n % per)

        def source_of(stage):
            downs = [n for n, _ in STREAM if n.startswith("down")]
            before = sum(n for name, n in STREAM if U0[name] < U0[stage] and (name in downs) == (stage in downs))
            return (down, before, DK * P) if stage in downs else (stream, before, SLOT)

        def used_up(u):
            if u < 0:
                return None
            stage = [n for n, _ in STREAM if U0[n] <= u][-1]
            r = u - U0[stage]
            if stage == "grp":
                return M0[stage] + r // R * GT + 2 * (r % R) + 2
            if stage.startswith("down"):
                return M0[stage] + r // 2 + 1
            return M0[stage] + (r + 1) * TILES_PER_UNIT.get(stage, 2)

        def signal(eng, *what):
            eng.drain()
            for s in what:
                eng.sem_inc(s, 1)

        def slot_of(stage, r):
            return (U0[stage] + r) % R

        def fill_of(stage, it, r):
            return (U0[stage] + r) // R + it

        def tile_wait(eng, stage, it, per, j):
            eng.wait_ge(ps_full, it * per + M0[stage] + j + 1)

        def tile_of(stage, j):
            return PS[(M0[stage] + j) % 2]

        def free_of(stage, j):
            return ps_free[(M0[stage] + j) % 2]

        def acquire(eng, stage, it, per, j):
            assert per % 2 == 0 or isinstance(it, int) and it == 0
            eng.wait_ge(free_of(stage, j), it * (per // 2) + (M0[stage] + j) // 2 + 1)

        ssd = carve([("BCt", 8, L), ("Xs", 4, L), ("Zs", 4, L), ("Bs", L), ("Cs", L), ("yT", 16, L),
                     ("dtT", 5, 32), ("acsT", 5, 32), ("w2", 5, 32), ("dC", 5, 32), ("eacs", 5, 32),
                     ("Btok", 5, P), ("Gm", 4, P), ("Gm0", 16),
                     ("S", 4, 512),
                     ("Dm", 2, 512), ("sel", HPG, P), ("L0", HPG, 16), ("raw", CONV - 1 + L), ("cv", L),
                     ("ea", 1), ("acs", L), ("xdt", 5, 512), ("ytok", 5, 512)])
        ssd_dt = carve([("_", 8 * L), ("dtv", L), ("dtt", L), ("dt", L), ("one", L)])
        xdt, ytok = ssd["xdt"], ssd["ytok"]
        xw2 = ytok
        acs_keep = ssd["acs"][0:32, :]
        sbm = carve([("kT", 8, L), ("qT", 8, L), ("v", 5, D), ("o", 5, D), ("ks", L), ("qs", L),
                     ("A", 2, 3 * BANK), ("W", 2, 3 * BANK), ("SP", 2, 3 * BANK)])
        u2 = sbm["o"].rearrange("p a b -> p (a b)")[:, 0:KD * L].rearrange("p (k l) -> p k l", k=KD)
        ev = carve([("qf", 4, S), ("kf", 4, S), ("vf", 4, S), ("qr", 4, S), ("kr", 4, S), ("vr", 4, S),
                    ("of", 4, S), ("or", 4, S), ("Pm", 2, 1280), ("PT", 2, 1280), ("qs", 2, S), ("ks", 2, S),
                    ("decay", RETH, S), ("sel", 4, P), ("negc", S), ("nm", 2, 4), ("rs", 2, 4), ("ri", 2, 4),
                    ("mu", 32), ("var", 32)])
        z_even = arena[:, 0:KD * S].rearrange("p (k l) -> p k l", k=KD)
        od = carve([("A2", 2, NG, L), ("q", 8, S), ("ksd", NG, S), ("kwd", NG, S), ("vs", 4, 256), ("vw", 4, 256),
                    ("o", 4, D), ("Pm", 2, 1280), ("PT", 2, 1280), ("gates", 48, 4), ("h1", 2, P),
                    ("h1v", 2, NG, 4, CB), ("kcmp", P), ("Vbd", NG, 256), ("cmp_bias", NH, P),
                    ("hb", 4), ("mxc", 16), ("rsc", 16), ("cfc", 16), ("nm", 2, 4), ("rs", 2, 4), ("ri", 2, 4)])
        odr = {}
        for n, name in enumerate(("kc", "vc", "ks", "kw")):
            at = 2 * NG * L + 8 * S + 2 * NG * S + 2 * 4 * 256 + 4 * D + n * 2 * S
            odr[name] = arena[:, at:at + 2 * S].rearrange("p (k l) -> p k l", k=2)
        ods = carve([("qs", 2, S), ("kss", S), ("kws", S), ("kcs", CB), ("bias", 2, S), ("X", 512), ("P2", 512),
                     ("PTc", 512)])
        z_odd = arena[:, 0:KD * S].rearrange("p (k l) -> p k l", k=KD)
        h2 = hT[:, :, META:L]
        uv = uT[:, :, 0:S]
        ffn = carve([("act", FT, L), ("rawg", FCONV - 1 + L), ("rawv", FCONV - 1 + L), ("cg", L), ("cvv", L)])

        NORM = {n: i for i, n in enumerate(["ssd", "ffn0", "sb", "ffn1", "final", "even", "odd", "last"])}
        H_BASE = {n: 8 * i for n, i in NORM.items()}
        U_BASE = {"ssd": 0, "ffn0": 8, "sb": 16, "ffn1": 32, "even": 40, "odd": 48, "last": 56}
        TURNS = [(3,), (2, 0), (1,)]
        OFF = {3: 0, 2: 512, 0: 896, 1: 1024}
        DOFF = {0: 0, 1: 512, 3: 896, 2: 1024}

        def scores_at(b, a):
            w = P * (a + 1)
            return PC[:, b, 0:w] if a == 1 else PS[b][:, OFF[a]:OFF[a] + w]

        def decayed_at(b, i):
            w = S - P * i
            return PC[:, b, 0:w] if i == 2 else PS[b][:, DOFF[i]:DOFF[i] + w]

        ev_od = {"fx": ev, "ns": od}


        block = ctx.enter_context(nc.Block())

        @block.sync
        def _(sp):
            def load_stage(stage, n):
                src, src0, width = source_of(stage)
                per = TILE_STEP.get(stage, (R * TILES_PER_UNIT.get(stage, 2)))

                def load(it, r, after_tiles):
                    u = U0[stage] + r
                    if after_tiles is not None:
                        sp.wait_ge(ps_full, after_tiles)
                    sp.dma_start(ring[:, u % R, 0:width],
                                 src[bass.ds(it * R + src0 + r, 1), :, :].rearrange("a p n -> (a p) n")
                                 ).then_inc(w_ready[u % R], 16)

                for r in range(min(R, n)):
                    load(0, r, used_up(U0[stage] + r - R))
                full = n // R
                if full > 1:
                    with sp.Fori(1, full) as it:
                        for r in range(R):
                            load(it, r, (it - 1) * per + used_up(U0[stage] + r))
                if full:
                    for r in range(n % R):
                        load(full, r, (full - 1) * per + used_up(U0[stage] + r))

            sp.dma_start(hT[:, :, :].rearrange("p k l -> p (k l)"), x_in).then_inc(loaded, 16)
            sp.dma_start(par[:, :], params_in).then_inc(loaded, 16)
            for stage, n in STREAM:
                load_stage(stage, n)
                if stage == "ev_vr":
                    at, n = TABLES["decay"]
                    sp.wait_ge(h_upd, 40)
                    sp.dma_start(ev["decay"].rearrange("p a b -> p (a b)"), tables_in[:, at:at + n]
                                 ).then_inc(sem("decay_in"), 16)
                if stage == "od_kw":
                    sp.wait_ge(sem("pad2"), 1)
                    for which, (raw, moved) in enumerate((("kc", 1), ("vc", 1), ("ks", 0), ("kw", 0))):
                        sp.wait_ge(sem("odk_full"), 2 * which + 2)
                        for gg in range(NG):
                            src = odr[raw][DH * (gg % 2):DH * (gg % 2) + DH, gg // 2, :]
                            dst = od["A2"][:, which, gg, :] if moved else od["ksd" if raw == "ks" else "kwd"][:, gg, :]
                            sp.dma_start(dst[0:DH, 0:S], src).then_inc(sem("dup"), 16)
                            sp.dma_start(dst[DH:P, 0:S - moved], src[:, moved:S]).then_inc(sem("dup"), 16)
                    at, n = TABLES["cmp_bias"]
                    sp.dma_start(od["cmp_bias"].rearrange("p a b -> p (a b)"), tables_in[:, at:at + n]
                                 ).then_inc(sem("cmp_in"), 16)
            sp.wait_ge(u_full, U_BASE["last"] + KD)
            sp.dma_start(out.rearrange("p (k l) -> p k l", k=KD), uv).then_inc(stored, 16)
            sp.wait_ge(stored, 16)


        @block.tensor
        def _(pe):
            mm = nc.tensor.matmul
            pe.wait_ge(loaded, 32)

            def norm_stats(name, width, v0):
                pc = PC[:, :, :].rearrange("p a b -> p (a b)")
                halves = [(0, LH), (LH, L)] if width == L else [(0, width)]
                for k in range(KD):
                    pe.wait_ge(sq_full, NORM[name] * KD + k + 1)
                    for a, b in halves:
                        last = mm(pc[:, v0 + a:v0 + b], ones, sq[:, k % 2, a:b], start=k == 0, stop=k == KD - 1)
                    last.then_inc(sq_free, 1)

            def project(stage, it, per, j, slot, k_n, mcol, moving, start=True, stop=True, k0=0):
                tile = tile_of(stage, j)
                width = moving.shape[2]
                v0 = V0 if width == L else 0
                for a, b in ([(0, LH), (LH, L)] if width == L else [(0, width)]):
                    for k in range(k_n):
                        last = mm(tile[:, v0 + a:v0 + b], ring[:, slot, :].rearrange(
                            "p (k m) -> p k m", k=k_n)[:, k, mcol:mcol + P], moving[:, k0 + k, a:b],
                            start=start and k == 0, stop=stop and k == k_n - 1)
                return last

            def unit_ready(stage, it, r):
                pe.wait_ge(w_ready[slot_of(stage, r)], 16 * it + 16 * (fill_of(stage, 0, r) + 1))

            def project_units(stage, n_units, moving):
                def body(it, count):
                    for r in range(count):
                        unit_ready(stage, it, r)
                        for m in range(2):
                            acquire(pe, stage, it, 2 * R, 2 * r + m)
                            last = project(stage, it, 2 * R, 2 * r + m, slot_of(stage, r), KD, m * P, moving)
                            last.then_inc(ps_full, 1)
                steps(pe, n_units, R, body)

            norm_stats("ssd", L, V0)
            pe.wait_ge(u_full, 8)
            acquire(pe, "dt", 0, 2, 0)
            w_dt = prm("w_dt").rearrange("p (k m) -> p k m", k=KD)
            for a, b in [(0, LH), (LH, L)]:
                for k in range(KD):
                    last = mm(tile_of("dt", 0)[0:32, V0 + a:V0 + b], w_dt[:, k, :], uT[:, k, a:b],
                              start=k == 0, stop=k == KD - 1)
            last.then_inc(ps_full, 1)
            project_units("bc", 4, uT)
            pe.wait_ge(sem("acs_full"), 1)
            acquire(pe, "dtt", 0, 2, 0)
            t = tile_of("dtt", 0)
            for c, (at, n) in enumerate(CHUNKS):
                nc.tensor.transpose(t[0:n, 32 * c:32 * c + 32], ssd_dt["dt"][0:32, at:at + n], ident[0:32, 0:32])
                last = nc.tensor.transpose(t[0:n, BANK + 32 * c:BANK + 32 * c + 32], acs_keep[0:32, at:at + n],
                                           ident[0:32, 0:32])
            last.then_inc(ps_full, 1)
            pe.wait_ge(sem("acsT_full"), 1)
            acquire(pe, "end", 0, 2, 0)
            t = tile_of("end", 0)
            mm(t[:, 0:32], prm("pick15", META), ssd["acsT"][0:META, 0, :], start=True, stop=True)
            mm(t[:, 32:160], prm("pick127"), ssd["acsT"][:, 1:5, :].rearrange("p a b -> p (a b)"),
               start=True, stop=True).then_inc(ps_full, 1)

            Xs, Bs, Cs, Btok, S_ = ssd["Xs"], ssd["Bs"], ssd["Cs"], ssd["Btok"], ssd["S"]
            with pe.Fori(0, GROUPS) as g:
                for r in range(4):
                    unit_ready("grp", g, r)
                    for m in range(2):
                        acquire(pe, "grp", g, GT, 2 * r + m)
                        last = project("grp", g, GT, 2 * r + m, slot_of("grp", r), KD, m * P, uT)
                        last.then_inc(ps_full, 1)
                pe.wait_ge(sem("bc_staged"), g + 1)
                acquire(pe, "grp", g, GT, 8)
                t = tile_of("grp", 8)
                nc.tensor.transpose(t[0:META, BANK:BANK + P], Bs[:, 0:META], ident)
                for c in range(1, 5):
                    at, n = CHUNKS[c]
                    last = nc.tensor.transpose(t[:, (c - 1) * P:c * P], Bs[:, at:at + n], ident)
                last.then_inc(ps_full, 1)
                acquire(pe, "grp", g, GT, 9)
                t = tile_of("grp", 9)
                mm(t[0:META, BANK:BANK + META], Bs[:, 0:META], Cs[:, 0:META], start=True, stop=True)
                for c in range(1, 5):
                    at, n = CHUNKS[c]
                    last = mm(t[:, (c - 1) * P:c * P], Bs[:, at:at + n], Cs[:, at:at + n], start=True, stop=True)
                last.then_inc(ps_full, 1)
                acquire(pe, "grp", g, GT, 10)
                t = tile_of("grp", 10)
                for e in range(HPG):
                    last = mm(t[:, e * META:(e + 1) * META], ssd["sel"][0:32, e, :], acs_keep[:, 0:META],
                              start=True, stop=True)
                last.then_inc(ps_full, 1)
                pe.wait_ge(sem("x_full"), 4 * g + 4)
                for j, cs in ((11, [0]), (12, [1, 2]), (13, [3, 4])):
                    acquire(pe, "grp", g, GT, j)
                    for i, c in enumerate(cs):
                        at, n = CHUNKS[c]
                        for q in range(4):
                            last = nc.tensor.transpose(tile_of("grp", j)[0:n, i * BANK + q * P:i * BANK + (q + 1) * P],
                                                       Xs[:, q, at:at + n], ident)
                    last.then_inc(ps_full, 1)
                pe.wait_ge(sem("btok_full"), g + 1)
                for c in range(4):
                    n = CHUNKS[c][1]
                    pe.wait_ge(sem("xw_full"), 5 * g + c + 1)
                    acquire(pe, "grp", g, GT, 14 + c)
                    mm(tile_of("grp", 14 + c)[:, 0:BANK], Btok[0:n, c, :], xw2[0:n, c, :],
                       start=True, stop=True).then_inc(ps_full, 1)
                for j in range(2):
                    acquire(pe, "grp", g, GT, 18 + j)
                    for i in range(2):
                        c = 1 + 2 * j + i
                        pe.wait_ge(sem("state_full"), 4 * g + c)
                        last = mm(tile_of("grp", 18 + j)[:, i * BANK:(i + 1) * BANK],
                                  Cs[:, CHUNKS[c][0]:CHUNKS[c][0] + P], S_[:, c - 1, :], start=True, stop=True)
                    last.then_inc(ps_full, 1)

                def spread(e):
                    if e >= 2:
                        pe.wait_ge(sem("dm_full"), HPG * g + e - 1)
                    mm(PC[:, e % 2, :], ssd["sel"][0:32, e, :], acs_keep[:, META:L], start=True, stop=True
                       ).then_inc(sem("pc_full"), 1)

                spread(0)
                spread(1)
                for e in range(HPG):
                    pe.wait_ge(sem("mt_full"), HPG * g + e + 1)
                    pe.wait_ge(sem("pd_free"), HPG * g + e + 1)
                    if e == HPG - 1:
                        acquire(pe, "grp", g, GT, 20)
                        pe.wait_ge(sem("m0_full"), g + 1)
                    for c in range(4):
                        last = mm(PD[:, e % 2, c * DH:(c + 1) * DH], ssd["Dm"][:, e % 2, c * P:(c + 1) * P],
                                  xdt[:, c + 1, e * DH:(e + 1) * DH], start=True, stop=True)
                    last.then_inc(sem("pd_full"), 1)
                    if e + 2 < HPG:
                        spread(e + 2)
                for e in range(HPG):
                    last = mm(tile_of("grp", 20)[0:META, e * DH:(e + 1) * DH], ssd["L0"][0:META, e, :],
                              xdt[0:META, 0, e * DH:(e + 1) * DH], start=True, stop=True)
                last.then_inc(ps_full, 1)
                pe.wait_ge(sem("ytok_full"), g + 1)
                for q in range(4):
                    acquire(pe, "grp", g, GT, 21 + q)
                    t = tile_of("grp", 21 + q)
                    for c in range(1, 5):
                        nc.tensor.transpose(t[:, BANK + (c - 1) * P:BANK + c * P],
                                            ytok[:, c, q * P:(q + 1) * P], ident)
                    last = nc.tensor.transpose(t[:, BANK - META:BANK], ytok[0:META, 0, q * P:(q + 1) * P],
                                               ident[0:META, 0:META])
                    last.then_inc(ps_full, 1)
                acquire(pe, "grp", g, GT, 25)
                for q in range(4):
                    pe.wait_ge(sem("gsq_full"), 4 * g + q + 1)
                    for a, b in [(0, LH), (LH, L)]:
                        last = mm(tile_of("grp", 25)[:, V0 + a:V0 + b], ones, sq[:, q % 2, a:b],
                                  start=q == 0, stop=q == 3)
                    last.then_inc(sem("gsq_free") if q < 3 else ps_full, 1)

            pe.wait_ge(sem("yT_full"), 4 * GROUPS)

            def sout(it, count):
                for r in range(count):
                    unit_ready("sout", it, r)
                    acquire(pe, "sout", it, R, r)
                    project("sout", it, R, r, slot_of("sout", r), 16, 0, ssd["yT"]).then_inc(ps_full, 1)
            steps(pe, 8, R, sout)

            def ffn_pe(i):
                norm_stats(f"ffn{i}", L, V0)
                pe.wait_ge(u_full, U_BASE[f"ffn{i}"] + 8)
                project_units(f"ffn{i}", FT, uT)
                pe.wait_ge(sem("act_full"), FT * (i + 1))

                def body(it, count):
                    for m in range(count // 2):
                        stage = f"down{i}"
                        acquire(pe, stage, it, 2, m)
                        tile = tile_of(stage, m)
                        for half in range(2):
                            unit_ready(stage, it, 2 * m + half)
                        s0, s1 = slot_of(stage, 2 * m), slot_of(stage, 2 * m + 1)
                        for a, b in [(0, LH), (LH, L)]:
                            for k in range(FT):
                                w = ring[:, s0 if k < DK else s1, 0:DK * P].rearrange("p (k m) -> p k m", k=DK)
                                last = mm(tile[:, V0 + a:V0 + b], w[:, k % DK, :], ffn["act"][:, k, a:b],
                                          start=k == 0, stop=k == FT - 1)
                        last.then_inc(ps_full, 1)
                steps(pe, 16, R, body)

            ffn_pe(0)

            def tokens_major(stage, n_units, moving, tokens):
                for r in range(n_units):
                    unit_ready(stage, 0, r)
                    w = ring[:, slot_of(stage, r), :].rearrange("p (k m) -> p k m", k=KD)
                    for t, at in enumerate(range(0, tokens, P)):
                        n = min(P, tokens - at)
                        j = r * -(-tokens // P) + t
                        acquire(pe, stage, 0, 2, j)
                        for k in range(KD):
                            last = mm(tile_of(stage, j)[0:n, 0:256], moving[:, k, at:at + n], w[:, k, :],
                                      start=k == 0, stop=k == KD - 1)
                        last.then_inc(ps_full, 1)

            norm_stats("sb", L, V0)
            pe.wait_ge(u_full, U_BASE["sb"] + 8)
            project_units("sbk", 4, uT)
            tokens_major("sbv", 4, uT, L)
            pe.wait_ge(u_full, U_BASE["sb"] + 16)
            project_units("sbq", 4, u2)
            pe.wait_ge(sem("qkv_full"), 3)
            neg_tri, neg_ones = prm("neg_tri"), prm("neg_ones")

            def zseg(e, seg):
                return PS[e][:, seg * BANK:(seg + 1) * BANK] if seg < 2 else PC[:, e, :]

            def hide(e, seg, at, n):
                return mm(zseg(e, seg)[0:n, at:at + n], ident_b[0:n, 0:n], hidden_b[0:n, 0:n], start=False, stop=True,
                          skip_group_check=True)

            with pe.Fori(0, SBH // 2) as j:
                pe.wait_ge(sem("staged"), j + 1)
                for e in range(2):
                    ks, qs = sbm["ks"][DH * e:DH * e + DH], sbm["qs"][DH * e:DH * e + DH]
                    pe.wait_ge(sem("w_exp"), 6 * j + 3 * e + 3)
                    mm(zseg(e, 0), ks[:, 0:P], qs[:, 0:S], start=True, stop=True)
                    hide(e, 0, 0, P).then_inc(sem("z_full"), 1)
                    mm(zseg(e, 1)[:, 0:384], ks[:, P:2 * P], qs[:, P:S], start=True, stop=True)
                    mm(zseg(e, 1)[:, 384:512], ks[:, 3 * P:S], qs[:, 3 * P:S], start=False, stop=True,
                       skip_group_check=True)
                    hide(e, 1, 0, P)
                    hide(e, 1, 384, P).then_inc(sem("z_full"), 1)
                    mm(zseg(e, 2)[:, 0:256], ks[:, 2 * P:3 * P], qs[:, 2 * P:S], start=True, stop=True)
                    for i in range(5):
                        n = P if i < 4 else META
                        mm(zseg(e, 2)[0:n, 256 + 16 * i:272 + 16 * i], ks[:, P * i:P * i + n], qs[:, S:L],
                           start=False, stop=True, skip_group_check=True)
                    hide(e, 2, 0, P)
                    hide(e, 2, 320, META).then_inc(sem("z_full"), 1)
                for e in range(2):
                    sp_ = sbm["SP"][:, e, :]

                    def add(seg, a, b, w, rhs):
                        out_ = zseg(e, seg)[0:w.shape[1], a:b]
                        if len(rhs.shape) == 3:
                            out_ = out_.rearrange("p (r c) -> p r c", r=rhs.shape[1])
                        return mm(out_, w, rhs, start=False, stop=True, skip_group_check=True)

                    pe.wait_ge(sem("sp_full2"), 6 * j + 3 * e + 3)
                    add(0, 0, 512, neg_tri, sp_[:, 0:512])
                    add(0, 128, 512, neg_ones, sp_[:, 512:896])
                    add(0, 256, 512, neg_ones, sp_[:, 1024:1280])
                    add(0, 384, 512, neg_ones, sp_[:, 896:1024]).then_inc(sem("c_full"), 1)
                    add(1, 0, 384, neg_tri, sp_[:, 512:896])
                    add(1, 384, 512, neg_tri, sp_[:, 896:1024])
                    add(1, 128, 384, neg_ones, sp_[:, 1024:1280])
                    add(1, 256, 384, neg_ones, sp_[:, 896:1024]).then_inc(sem("c_full"), 1)
                    add(2, 0, 256, neg_tri, sp_[:, 1024:1280])
                    add(2, 128, 256, neg_ones, sp_[:, 896:1024])
                    add(2, 256, 320, neg_tri, sp_[:, 1280:1344])
                    add(2, 320, 336, neg_tri[0:META, 0:META], sp_[0:META, 1344:1360])
                    for i in range(1, 5):
                        n = P if i < 4 else META
                        rhs = sp_[0:n, 1280 + 16 * i:1296 + 16 * i]
                        if i > 1:
                            rhs = rhs.unsqueeze(1).to_broadcast([n, i, META])
                        last = add(2, 256, 256 + 16 * i, neg_ones[0:n, :], rhs)
                    last.then_inc(sem("c_full"), 1)
                for e in range(2):
                    pe.wait_ge(sem("o_free"), 2 * j + e + 1)
                    pe.wait_ge(sem("w_exp"), 6 * j + 3 * e + 9)
                    W_ = sbm["W"][:, e, :]
                    col = [0, 512, 1024, 896]
                    first = [0, 1, 2, 3]
                    v = lambda i: sbm["v"][:, i, bass.ds((2 * j + e) * DH, DH)]
                    for a in range(4):
                        for i in range(a + 1):
                            c = col[i] + P * (a - first[i])
                            mm(PD[:, e, a * DH:(a + 1) * DH], W_[:, c:c + P], v(i), start=i == 0, stop=i == a)
                    for i in range(5):
                        last = mm(PD[0:META, e, 256:320], W_[:, 1280 + 16 * i:1296 + 16 * i], v(i),
                                  start=i == 0, stop=i == 4)
                    last.then_inc(sem("o_full"), 1)
            pe.wait_ge(sem("o_free"), SBH + 2)
            for k in range(8):
                acquire(pe, "oT", 0, 2, k)
                t = tile_of("oT", k)
                for a in range(4):
                    nc.tensor.transpose(t[:, a * P:(a + 1) * P], sbm["o"][:, a, k * P:(k + 1) * P], ident)
                nc.tensor.transpose(t[:, S:L], sbm["o"][0:META, 4, k * P:(k + 1) * P], ident[0:META, 0:META]
                                    ).then_inc(ps_full, 1)
            pe.wait_ge(sem("oT_full"), 8)
            project_units("wo", 4, uT)
            ffn_pe(1)

            def ret_out(it, h):
                pe.wait_ge(sem("ret_m"), it * 4 + h + 3)
                pe.wait_ge(sem("ret_free"), it * 4 + h + 1)
                v = lambda i: ev["vr"][:, i, bass.ds((it * 4 + h) * DH, DH)]
                for a in range(4):
                    for i in range(a + 1):
                        c = DOFF[i] + P * (a - i)
                        last = mm(PD[:, h % 2, a * DH:(a + 1) * DH], ev["Pm"][:, h % 2, c:c + P], v(i),
                                  start=i == 0, stop=i == a)
                last.then_inc(sem("ret_o"), 1)

            def outputs_T(stage, of):
                for k in range(8):
                    acquire(pe, stage, 0, 2, k)
                    for a in range(4):
                        last = nc.tensor.transpose(tile_of(stage, k)[:, a * P:(a + 1) * P], of(k, a), ident)
                    last.then_inc(ps_full, 1)

            norm_stats("final", S, 0)
            norm_stats("even", S, 0)
            pe.wait_ge(u_full, U_BASE["even"] + 8)
            acquire(pe, "ev_f", 0, 2, 0)
            w_f = prm("w_f").rearrange("p (k m) -> p k m", k=KD)
            for k in range(KD):
                last = mm(tile_of("ev_f", 0)[0:FOXH, 0:S], w_f[:, k, :], uv[:, k, :], start=k == 0, stop=k == KD - 1)
            last.then_inc(ps_full, 1)
            for x in "fr":
                project_units(f"ev_q{x}", 2, uv)
                project_units(f"ev_k{x}", 2, uv)
                tokens_major(f"ev_v{x}", 2, uv, S)

            def rows_pe(name, per_it, it, scores, value):
                for s in range(per_it + 1):
                    if s < per_it:
                        pe.wait_ge(sem(name + "_nm"), it * per_it + s + 1)
                        scores(s)
                    if s:
                        n = s - 1
                        N = it * per_it + n
                        par_ = n % 2
                        for i, tiles in enumerate(TURNS):
                            pe.wait_ge(sem(name + "_p"), N * 3 + i + 1)
                            if i == 0:
                                pe.wait_ge(sem(name + "_ptd"), N + 1)
                            else:
                                pe.wait_ge(sem(name + "_pta"), N * 2 + i)
                            for a in tiles:
                                for b in range(a + 1):
                                    last = nc.tensor.transpose(
                                        scores_at(1, a)[:, b * P:(b + 1) * P],
                                        ev_od[name]["Pm"][:, par_, OFF[a] + b * P:OFF[a] + (b + 1) * P], ident)
                            last.then_inc(sem(name + "_tr"), 1)
                        pe.wait_ge(sem(name + "_ptd"), N + 2)
                        pe.wait_ge(sem(name + "_pta"), N * 2 + 3)
                        pe.wait_ge(sem(name + "_comb"), N + 1)
                        for a in range(4):
                            for b in range(a + 1):
                                last = mm(PD[:, par_, a * DH:(a + 1) * DH],
                                          ev_od[name]["PT"][:, par_, OFF[a] + b * P:OFF[a] + (b + 1) * P],
                                          value(n, b), start=b == 0, stop=b == a)
                        last.then_inc(sem(name + "_o"), 1)

            pe.wait_ge(sem("ev_full"), 6)
            pe.wait_ge(sem("negc_full"), 1)
            with pe.Fori(0, 2) as it:
                pe.wait_ge(sem("fstaged"), it + 1)

                def fox_scores(h):
                    rows = slice(DH * (h % 2), DH * (h % 2) + DH)
                    for tiles in TURNS:
                        for a in tiles:
                            w = P * (a + 1)
                            mm(scores_at(0, a), ev["qs"][rows, h // 2, a * P:w], ev["ks"][rows, h // 2, 0:w],
                               start=True, stop=False)
                            last = mm(scores_at(0, a), ev["sel"][0:FOXH, h, :], ev["negc"][0:FOXH, 0:w],
                                      start=False, stop=True)
                        last.then_inc(sem("fx_s"), 1)

                rows_pe("fx", 4, it, fox_scores, lambda h, b: ev["vf"][:, b, bass.ds((it * 4 + h) * DH, DH)])
            with pe.Fori(0, 2) as it:
                pe.wait_ge(sem("fstaged"), it + 3)
                for h in range(4):
                    rows = slice(DH * (h % 2), DH * (h % 2) + DH)
                    if h < 2:
                        pe.wait_ge(sem("ret_m"), it * 4 + h + 1)
                    else:
                        pe.wait_ge(sem("ret_m"), it * 4 + h + 1)
                    for i in (0, 1, 3, 2):
                        last = mm(decayed_at(h % 2, i), ev["ks"][rows, h // 2, i * P:(i + 1) * P],
                                  ev["qs"][rows, h // 2, i * P:S], start=True, stop=True)
                    last.then_inc(sem("ret_s"), 1)
                    if h:
                        ret_out(it, h - 1)
                ret_out(it, 3)
            project_units("ev_z", 4, uv)
            pe.wait_ge(sem("mix_full"), 1)
            outputs_T("ev_y", lambda k, a: (ev["of"] if k < 4 else ev["or"])[:, a, (k % 4) * P:(k % 4 + 1) * P])
            pe.wait_ge(sem("y_full"), 8)
            project_units("eout", 4, uv)
            norm_stats("odd", S, 0)
            pe.wait_ge(u_full, U_BASE["odd"] + 8)
            acquire(pe, "od_g", 0, 2, 0)
            w_g = prm("w_gate").rearrange("p (k m) -> p k m", k=KD)
            for a in range(4):
                for k in range(KD):
                    last = mm(tile_of("od_g", 0)[:, a * 48:(a + 1) * 48], uv[:, k, a * P:(a + 1) * P], w_g[:, k, :],
                              start=k == 0, stop=k == KD - 1)
            last.then_inc(ps_full, 1)
            project_units("od_q", 4, uv)
            for x in ("kc", "vc", "ks", "kw"):
                project_units(f"od_{x}", 1, uv)
            tokens_major("od_vs", 1, uv, S)
            tokens_major("od_vw", 1, uv, S)
            for which, (stage, pe_) in enumerate((("ck", "pe_k"), ("cv", "pe_v"))):
                pe.wait_ge(sem("dup"), 16 * 2 * NG * (which + 1) if False else 16 * 2 * NG * 4)
                for hid in range(2):
                    unit_ready(stage, 0, hid)
                    acquire(pe, stage, 0, 2, hid)
                    t = tile_of(stage, hid)
                    w = ring[:, slot_of(stage, hid), :].rearrange("p (k m) -> p k m", k=16)
                    for l2 in range(16):
                        mm(t[:, 0:P].rearrange("p (g c) -> p g c", g=NG), w[:, l2, :],
                           od["A2"][:, which, :, 2 * l2:2 * l2 + 16 * (CB - 1) + 1:16], start=l2 == 0, stop=l2 == 15)
                    for l2 in range(16):
                        last = mm(t[:, BANK:BANK + 1], w[:, l2, :], prm(pe_)[:, l2:l2 + 1], start=l2 == 0, stop=l2 == 15)
                    last.then_inc(ps_full, 1)
                pe.wait_ge(sem("h1_full"), 2 * which + 2)
                acquire(pe, stage + "2", 0, 2, 0)
                t = tile_of(stage + "2", 0)
                if which == 0:
                    for hid in range(2):
                        last = mm(t[:, 0:P], prm("wk2").rearrange("p (a m) -> p a m", a=2)[:, hid, :], od["h1"][:, hid, :],
                                  start=hid == 0, stop=hid == 1)
                else:
                    for g in range(NG):
                        for hid in range(2):
                            last = mm(t[:, g * DH:(g + 1) * DH], od["h1v"][:, hid, g, :, :].rearrange("p a b -> p (a b)"),
                                      prm("wv2").rearrange("p (a m) -> p a m", a=2)[:, hid, :], start=hid == 0, stop=hid == 1)
                last.then_inc(ps_full, 1)
            pe.wait_ge(sem("od_full"), 5)
            with pe.Fori(0, NG) as g:
                pe.wait_ge(sem("gstaged"), g + 1)
                for i in range(4):
                    rows = slice(DH * (i % 2), DH * (i % 2) + DH)
                    for a in range(4):
                        c = i % 2 * BANK + (4 * (i // 2) + a) * CB
                        last = mm(PS[0][:, c:c + CB], ods["qs"][rows, i // 2, a * P:(a + 1) * P],
                                  ods["kcs"][rows, :], start=True, stop=True)
                last.then_inc(sem("cs_full"), 1)
                pe.wait_ge(sem("cp_full"), g + 1)
                for a in range(4):
                    last = nc.tensor.transpose(PS[1][:, a * P:(a + 1) * P], ods["P2"][:, a * P:(a + 1) * P], ident)
                last.then_inc(sem("ct_full"), 1)
                pe.wait_ge(sem("cpt_full"), g + 1)
                for a in range(4):
                    last = mm(PS[0][:, a * 256:(a + 1) * 256], ods["PTc"][:, a * P:(a + 1) * P],
                              od["Vbd"][:, bass.ds(g, 1), :].rearrange("p a b -> p (a b)"), start=True, stop=True)
                last.then_inc(sem("co_full"), 1)
                pe.wait_ge(sem("cc_full"), g + 1)

                def nsa_scores(n):
                    i = n // 2
                    rows = slice(DH * (i % 2), DH * (i % 2) + DH)
                    k_ = ods["kss" if n % 2 == 0 else "kws"]
                    for tiles in TURNS:
                        for a in tiles:
                            last = mm(scores_at(0, a), ods["qs"][rows, i // 2, a * P:(a + 1) * P], k_[rows, 0:P * (a + 1)],
                                      start=True, stop=True)
                        last.then_inc(sem("ns_s"), 1)

                rows_pe("ns", 8, g, nsa_scores,
                        lambda n, b: od["vs" if n % 2 == 0 else "vw"][:, b, bass.ds(g * DH, DH)])
            pe.wait_ge(sem("nsa_full"), 1)
            project_units("od_z", 4, uv)
            outputs_T("od_y", lambda k, a: od["o"][:, a, k * P:(k + 1) * P])
            pe.wait_ge(sem("y_full"), 16)
            project_units("oout", 4, uv)
            norm_stats("last", S, 0)

        @block.scalar
        def _(act):
            A = nc.scalar.activation
            act.wait_ge(loaded, 32)

            def squares(name, h, width):
                for k in range(KD):
                    if name in H_BASE and H_BASE[name]:
                        act.wait_ge(h_upd, H_BASE[name] - 8 + k + 1)
                    n = NORM[name] * KD + k
                    if n >= 2:
                        act.wait_ge(sq_free, n - 1)
                    A(sq[:, k % 2, 0:width], h[:, k, 0:width], ACT.Square).then_inc(sq_full, 1)

            def deviation(name, width, v0):
                pc = PC[:, :, :].rearrange("p a b -> p (a b)")
                act.wait_ge(sq_free, (NORM[name] + 1) * KD)
                A(sd[:, 0:width], pc[:, v0:v0 + width], ACT.Sqrt, bias=prm("eps"), scale=1.0 / D
                  ).then_inc(sd_full, 1)

            squares("ssd", hT, L)
            deviation("ssd", L, V0)
            act.wait_ge(sem("dtv_full"), 1)
            dtt = ssd_dt["dtt"][0:32, :]
            A(dtt, ssd_dt["dtv"][0:32, :], ACT.Abs)
            act.drain()
            A(dtt, dtt, ACT.Exp, scale=-1.0)
            act.drain()
            A(dtt, dtt, ACT.Ln, bias=1.0)
            A(ssd["ea"][0:32, :], prm("a_log", 32), ACT.Exp)
            signal(act, sem("sp_full"))

            def conv_tile(stage, it, per, j, n, dst, wait_dst=None):
                tile_wait(act, stage, it, per, j)
                A(ssd["raw"][:, CONV - 1:], tile_of(stage, j)[:, V0:V0 + L], ACT.Copy)
                signal(act, raw_full, free_of(stage, j))
                act.wait_ge(conv_full, n + 1)
                return A(dst, ssd["cv"], ACT.Silu)

            act.wait_ge(sem("raw_pad"), 1)
            for j in range(8):
                last = conv_tile("bc", 0, 8, j, j, ssd["BCt"][:, j, :])
                last.then_inc(sem("bc_full"), 1)
            act.wait_ge(sem("wdiff_full"), 1)
            A(ssd["w2"][0:META, 0, :], ssd["w2"][0:META, 0, :], ACT.Exp)
            A(ssd["w2"][:, 1:5, :], ssd["w2"][:, 1:5, :], ACT.Exp).then_inc(sem("w2_exp"), 1)
            A(ssd["dC"][:, :, :], tile_of("end", 0)[:, 0:160].rearrange("p (a b) -> p a b", a=5), ACT.Exp
              ).then_inc(free_of("end", 0), 1)
            A(ssd["eacs"][:, 1:5, :], ssd["acsT"][:, 1:5, :], ACT.Exp).then_inc(sem("dc_full"), 1)

            with act.Fori(0, GROUPS) as g:
                act.wait_ge(sem("grp_done"), g + 1)
                for q in range(4):
                    conv_tile("grp", g, GT, q, g * 4 + 8 + q, ssd["Xs"][:, q, :]).then_inc(sem("x_full"), 1)
                for q in range(4):
                    tile_wait(act, "grp", g, GT, 4 + q)
                    A(ssd["Zs"][:, q, :], tile_of("grp", 4 + q)[:, V0:V0 + L], ACT.Silu).then_inc(free_of("grp", 4 + q), 1)
                tile_wait(act, "grp", g, GT, 8)
                t = tile_of("grp", 8)
                A(ssd["Btok"][0:META, 0, :], t[0:META, BANK:BANK + P], ACT.Copy)
                A(ssd["Btok"][:, 1:5, :].rearrange("p a b -> p (a b)"), t[:, 0:BANK], ACT.Copy)
                signal(act, sem("btok_full"), free_of("grp", 8))
                act.wait_ge(sem("l0_full"), g + 1)
                A(ssd["L0"][0:META, :, :], ssd["L0"][0:META, :, :], ACT.Exp).then_inc(sem("l0_exp"), 1)
                for e in range(HPG):
                    act.wait_ge(sem("dm_full"), HPG * g + e + 1)
                    A(ssd["Dm"][:, e % 2, :], ssd["Dm"][:, e % 2, :], ACT.Exp).then_inc(sem("dm_exp"), 1)
                for q in range(4):
                    act.wait_ge(sem("y2_full"), 4 * g + q + 1)
                    if q >= 2:
                        act.wait_ge(sem("gsq_free"), 3 * g + q - 1)
                    A(sq[:, q % 2, :], ssd["yT"][:, bass.ds(4 * g + q, 1), :].rearrange("p a l -> p (a l)"), ACT.Square
                      ).then_inc(sem("gsq_full"), 1)
                tile_wait(act, "grp", g, GT, 25)
                A(sd[:, :], tile_of("grp", 25)[:, V0:V0 + L], ACT.Sqrt, bias=prm("eps"), scale=1.0 / 512)
                signal(act, sem("gsd_full"), free_of("grp", 25))

            def ffn_act(i):
                squares(f"ffn{i}", hT, L)
                deviation(f"ffn{i}", L, V0)
                act.wait_ge(sem("fpad"), i + 1)
                stage = f"ffn{i}"

                def body(it, count):
                    for r in range(count):
                        for m, raw in ((0, "rawg"), (1, "rawv")):
                            tile_wait(act, stage, it, 2 * R, 2 * r + m)
                            A(ffn[raw][:, FCONV - 1:], tile_of(stage, 2 * r + m)[:, V0:V0 + L], ACT.Copy)
                            signal(act, raw_full, free_of(stage, 2 * r + m))
                        act.wait_ge(conv_full, it * 2 * R + CONV_BASE[stage] + 2 * r + 2)
                        A(ffn["cg"], ffn["cg"], ACT.Silu).then_inc(sem("glu"), 1)
                steps(act, FT, R, body)

            ffn_act(0)

            def evacuate(stage, n, per, dst, width, func=ACT.Copy, scale=1.0, done=None):
                def body(it, count):
                    for j in range(count):
                        tile_wait(act, stage, it, per, j)
                        v0 = V0 if width == L else 0
                        A(dst[:, bass.ds(it * per + j, 1), 0:width].rearrange("p a l -> p (a l)"),
                          tile_of(stage, j)[:, v0:v0 + width], func, scale=scale).then_inc(free_of(stage, j), 1)
                steps(act, n, per, body)
                if done:
                    signal(act, sem(done))

            def evacuate_v(stage, n_units, tokens, dst, done):
                tt = -(-tokens // P)
                for r in range(n_units):
                    for t in range(tt):
                        n = min(P, tokens - t * P)
                        tile_wait(act, stage, 0, 2, r * tt + t)
                        A(dst[0:n, t, 256 * r:256 * (r + 1)], tile_of(stage, r * tt + t)[0:n, 0:256], ACT.Copy
                          ).then_inc(free_of(stage, r * tt + t), 1)
                signal(act, sem(done))

            squares("sb", hT, L)
            deviation("sb", L, V0)
            evacuate("sbk", 8, 8, sbm["kT"], L, done="qkv_full")
            act.wait_ge(sem("v_zero"), 1)
            evacuate_v("sbv", 4, L, sbm["v"], "qkv_full")
            evacuate("sbq", 8, 8, sbm["qT"], L, scale=DH ** -0.5, done="qkv_full")
            act.sem_inc(sem("w_exp"), 6)
            SEGS = [(0, 512), (512, 1024), (1024, 1344)]
            with act.Fori(0, SBH // 2) as j:
                zs = lambda e, seg: PS[e][:, seg * BANK:(seg + 1) * BANK] if seg < 2 else PC[:, e, :]
                for e in range(2):
                    A_ = sbm["A"][:, e, :]
                    for i, (a, b) in enumerate(SEGS):
                        act.wait_ge(sem("z_full"), 6 * j + 3 * e + i + 2)
                        A(A_[:, a:b], zs(e, i)[:, 0:b - a], ACT.Abs)
                    A(A_[0:META, 1344:1360], PC[0:META, e, 320:336], ACT.Abs)
                    act.drain()
                    for a, b in SEGS:
                        A(A_[:, a:b], A_[:, a:b], ACT.Exp, scale=-1.0)
                    A(A_[0:META, 1344:1360], A_[0:META, 1344:1360], ACT.Exp, scale=-1.0)
                    act.drain()
                    A(A_[0:META, 1344:1360], A_[0:META, 1344:1360], ACT.Ln, bias=1.0)
                    for i, (a, b) in enumerate(SEGS):
                        A(A_[:, a:b], A_[:, a:b], ACT.Ln, bias=1.0).then_inc(sem("l_full"), 1)
                for e in range(2):
                    W_ = sbm["W"][:, e, :]
                    for i, (a, b) in enumerate(SEGS):
                        act.wait_ge(sem("c_full"), 6 * j + 3 * e + i + 1)
                        if i == 2:
                            A(W_[0:META, 1344:1360], PC[0:META, e, 320:336], ACT.Exp)
                        A(W_[:, a:b], zs(e, i)[:, 0:b - a], ACT.Exp).then_inc(sem("w_exp"), 1)
            for k in range(8):
                tile_wait(act, "oT", 0, 2, k)
                A(uT[:, k, :], tile_of("oT", k)[:, 0:L], ACT.Copy)
                signal(act, free_of("oT", k), sem("oT_full"))
            ffn_act(1)

            squares("final", h2, S)
            deviation("final", S, 0)
            squares("even", h2, S)
            deviation("even", S, 0)
            act.wait_ge(sem("fl_v"), 1)
            t1 = ev["Pm"][0:FOXH, 1, 0:S]
            A(t1, ev["Pm"][0:FOXH, 0, 0:S], ACT.Abs)
            act.drain()
            A(t1, t1, ACT.Exp, scale=-1.0)
            act.drain()
            A(t1, t1, ACT.Ln, bias=1.0)
            signal(act, sem("fl_l"))
            for x in "fr":
                evacuate(f"ev_q{x}", 4, 4, ev[f"q{x}"], S, scale=DH ** -0.5 if x == "f" else 1.0, done="ev_full")
                evacuate(f"ev_k{x}", 4, 4, ev[f"k{x}"], S, done="ev_full")
                evacuate_v(f"ev_v{x}", 2, S, ev[f"v{x}"], "ev_full")

            def rows_act(name, per_it, it, before=None):
                for s in range(per_it + 1):
                    if s < per_it:
                        if before:
                            before(s)
                        act.wait_ge(sem(name + "_nm"), it * per_it + s + 2)
                        par_ = s % 2
                        for i, tiles in enumerate(TURNS):
                            for a in tiles:
                                p_ = ev_od[name]["Pm"][:, par_, OFF[a]:OFF[a] + P * (a + 1)]
                                A(p_, p_, ACT.Exp, bias=ev_od[name]["nm"][:, par_, a:a + 1],
                                  accum_out=ev_od[name]["rs"][:, par_, a:a + 1])
                            signal(act, sem(name + "_p"))
                    if s:
                        N = it * per_it + s - 1
                        par_ = (s - 1) % 2
                        PT = ev_od[name]["PT"][:, par_, :]
                        act.wait_ge(sem(name + "_tr"), N * 3 + 2)
                        A(PT[:, 512:1024], PS[1][:, 512:1024], ACT.Copy).then_inc(sem(name + "_pta"), 1)
                        act.wait_ge(sem(name + "_tr"), N * 3 + 3)
                        A(PT[:, 1024:1280], PC[:, 1, 0:256], ACT.Copy).then_inc(sem(name + "_pta"), 1)

            act.sem_inc(sem("fx_pta"), 1)
            act.sem_inc(sem("ns_pta"), 1)
            with act.Fori(0, 2) as it:
                rows_act("fx", 4, it)
            with act.Fori(0, 2) as it:
                for h in range(4):
                    act.wait_ge(sem("ret_o"), it * 4 + h + 1)
                    A(ev["or"].rearrange("p a (h d) -> p a h d", h=RETH)[:, :, bass.ds(it * 4 + h, 1), :].rearrange(
                        "p a h d -> p a (h d)"), PD[:, h % 2, 0:256].rearrange("p (a d) -> p a d", a=4), ACT.Copy
                      ).then_inc(sem("ret_free"), 1)
            act.wait_ge(sem("gn_d"), 1)
            A(ev["Pm"].rearrange("p a b -> p (a b)")[:, 0:2048], ev["or"].rearrange("p a b -> p (a b)"), ACT.Square)
            signal(act, sem("gn_sq"))
            act.wait_ge(sem("gn_var"), 1)
            A(ev["var"], ev["var"], ACT.Sqrt, bias=prm("gn_eps"), scale=1.0 / DH)
            signal(act, sem("gn_sd"))
            evacuate("ev_z", 8, 8, z_even, S, func=ACT.Silu, done="z_full2")
            squares("odd", h2, S)
            deviation("odd", S, 0)
            act.wait_ge(sem("g_full"), 1)
            A(od["gates"].rearrange("p a b -> p (a b)"), od["gates"].rearrange("p a b -> p (a b)"), ACT.Sigmoid)
            signal(act, sem("gates_full"))
            evacuate("od_q", 8, 8, od["q"], S, scale=DH ** -0.5, done="od_full")
            for x in ("kc", "vc", "ks", "kw"):
                evacuate(f"od_{x}", 2, 2, odr[x], S)
                act.drain()
                act.sem_inc(sem("odk_full"), 2)
            evacuate_v("od_vs", 1, S, od["vs"], "od_full")
            evacuate_v("od_vw", 1, S, od["vw"], "od_full")
            for which, stage in enumerate(("ck", "cv")):
                for hid in range(2):
                    tile_wait(act, stage, 0, 2, hid)
                    t = tile_of(stage, hid)
                    A(od["hb"][:, 2 * which + hid:2 * which + hid + 1], t[:, BANK:BANK + 1], ACT.Copy)
                    act.drain()
                    b_ = od["hb"][:, 2 * which + hid:2 * which + hid + 1]
                    if which == 0:
                        A(od["h1"][:, hid, :], t[:, 0:P], ACT.Silu, bias=b_)
                    else:
                        A(od["h1v"][:, hid, 0, :, :], t[:, 0:CB].unsqueeze(1).to_broadcast([P, 4, CB]), ACT.Silu, bias=b_)
                        for g in range(1, NG):
                            A(od["h1v"][:, hid, g, :, :], t[:, CB * g:CB * (g + 1)].unsqueeze(1).to_broadcast([P, 4, CB]),
                              ACT.Silu, bias=b_)
                    signal(act, free_of(stage, hid), sem("h1_full"))
                tile_wait(act, stage + "2", 0, 2, 0)
                t = tile_of(stage + "2", 0)
                if which == 0:
                    A(od["kcmp"], t[:, 0:P], ACT.Copy)
                else:
                    act.wait_ge(sem("vbd_zero"), 1)
                    for i in range(4):
                        rows = slice(CB * i, CB * (i + 1))
                        A(od["Vbd"][rows, :, i * DH:(i + 1) * DH], t[rows, 0:256].rearrange("p (g d) -> p g d", g=NG), ACT.Copy)
                signal(act, free_of(stage + "2", 0), sem("od_full"))
            with act.Fori(0, NG) as g:
                act.wait_ge(sem("cx_full"), g + 1)
                A(ods["X"], ods["X"], ACT.Exp)
                signal(act, sem("cx_exp"))
                act.wait_ge(sem("ct_full"), g + 1)
                A(ods["PTc"], PS[1][:, 0:512], ACT.Copy)
                signal(act, sem("cpt_full"))

                def bias(n):
                    if n % 2 == 0:
                        i = n // 2
                        if i >= 2:
                            act.wait_ge(sem("ns_nm"), g * 8 + 2 * i - 1)
                        A(ods["bias"][:, i % 2, :], prm("alibi"), ACT.Copy, scale=prm("slopes")[:, bass.ds(4 * g + i, 1)])
                        signal(act, sem("bias_full"))
                rows_act("ns", 8, g, bias)
            act.wait_ge(sem("nsa_full"), 1)
            evacuate("od_z", 8, 8, z_odd, S, func=ACT.Silu, done="z_full2")
            squares("last", h2, S)
            deviation("last", S, 0)

        @block.vector
        def _(dve):
            V = nc.vector
            for b in range(2):
                dve.sem_inc(ps_free[b], 1)
            for name, n in (("pd_free", 2), ("grp_done", 1)):
                dve.sem_inc(sem(name), n)
            dve.wait_ge(loaded, 32)

            def normalise(name, h, width, outs, h0=0):
                dve.wait_ge(sd_full, NORM[name] + 1)
                V.reciprocal(rstd[:, 0:width], sd[:, 0:width])
                dve.drain()
                for dst, gain in outs:
                    for k in range(KD):
                        V.scalar_tensor_tensor(dst[:, k, 0:width], h[:, k, h0:h0 + width], prm(gain)[:, k:k + 1],
                                               rstd[:, 0:width], ALU.mult, ALU.mult).then_inc(u_full, 1)

            V.memset(ssd["raw"][:, 0:CONV - 1], 0.0).then_inc(sem("raw_pad"), 1)
            V.memset(ssd_dt["one"][0:32, :], 1.0)
            normalise("ssd", hT, L, [(uT, "ssd_norm")])
            tile_wait(dve, "dt", 0, 2, 0)
            dtv, dtt, dt = (ssd_dt[n][0:32, :] for n in ("dtv", "dtt", "dt"))
            V.tensor_scalar(dtv, tile_of("dt", 0)[0:32, V0:V0 + L], prm("dt_bias", 32), None, ALU.add)
            signal(dve, sem("dtv_full"), free_of("dt", 0))
            dve.wait_ge(sem("sp_full"), 1)
            V.scalar_tensor_tensor(dt, dtv, 0.0, dtt, ALU.max, ALU.add)
            dve.drain()
            V.tensor_scalar(dtv, dt, ssd["ea"][0:32, :], -1.0, ALU.mult, ALU.mult)
            dve.drain()
            for at, n in CHUNKS:
                last = V.tensor_tensor_scan(acs_keep[:, at:at + n], ssd_dt["one"][0:32, at:at + n],
                                            dtv[:, at:at + n], 0.0, ALU.mult, ALU.add)
            last.then_inc(sem("acs_full"), 1)

            def conv_tile(n, tile, slot=None):
                raw, cv = ssd["raw"], ssd["cv"]
                w = lambda k: prm("conv_w")[:, bass.ds(tile * CONV + k, 1)]
                dve.wait_ge(raw_full, n + 1)
                V.tensor_scalar(cv, raw[:, 0:L], w(0), prm("conv_b")[:, bass.ds(tile, 1)], ALU.mult, ALU.add)
                for k in range(1, CONV):
                    dve.drain()
                    last = V.scalar_tensor_tensor(cv, raw[:, k:k + L], w(k), cv, ALU.mult, ALU.add)
                last.then_inc(conv_full, 1)

            for j in range(8):
                conv_tile(j, j)
            tile_wait(dve, "dtt", 0, 2, 0)
            t = tile_of("dtt", 0)
            V.tensor_copy(ssd["dtT"][0:META, 0, :], t[0:META, 0:32])
            V.tensor_copy(ssd["dtT"][:, 1:5, :], t[:, 32:160].rearrange("p (a b) -> p a b", a=4))
            V.tensor_copy(ssd["acsT"][0:META, 0, :], t[0:META, BANK:BANK + 32])
            V.tensor_copy(ssd["acsT"][:, 1:5, :], t[:, BANK + 32:BANK + 160].rearrange("p (a b) -> p a b", a=4))
            signal(dve, sem("acsT_full"), free_of("dtt", 0))
            tile_wait(dve, "end", 0, 2, 0)
            t = tile_of("end", 0)
            V.tensor_tensor(ssd["w2"][0:META, 0, :], t[0:META, 0:32], ssd["acsT"][0:META, 0, :], ALU.subtract)
            V.tensor_tensor(ssd["w2"][:, 1:5, :], t[:, 32:160].rearrange("p (a b) -> p a b", a=4),
                            ssd["acsT"][:, 1:5, :], ALU.subtract).then_inc(sem("wdiff_full"), 1)
            dve.wait_ge(sem("w2_exp"), 1)
            V.tensor_tensor(ssd["w2"][0:META, 0, :], ssd["w2"][0:META, 0, :], ssd["dtT"][0:META, 0, :], ALU.mult)
            V.tensor_tensor(ssd["w2"][:, 1:5, :], ssd["w2"][:, 1:5, :], ssd["dtT"][:, 1:5, :], ALU.mult)
            dve.drain()
            dve.wait_ge(sem("dc_full"), 1)

            Xs, Zs, S_, Dm, L0, yT = (ssd[n] for n in ("Xs", "Zs", "S", "Dm", "L0", "yT"))

            def per_head(a, n):
                return a.rearrange("p (h d) -> p h d", h=HPG)

            def of_heads(a, n, c, g):
                return a[0:n, c, bass.ds(g * HPG, HPG)].unsqueeze(2).to_broadcast([n, HPG, DH])

            with dve.Fori(0, GROUPS) as g:
                for q in range(4):
                    conv_tile(g * 4 + 8 + q, g * 4 + 8 + q)
                tile_wait(dve, "grp", g, GT, 9)
                t = tile_of("grp", 9)
                V.tensor_tensor(ssd["Gm0"][0:META, :], t[0:META, BANK:BANK + META], prm("mask_sl", META)[:, 0:META],
                                ALU.mult)
                V.tensor_tensor(ssd["Gm"][:, :, :], t[:, 0:BANK].rearrange("p (a b) -> p a b", a=4),
                                prm("mask_sl").unsqueeze(1).to_broadcast([P, 4, P]), ALU.mult
                                ).then_inc(free_of("grp", 9), 1)
                tile_wait(dve, "grp", g, GT, 10)
                V.tensor_tensor(L0[0:META, :, :],
                                tile_of("grp", 10)[0:META, 0:HPG * META].rearrange("p (h l) -> p h l", h=HPG),
                                ssd["acsT"][0:META, 0, bass.ds(g * HPG, HPG)].unsqueeze(2).to_broadcast(
                                    [META, HPG, META]), ALU.subtract).then_inc(free_of("grp", 10), 1)
                dve.drain()
                V.tensor_scalar(L0[0:META, :, :], L0[0:META, :, :], 0.0, None, ALU.min).then_inc(sem("l0_full"), 1)
                for j, cs in ((11, [0]), (12, [1, 2]), (13, [3, 4])):
                    tile_wait(dve, "grp", g, GT, j)
                    for i, c in enumerate(cs):
                        n = CHUNKS[c][1]
                        x = per_head(tile_of("grp", j)[0:n, i * BANK:(i + 1) * BANK], n)
                        V.tensor_tensor(per_head(xw2[0:n, c, :], n), x, of_heads(ssd["w2"], n, c, g), ALU.mult
                                        ).then_inc(sem("xw_full"), 1)
                        last = V.tensor_tensor(per_head(xdt[0:n, c, :], n), x, of_heads(ssd["dtT"], n, c, g), ALU.mult)
                    last.then_inc(free_of("grp", j), 1)
                for c in range(4):
                    tile_wait(dve, "grp", g, GT, 14 + c)
                    add = tile_of("grp", 14 + c)[:, 0:BANK]
                    if c == 0:
                        V.tensor_copy(S_[:, 0, :], add).then_inc(free_of("grp", 14), 1)
                    else:
                        V.tensor_tensor(per_head(S_[:, c, :], P), per_head(S_[:, c - 1, :], P),
                                        of_heads(ssd["dC"], P, c, g), ALU.mult)
                        dve.drain()
                        V.tensor_tensor(S_[:, c, :], S_[:, c, :], add, ALU.add).then_inc(free_of("grp", 14 + c), 1)
                    dve.drain()
                    dve.sem_inc(sem("state_full"), 1)
                for j in range(2):
                    tile_wait(dve, "grp", g, GT, 18 + j)
                    for i in range(2):
                        c = 1 + 2 * j + i
                        last = V.tensor_tensor(per_head(ytok[:, c, :], P),
                                               per_head(tile_of("grp", 18 + j)[:, i * BANK:(i + 1) * BANK], P),
                                               of_heads(ssd["eacs"], P, c, g), ALU.mult)
                    last.then_inc(free_of("grp", 18 + j), 1)
                dve.wait_ge(sem("l0_exp"), g + 1)
                V.tensor_tensor(L0[0:META, :, :], L0[0:META, :, :],
                                ssd["Gm0"][0:META, :].unsqueeze(1).to_broadcast([META, HPG, META]), ALU.mult
                                ).then_inc(sem("m0_full"), 1)

                def decay(e):
                    dve.wait_ge(sem("pc_full"), HPG * g + e + 1)
                    for c in range(4):
                        last = V.tensor_scalar(Dm[:, e % 2, c * P:(c + 1) * P], PC[:, e % 2, c * P:(c + 1) * P],
                                               ssd["acsT"][:, c + 1, bass.ds(g * HPG + e, 1)], 0.0,
                                               ALU.subtract, ALU.min)
                    last.then_inc(sem("dm_full"), 1)

                def weigh(e):
                    dve.wait_ge(sem("dm_exp"), HPG * g + e + 1)
                    V.tensor_tensor(Dm[:, e % 2, :], Dm[:, e % 2, :], ssd["Gm"].rearrange("p a b -> p (a b)"),
                                    ALU.mult).then_inc(sem("mt_full"), 1)

                def gather(e):
                    dve.wait_ge(sem("pd_full"), HPG * g + e + 1)
                    y = ytok[:, 1:5, e * DH:(e + 1) * DH]
                    V.tensor_tensor(y, y, PD[:, e % 2, 0:4 * DH].rearrange("p (c d) -> p c d", c=4), ALU.add
                                    ).then_inc(sem("pd_free"), 1)

                dve.drain()
                for e in range(HPG + 2):
                    if e >= 2:
                        gather(e - 2)
                    if e < HPG:
                        decay(e)
                    if 1 <= e <= HPG:
                        weigh(e - 1)
                tile_wait(dve, "grp", g, GT, 20)
                V.tensor_copy(ytok[0:META, 0, :], tile_of("grp", 20)[0:META, 0:BANK]).then_inc(free_of("grp", 20), 1)
                dve.drain()
                dve.sem_inc(sem("ytok_full"), 1)
                for q in range(4):
                    tile_wait(dve, "grp", g, GT, 21 + q)
                    V.scalar_tensor_tensor(Xs[:, q, :], Xs[:, q, :], prm("d_skip")[:, bass.ds(4 * g + q, 1)],
                                           tile_of("grp", 21 + q)[:, BANK - META:BANK - META + L],
                                           ALU.mult, ALU.add).then_inc(free_of("grp", 21 + q), 1)
                    dve.drain()
                    V.tensor_tensor(yT[:, bass.ds(4 * g + q, 1), :].rearrange("p a l -> p (a l)"), Xs[:, q, :],
                                    Zs[:, q, :], ALU.mult).then_inc(sem("y2_full"), 1)
                dve.wait_ge(sem("gsd_full"), g + 1)
                V.reciprocal(rstd[:, :], sd[:, :])
                dve.drain()
                for q in range(4):
                    y = yT[:, bass.ds(4 * g + q, 1), :].rearrange("p a l -> p (a l)")
                    V.scalar_tensor_tensor(y, y, prm("gate_norm")[:, bass.ds(4 * g + q, 1)], rstd[:, :],
                                           ALU.mult, ALU.mult).then_inc(sem("yT_full"), 1)
                dve.sem_inc(sem("grp_done"), 1)
            dve.drain()

            def residual(stage, n, per):
                def body(it, count):
                    for j in range(count):
                        tile_wait(dve, stage, it, per, j)
                        h = hT[:, bass.ds(it * per + j, 1), :].rearrange("p a l -> p (a l)")
                        V.tensor_tensor(h, h, tile_of(stage, j)[:, V0:V0 + L], ALU.add).then_inc(free_of(stage, j), 1)
                        dve.drain()
                        dve.sem_inc(h_upd, 1)
                steps(dve, n, per, body)

            residual("sout", 8, R)

            def ffn_dve(i):
                stage = f"ffn{i}"
                for raw in ("rawg", "rawv"):
                    last = V.memset(ffn[raw][:, 0:FCONV - 1], 0.0)
                last.then_inc(sem("fpad"), 1)
                normalise(stage, hT, L, [(uT, f"ffn_norm{i}")])

                def body(it, count):
                    for r in range(count):
                        for m, (raw, cv) in enumerate((("rawg", "cg"), ("rawv", "cvv"))):
                            w = lambda k: prm(f"fconv_w{i}")[:, bass.ds((it * 2 * R + 2 * r + m) * FCONV + k, 1)]
                            b = prm(f"fconv_b{i}")[:, bass.ds(it * 2 * R + 2 * r + m, 1)]
                            dve.wait_ge(raw_full, it * 2 * R + CONV_BASE[stage] + 2 * r + m + 1)
                            V.tensor_scalar(ffn[cv], ffn[raw][:, 0:L], w(0), b, ALU.mult, ALU.add)
                            for k in range(1, FCONV):
                                dve.drain()
                                last = V.scalar_tensor_tensor(ffn[cv], ffn[raw][:, k:k + L], w(k), ffn[cv],
                                                              ALU.mult, ALU.add)
                            last.then_inc(conv_full, 1)
                        dve.wait_ge(sem("glu"), it * R + FT * i + r + 1)
                        V.tensor_tensor(ffn["act"][:, bass.ds(it * R + r, 1), :].rearrange("p a l -> p (a l)"),
                                        ffn["cg"], ffn["cvv"], ALU.mult).then_inc(sem("act_full"), 1)
                        dve.drain()
                steps(dve, FT, R, body)
                residual(f"down{i}", 8, 2)

            ffn_dve(0)


            V.memset(sbm["v"][:, 4, :], 0.0)
            V.tensor_copy(ident_b[:, :], ident)
            V.tensor_copy(hidden_b[:, :], prm("hidden"))
            V.memset(sbm["W"][:, :, :], 0.0)
            signal(dve, sem("v_zero"))
            normalise("sb", hT, L, [(uT, "kv_norm"), (u2, "sb_norm")])
            for name in ("o_free",):
                dve.sem_inc(sem(name), 2)
            SEGS = [(0, 512), (512, 1024), (1024, 1344)]
            TAIL = slice(1344, 1360)
            with dve.Fori(0, SBH // 2) as j:
                zs = lambda e, seg: PS[e][:, seg * BANK:(seg + 1) * BANK] if seg < 2 else PC[:, e, :]
                for e in range(2):
                    for i, (a, b) in enumerate(SEGS):
                        dve.wait_ge(sem("l_full"), 6 * j + 3 * e + i + 1)
                        if i == 2:
                            V.scalar_tensor_tensor(sbm["SP"][0:META, e, TAIL], PC[0:META, e, 320:336], 0.0,
                                                   sbm["A"][0:META, e, TAIL], ALU.max, ALU.add)
                        V.scalar_tensor_tensor(sbm["SP"][:, e, a:b], zs(e, i)[:, 0:b - a], 0.0, sbm["A"][:, e, a:b],
                                               ALU.max, ALU.add).then_inc(sem("sp_full2"), 1)
                for e in range(2):
                    dve.wait_ge(sem("o_full"), 2 * j + e + 1)
                    V.tensor_copy(sbm["o"][0:META, 4, bass.ds((2 * j + e) * DH, DH)], PD[0:META, e, 256:320])
                    V.tensor_copy(sbm["o"][:, 0:4, bass.ds((2 * j + e) * DH, DH)],
                                  PD[:, e, 0:256].rearrange("p (a d) -> p a d", a=4)).then_inc(sem("o_free"), 1)
            residual("wo", 8, R)
            ffn_dve(1)

            def residual2(stage):
                for j in range(8):
                    tile_wait(dve, stage, 0, 8, j)
                    V.tensor_tensor(h2[:, j, :], h2[:, j, :], tile_of(stage, j)[:, 0:S], ALU.add)
                    signal(dve, free_of(stage, j), h_upd)

            dve.wait_ge(sd_full, NORM["final"] + 1)
            V.reciprocal(rstd[:, 0:S], sd[:, 0:S])
            dve.drain()
            for k in range(KD):
                V.scalar_tensor_tensor(h2[:, k, :], h2[:, k, :], prm("final_norm")[:, k:k + 1], rstd[:, 0:S],
                                       ALU.mult, ALU.mult).then_inc(h_upd, 1)
            dve.drain()
            normalise("even", h2, S, [(uv, "even_norm")])
            fv, fl = ev["Pm"][0:FOXH, 0, 0:S], ev["Pm"][0:FOXH, 1, 0:S]
            tile_wait(dve, "ev_f", 0, 2, 0)
            V.tensor_scalar(fv, tile_of("ev_f", 0)[0:FOXH, 0:S], prm("b_f", FOXH), None, ALU.add)
            V.memset(ev["PT"][0:FOXH, 0, 0:S], 1.0)
            signal(dve, sem("fl_v"), free_of("ev_f", 0))
            dve.wait_ge(sem("fl_l"), 1)
            V.tensor_scalar(fv, fv, 0.0, None, ALU.min)
            dve.drain()
            V.tensor_tensor(fl, fl, fv, ALU.subtract)
            dve.drain()
            V.tensor_tensor_scan(ev["negc"][0:FOXH, :], ev["PT"][0:FOXH, 0, 0:S], fl, 0.0, ALU.mult, ALU.add)
            signal(dve, sem("negc_full"))

            def rows_dve(name, per_it, it, table, finish):
                m = ev_od[name]
                for s in range(per_it + 1):
                    par_ = s % 2
                    if s < per_it:
                        N = it * per_it + s
                        t_ = table(s)
                        for i, tiles in enumerate(TURNS):
                            dve.wait_ge(sem(name + "_s"), N * 3 + i + 1)
                            dve.sem_inc(sem(name + "_seen"), 1)
                            for a in tiles:
                                w = P * (a + 1)
                                V.tensor_tensor_reduce(out=m["Pm"][:, par_, OFF[a]:OFF[a] + w], in0=scores_at(0, a),
                                                       in1=t_[:, 512 - w:512], scale=1.0, scalar=-3e38, op0=ALU.add,
                                                       op1=ALU.max, accum_out=m["nm"][:, par_, a:a + 1])
                        dve.drain()
                        V.tensor_scalar(m["nm"][:, par_, :], m["nm"][:, par_, :], -1.0, None, ALU.mult
                                        ).then_inc(sem(name + "_nm"), 1)
                    if s:
                        N = it * per_it + s - 1
                        q = (s - 1) % 2
                        dve.wait_ge(sem(name + "_tr"), N * 3 + 1)
                        V.tensor_copy(m["PT"][:, q, 0:512], PS[1][:, 0:512]).then_inc(sem(name + "_ptd"), 1)
                        dve.wait_ge(sem(name + "_o"), N + 1)
                        V.reciprocal(m["ri"][:, q, :], m["rs"][:, q, :])
                        dve.drain()
                        finish(s - 1, q)
                        signal(dve, sem(name + "_comb"))

            for name in ("fx", "ns"):
                dve.sem_inc(sem(name + "_nm"), 1)
                dve.sem_inc(sem(name + "_ptd"), 1)
                dve.sem_inc(sem(name + "_comb"), 2)
            dve.sem_inc(sem("ret_m"), 2)
            dve.sem_inc(sem("ret_free"), 2)
            with dve.Fori(0, 2) as it:
                def fox_out(h, q):
                    V.tensor_tensor(ev["of"][:, :, bass.ds((it * 4 + h) * DH, DH)],
                                    PD[:, q, 0:256].rearrange("p (a d) -> p a d", a=4),
                                    ev["ri"][:, q, :].unsqueeze(2).to_broadcast([P, 4, DH]), ALU.mult)
                rows_dve("fx", 4, it, lambda s: prm("causal"), fox_out)
            dve.wait_ge(sem("decay_in"), 16)
            with dve.Fori(0, 2) as it:
                for h in range(4):
                    dve.drain()
                    dve.wait_ge(sem("ret_s"), it * 4 + h + 1)
                    for i in (0, 1, 3, 2):
                        w = S - P * i
                        last = V.tensor_tensor(ev["Pm"][:, h % 2, DOFF[i]:DOFF[i] + w], decayed_at(h % 2, i),
                                               ev["decay"][:, bass.ds(it * 4 + h, 1), 0:w].rearrange("p a b -> p (a b)"),
                                               ALU.mult)
                    last.then_inc(sem("ret_m"), 1)
            rt = ev["or"].rearrange("p a (h d) -> p (a h) d", h=RETH)
            dve.wait_ge(sem("ret_free"), 10)
            V.tensor_reduce(ev["mu"], rt, AX.X, ALU.add)
            dve.drain()
            V.tensor_scalar(ev["mu"], ev["mu"], 1.0 / DH, None, ALU.mult)
            dve.drain()
            V.tensor_tensor(rt, rt, ev["mu"].unsqueeze(2).to_broadcast([P, 32, DH]), ALU.subtract)
            signal(dve, sem("gn_d"))
            dve.wait_ge(sem("gn_sq"), 1)
            V.tensor_reduce(ev["var"], ev["Pm"].rearrange("p a b -> p (a b)")[:, 0:2048].rearrange(
                "p (a d) -> p a d", a=32), AX.X, ALU.add)
            signal(dve, sem("gn_var"))
            dve.wait_ge(sem("gn_sd"), 1)
            V.reciprocal(ev["mu"], ev["var"])
            dve.drain()
            V.tensor_tensor(rt, rt, ev["mu"].unsqueeze(2).to_broadcast([P, 32, DH]), ALU.mult)
            signal(dve, sem("mix_full"))

            def gated(stage, z, gn):
                dve.wait_ge(sem("z_full2"), 1 if gn else 2)
                for k in range(8):
                    tile_wait(dve, stage, 0, 2, k)
                    t = tile_of(stage, k)[:, 0:S]
                    if gn and k >= 4:
                        V.scalar_tensor_tensor(uv[:, k, :], t, prm("gn_g")[:, k - 4:k - 3], z[:, k, :], ALU.mult, ALU.mult)
                    else:
                        V.tensor_tensor(uv[:, k, :], t, z[:, k, :], ALU.mult)
                    signal(dve, free_of(stage, k), sem("y_full"))

            gated("ev_y", z_even, True)
            residual2("eout")
            V.memset(od["A2"].rearrange("p a b c -> p (a b c)"), 0.0)
            V.memset(od["Vbd"][:, :, :], 0.0)
            signal(dve, sem("pad2"), sem("vbd_zero"))
            normalise("odd", h2, S, [(uv, "odd_norm")])
            tile_wait(dve, "od_g", 0, 2, 0)
            V.tensor_tensor(od["gates"][:, :, :].rearrange("p c a -> p a c"),
                            tile_of("od_g", 0)[:, 0:192].rearrange("p (a c) -> p a c", a=4),
                            prm("b_gate").unsqueeze(1).to_broadcast([P, 4, 48]), ALU.add)
            signal(dve, sem("g_full"), free_of("od_g", 0))
            dve.wait_ge(sem("gates_full"), 1)
            dve.wait_ge(sem("cmp_in"), 16)
            with dve.Fori(0, NG) as g:
                def gate(b):
                    v = od["gates"].rearrange("p (h b) a -> p h b a", b=3)
                    return v[:, bass.ds(4 * g, 4), b, :]

                X, P2 = ods["X"], ods["P2"]
                dve.wait_ge(sem("cs_full"), g + 1)
                V.tensor_tensor(X.rearrange("p (j e c) -> p e j c", j=2, e=2),
                                PS[0].rearrange("p (e k) -> p e k", e=2)[:, :, 0:256].rearrange("p e (j c) -> p e j c", j=2),
                                od["cmp_bias"][:, bass.ds(4 * g, 4), :].rearrange("p (j e) c -> p e j c", j=2), ALU.add)
                dve.drain()
                X3 = X.rearrange("p (a c) -> p a c", a=16)
                V.tensor_reduce(od["mxc"], X3, AX.X, ALU.max)
                dve.drain()
                V.tensor_tensor(X3, X3, od["mxc"].unsqueeze(2).to_broadcast([P, 16, CB]), ALU.subtract)
                signal(dve, sem("cx_full"))
                dve.wait_ge(sem("cx_exp"), g + 1)
                V.tensor_reduce(od["rsc"], X3, AX.X, ALU.add)
                V.tensor_tensor(P2.rearrange("p (a i c) -> p i a c", a=4, i=4), X.rearrange("p (i a c) -> p i a c", i=4, a=4),
                                prm("cmp_seen").rearrange("p (a c) -> p a c", a=4).unsqueeze(1).to_broadcast([P, 4, 4, CB]),
                                ALU.mult)
                signal(dve, sem("cp_full"))
                V.reciprocal(od["rsc"], od["rsc"])
                dve.drain()
                V.tensor_tensor(od["cfc"].rearrange("p (i a) -> p i a", i=4), od["rsc"].rearrange("p (i a) -> p i a", i=4),
                                gate(0), ALU.mult)
                dve.drain()
                dve.wait_ge(sem("co_full"), g + 1)
                V.tensor_tensor(od["o"].rearrange("p a (h d) -> p a h d", d=DH)[:, :, bass.ds(4 * g, 4), :],
                                PS[0][:, :].rearrange("p (a i d) -> p a i d", a=4, i=4),
                                od["cfc"].rearrange("p (i a) -> p a i", i=4).unsqueeze(3).to_broadcast([P, 4, 4, DH]),
                                ALU.mult)
                signal(dve, sem("cc_full"))

                def table(n):
                    if n % 2 == 0:
                        dve.wait_ge(sem("bias_full"), 4 * g + n // 2 + 1)
                    return ods["bias"][:, n // 2 % 2, :]

                def add_out(n, q):
                    i, b = n // 2, 1 + n % 2
                    gt = od["gates"].rearrange("p (h b) a -> p h b a", b=3)[:, bass.ds(4 * g + i, 1), b, :]
                    V.tensor_tensor(od["ri"][:, q, :], od["ri"][:, q, :], gt.rearrange("p h a -> p (h a)"), ALU.mult)
                    dve.drain()
                    tmp = od["nm"]
                    t_ = ods["X"][:, 0:256].rearrange("p (a d) -> p a d", a=4)
                    V.tensor_tensor(t_, PD[:, q, 0:256].rearrange("p (a d) -> p a d", a=4),
                                    od["ri"][:, q, :].unsqueeze(2).to_broadcast([P, 4, DH]), ALU.mult)
                    dve.drain()
                    o_ = od["o"][:, :, bass.ds((4 * g + i) * DH, DH)]
                    V.tensor_tensor(o_, o_, t_, ALU.add)
                rows_dve("ns", 8, g, table, add_out)
            signal(dve, sem("nsa_full"))
            gated("od_y", z_odd, False)
            residual2("oout")
            normalise("last", h2, S, [(uv, "final_g")])

        @block.gpsimd
        def _(pool):
            G = nc.gpsimd
            pool.wait_ge(loaded, 32)
            pool.wait_ge(sem("bc_full"), 8)
            with pool.Fori(0, GROUPS) as g:
                pool.wait_ge(sem("grp_done"), g + 1)
                G.tensor_copy(ssd["Bs"], ssd["BCt"][:, bass.ds(g, 1), :].rearrange("p a l -> p (a l)"))
                G.tensor_copy(ssd["Cs"], ssd["BCt"][:, bass.ds(g + GROUPS, 1), :].rearrange("p a l -> p (a l)"))
                G.tensor_copy(ssd["sel"][0:32, :, :], ident[0:32, bass.ds(g * HPG, HPG)].unsqueeze(2).to_broadcast(
                    [32, HPG, P])).then_inc(sem("bc_staged"), 1)

            pool.sem_inc(sem("z_full"), 1)
            pool.wait_ge(sem("qkv_full"), 3)

            with pool.Fori(0, SBH // 2) as j:
                pool.wait_ge(sem("z_full"), 6 * j + 1)
                G.tensor_copy(sbm["ks"], sbm["kT"][:, bass.ds(j, 1), :].rearrange("p a l -> p (a l)"))
                G.tensor_copy(sbm["qs"], sbm["qT"][:, bass.ds(j, 1), :].rearrange("p a l -> p (a l)")
                              ).then_inc(sem("staged"), 1)

            pool.wait_ge(sem("ev_full"), 6)
            with pool.Fori(0, 2) as it:
                pool.wait_ge(sem("fx_nm"), it * 4 + 1)
                G.tensor_copy(ev["qs"], ev["qf"][:, bass.ds(2 * it, 2), :])
                G.tensor_copy(ev["ks"], ev["kf"][:, bass.ds(2 * it, 2), :])
                G.tensor_copy(ev["sel"][0:FOXH, :, :], ident[0:FOXH, bass.ds(4 * it, 4)].unsqueeze(2).to_broadcast(
                    [FOXH, 4, P])).then_inc(sem("fstaged"), 1)
            pool.wait_ge(sem("fx_nm"), 9)
            with pool.Fori(0, 2) as it:
                pool.wait_ge(sem("ret_m"), it * 4 + 2)
                G.tensor_copy(ev["qs"], ev["qr"][:, bass.ds(2 * it, 2), :])
                G.tensor_copy(ev["ks"], ev["kr"][:, bass.ds(2 * it, 2), :]).then_inc(sem("fstaged"), 1)
            pool.wait_ge(sem("od_full"), 5)
            pool.wait_ge(sem("dup"), 16 * 8 * NG)
            with pool.Fori(0, NG) as g:
                pool.wait_ge(sem("ns_nm"), g * 8 + 1)
                G.tensor_copy(ods["qs"], od["q"][:, bass.ds(2 * g, 2), :])
                G.tensor_copy(ods["kss"], od["ksd"][:, bass.ds(g, 1), :].rearrange("p a b -> p (a b)"))
                G.tensor_copy(ods["kws"], od["kwd"][:, bass.ds(g, 1), :].rearrange("p a b -> p (a b)"))
                G.tensor_copy(ods["kcs"], od["kcmp"][:, bass.ds(g * CB, CB)]).then_inc(sem("gstaged"), 1)


TILES_PER_UNIT = {"sout": 1, "sbv": 5, "down0": 0.5, "down1": 0.5, "ev_vf": 4, "ev_vr": 4, "od_vs": 4,
                  "od_vw": 4, "ck": 1, "cv": 1}
TILE_STEP = {"grp": GT, "down0": 2, "down1": 2}
CONV_BASE = {"ffn0": 24, "ffn1": 24 + 2 * FT}


def tile_w(w, kt, m0, m1):
    return w[:, m0:m1].reshape(kt, P, m1 - m0).transpose(1, 0, 2).reshape(P, -1)


def pack(i):
    f = np.float32
    W = i["ssd_w_in"][0]
    cols = lambda w, a, n, step=256: [tile_w(w, KD, a + step * u, a + step * (u + 1)) for u in range(n)]
    units = cols(W, 2 * DI, 4)
    for g in range(GROUPS):
        units += cols(W, DI + 512 * g, 2) + cols(W, 512 * g, 2)
    units += [tile_w(i["ssd_w_out"][0], 16, P * m, P * (m + 1)) for m in range(8)]

    def up(l):
        w = i["ffn_w_up"][l]
        F = FT * P
        return [tile_w(np.concatenate([w[:, P * j:P * j + P], w[:, F + P * j:F + P * j + P]], 1), KD, 0, 256)
                for j in range(FT)]
    units += up(0)
    kv = i["w_kv"]
    units += cols(kv, 0, 4) + cols(kv, D, 4) + cols(i["sb_w_q"][0], 0, 4) + cols(i["sb_w_o"][0], 0, 4) + up(1)
    ev = i["even_w_in_2"][0]
    for a in (0, 512, 1024, 1544, 2056, 2568):
        units += cols(ev, a, 2)
    units += cols(ev, 3080, 4) + cols(i["even_w_out_2"][0], 0, 4)
    od = i["odd_w_in_2"][0]
    units += cols(od, 0, 4)
    for n in (0, 1, 2, 4, 3, 5):
        units += cols(od, 1024 + 256 * n, 1)
    for w in (i["odd_wk1_2"][0], i["odd_wv1_2"][0]):
        units += [tile_w(w, 16, P * m, P * (m + 1)) for m in range(2)]
    units += cols(od, 2608, 4) + cols(i["odd_w_out_2"][0], 0, 4)
    stream = np.stack(units)
    down = np.stack([tile_w(i["ffn_w_down"][l][DK * P * half:DK * P * (half + 1)], DK, P * m, P * (m + 1))
                     for l in range(2) for m in range(8) for half in range(2)])

    par = np.zeros((P, N_PARAMS), f)

    def put(name, a, rows=P):
        at, n = PARAMS[name]
        par[0:rows, at:at + n] = np.asarray(a).reshape(rows, n)

    col = lambda v: v.reshape(-1, P).T
    for name, v in (("ssd_norm", i["ssd_norm"][0]), ("kv_norm", i["kv_norm"]), ("sb_norm", i["sb_norm"][0]),
                    ("ffn_norm0", i["ffn_norm"][0]), ("ffn_norm1", i["ffn_norm"][1]),
                    ("final_norm", i["final_norm"]), ("even_norm", i["even_norm_g_2"][0]),
                    ("odd_norm", i["odd_norm_g_2"][0]), ("final_g", i["final_g_2"]),
                    ("gate_norm", i["ssd_gate_norm"][0]), ("gn_g", i["even_gn_g_2"][0])):
        put(name, col(v))
    order = np.concatenate([np.arange(DI, DI + 1024), np.arange(DI)])
    put("conv_w", i["ssd_conv_w"][0][:, order].reshape(CONV, 24, P).transpose(2, 1, 0))
    put("conv_b", col(i["ssd_conv_b"][0][order]))
    for l in range(2):
        w = i["ffn_conv_w"][l].reshape(FCONV, 2, FT, P)
        put(f"fconv_w{l}", w.transpose(3, 2, 1, 0))
        put(f"fconv_b{l}", i["ffn_conv_b"][l].reshape(2, FT, P).transpose(2, 1, 0))
    put("d_skip", np.repeat(i["ssd_d_skip"][0], DH).reshape(16, P).T)
    put("dt_bias", i["ssd_dt_bias"][0], 32)
    put("a_log", i["ssd_a_log"][0], 32)
    put("w_dt", tile_w(W, KD, 2 * DI + 1024, 2 * DI + 1056))
    put("w_f", tile_w(ev, KD, 1536, 1544))
    put("w_gate", tile_w(od, KD, 2560, 2608))
    put("b_f", i["even_b_f_2"][0], 8)
    put("b_gate", np.broadcast_to(i["odd_b_gate_2"][0], (P, 48)))
    for name, v in (("pe_k", i["odd_pe_k_2"][0]), ("pe_v", i["odd_pe_v_2"][0])):
        put(name, v.reshape(16, P).T)
    wk2 = i["odd_wk2_2"][0].reshape(2, P, DH).transpose(1, 0, 2)
    put("wk2", np.concatenate([wk2, wk2], 2))
    put("wv2", i["odd_wv2_2"][0].reshape(2, P, DH).transpose(1, 0, 2))
    r = np.arange(P)
    put("ident", np.eye(P, dtype=f))
    put("ones", np.ones((P, P), f))
    put("neg_tri", np.where(r[:, None] >= r[None, :], -1.0, 0.0))
    put("neg_ones", -np.ones((P, P), f))
    put("pick127", np.repeat((r == 127)[:, None], P, 1))
    put("pick15", np.repeat((r == 15)[:, None], P, 1))
    put("mask_sl", r[:, None] <= r[None, :])
    put("hidden", np.where(r[None, :] <= r[:, None], -BIG, 0.0))
    put("eps", np.full((P, 1), EPS))
    put("gn_eps", np.full((P, 1), GN_EPS))
    slopes = (2.0 ** (-8.0 * (np.arange(NH) + 1) / NH)).astype(f)
    put("slopes", np.broadcast_to(slopes, (P, NH)))
    sigma = np.arange(512) - 384
    seen = sigma[None, :] <= r[:, None]
    put("alibi", np.where(seen, sigma[None, :] - r[:, None], -BIG))
    put("causal", np.where(seen, 0.0, -BIG))
    t = r[:, None, None] + P * np.arange(4)[None, :, None]
    c_end = 16 * np.arange(CB)[None, None, :] + 31
    ok = (c_end <= t) & (np.arange(CB) < N_CMP)[None, None, :]
    put("cmp_seen", ok.astype(f))
    tab = np.zeros((P, N_TABLES), f)
    lg = np.log(1.0 - 2.0 ** (-5.0 - np.arange(RETH)))
    tau = np.arange(512)[None, None, :] - r[:, None, None]
    dec = np.where(tau >= 0, np.exp(lg[None, :, None] * np.maximum(tau, 0)), 0.0).astype(f) * f(DH ** -0.5)
    tab[:, 0:RETH * 512] = dec.reshape(P, -1)
    bias = np.where(ok[:, None], -slopes[None, :, None, None] * (t - c_end).astype(f)[:, None], f(-BIG))
    tab[:, RETH * 512:] = bias.reshape(P, -1)
    x = np.concatenate([i["meta_tokens"], i["x"][0]], 0)
    xT = x.T.reshape(KD, P, L).transpose(1, 0, 2).reshape(P, KD * L)
    c = np.ascontiguousarray
    return {"x_in": c(xT), "stream": c(stream), "down": c(down), "params": par, "tables": tab}


def kernel(**inputs):
    import concourse.bacc as bacc
    from concourse.bass_utils import run_bass_kernel_spmd

    nc = bacc.Bacc("TRN2", target_bir_lowering=False, num_devices=1)
    arrays = pack({k: np.asarray(v) for k, v in inputs.items()})
    aps = [nc.dram_tensor(n, arrays[n].shape, F32, kind="ExternalInput").ap()
           for n in ("x_in", "stream", "down", "params", "tables")]
    out = nc.dram_tensor("out", (P, KD * S), F32, kind="ExternalOutput").ap()
    build(nc, *aps, out)
    got = run_bass_kernel_spmd(nc, [arrays], core_ids=[0]).results[0]["out"]
    return got.reshape(P, KD, S).transpose(2, 1, 0).reshape(1, S, D)
```

```python
from contextlib import ExitStack

import numpy as np

import concourse.bass as bass
from concourse import mybir

F32 = mybir.dt.float32
ACT = mybir.ActivationFunctionType
ALU = mybir.AluOpType
AX = mybir.AxisListType

P = 128
D = 1024
KD = D // P
META = 16
S = 512
L = META + S
LH = L // 2
BANK = 512
EPS = 1e-6
GN_EPS = 1e-5
BIG = 1e30

GROUPS = 4
HPG = 8
HEADS = 32
DI = 2048
CHUNKS = [(0, META)] + [(META + P * c, P) for c in range(4)]
CONV = 4
FT = 22
FCONV = 3
SBH = 16
DH = 64
FOXH = 8
RETH = 8
NH = 16
NG = 4
CB = 32
N_CMP = 31

R = 4
SLOT = 2048
DK = FT // 2


def layout(fields):
    at, out = 0, {}
    for name, width in fields:
        out[name] = (at, width)
        at += width
    return out, at


PARAMS, N_PARAMS = layout([
    ("ssd_norm", 8), ("kv_norm", 8), ("sb_norm", 8), ("ffn_norm0", 8), ("ffn_norm1", 8),
    ("final_norm", 8), ("even_norm", 8), ("odd_norm", 8), ("final_g", 8), ("gate_norm", 16),
    ("conv_w", 24 * CONV), ("conv_b", 24), ("fconv_w0", 2 * FT * FCONV), ("fconv_b0", 2 * FT),
    ("fconv_w1", 2 * FT * FCONV), ("fconv_b1", 2 * FT), ("d_skip", 16), ("dt_bias", 1), ("a_log", 1),
    ("w_dt", 8 * 32), ("w_f", 8 * 8), ("w_gate", 8 * 48), ("b_f", 1), ("b_gate", 48), ("gn_g", 4),
    ("pe_k", 16), ("pe_v", 16), ("wk2", 256), ("wv2", 128),
    ("ident", P), ("ones", P), ("neg_tri", P), ("neg_ones", P), ("pick127", P), ("pick15", P),
    ("mask_sl", P), ("hidden", P), ("eps", 1), ("gn_eps", 1), ("slopes", NH), ("alibi", 512), ("causal", 512),
    ("cmp_seen", 4 * CB),
])
TABLES, N_TABLES = layout([("decay", RETH * 512), ("cmp_bias", NH * 4 * CB)])

STREAM = [("bc", 4), ("grp", 16), ("sout", 8), ("ffn0a", 11), ("down0a", 8), ("ffn0b", 11), ("down0b", 8),
          ("sbk", 4), ("sbv", 4), ("sbq", 4), ("wo", 4),
          ("ffn1a", 11), ("down1a", 8), ("ffn1b", 11), ("down1b", 8),
          ("ev_qf", 2), ("ev_kf", 2), ("ev_vf", 2), ("ev_qr", 2), ("ev_kr", 2), ("ev_vr", 2),
          ("ev_z", 4), ("eout", 4),
          ("od_q", 4), ("od_kc", 1), ("od_vc", 1), ("od_ks", 1), ("od_kw", 1), ("od_vs", 1),
          ("od_vw", 1), ("ck", 2), ("cv", 2), ("od_z", 4), ("oout", 4)]
GT = 26
TILES = [("dt", 1), ("bc", 8), ("dtt", 1), ("end", 1), ("grp", 4 * GT), ("sout", 8),
         ("ffn0a", 22), ("down0a", 8), ("ffn0b", 22), ("down0b", 8),
         ("sbk", 8), ("sbv", 20), ("sbq", 8), ("oT", 8), ("wo", 8),
         ("ffn1a", 22), ("down1a", 8), ("ffn1b", 22), ("down1b", 8),
         ("ev_f", 1), ("ev_qf", 4), ("ev_kf", 4), ("ev_vf", 8), ("ev_qr", 4), ("ev_kr", 4), ("ev_vr", 8),
         ("ev_z", 8), ("ev_y", 8), ("eout", 8),
         ("od_g", 1), ("od_q", 8), ("od_kc", 2), ("od_vc", 2), ("od_ks", 2), ("od_kw", 2),
         ("od_vs", 4), ("od_vw", 4), ("ck", 2), ("ck2", 1), ("cv", 2), ("cv2", 1),
         ("od_z", 8), ("od_y", 8), ("oout", 8)]


SPLIT_RUNS = [("ffn0a", "sbq"), ("wo", "ev_vr"), ("ev_z", "od_vw"), ("od_z", "oout")]


def bases(pairs):
    at, out = 0, {}
    for name, n in pairs:
        out[name] = at
        at += n
    return out, at


U0, N_UNITS = bases(STREAM)
M0, N_TILES = bases(TILES)
RUN_OF = {}
H0 = {}
N0 = {}
_run, _n, _m = None, 0, 0
for _stage, _units in STREAM:
    for _i, (_a, _b) in enumerate(SPLIT_RUNS):
        if _a == _stage:
            _run = _i
    if _run is not None:
        RUN_OF[_stage], H0[_stage] = _run, _n
        _n += _units
        if SPLIT_RUNS[_run][1] == _stage:
            _run = None
    else:
        N0[_stage] = _m
        _m += _units


def build(nc, x_in, stream, down, params_in, tables_in, out):
    ctx = ExitStack()
    with ctx:
        def sb(name, shape):
            return ctx.enter_context(nc.sbuf_tensor(name, shape, F32))

        rounded = {}

        def sb_at(name, shape):
            at = -(-nc.sbuf_base // 32) * 32
            return sb(name, shape), at

        def round_over(of, at, first, cols):
            t = nc.alloc_sbuf_tensor_at(f"{of}_r{first}", [P, cols], mybir.dt.float32r, offset=at + 4 * first)
            rounded.setdefault(of, []).append((first, cols, t))

        sems = {}

        def sem(name):
            if name not in sems:
                sems[name] = ctx.enter_context(nc.semaphore(name))
            return sems[name]

        ring, ring_at = sb_at("ring", [P, R, SLOT])
        par = sb("par", [P, N_PARAMS])
        hT = sb("hT", [P, KD, L])
        uT, uT_at = sb_at("uT", [P, KD, L])
        sq = sb("sq", [P, 2, L])
        sd = sb("sd", [P, L])
        rstd = sd
        ARENA = 30864
        HS = 2
        HRING = ARENA - HS * SLOT
        UH = HRING - KD * L
        arena, arena_at = sb_at("arena", [P, ARENA])
        ident_b = ctx.enter_context(nc.sbuf_tensor("ident_b", [P, P], mybir.dt.bfloat16))
        hidden_b = ctx.enter_context(nc.sbuf_tensor("hidden_b", [P, P], mybir.dt.bfloat16))
        PS = [ctx.enter_context(nc.psum_tensor(f"PS{i}", [P, 2 * BANK], F32)) for i in range(2)]
        PC = ctx.enter_context(nc.psum_tensor("PC", [P, 2, BANK], F32))
        PD = ctx.enter_context(nc.psum_tensor("PD", [P, 2, BANK], F32))

        def prm(name, rows=P):
            at, n = PARAMS[name]
            return par[0:rows, at:at + n]

        def carve(fields):
            at, views = 0, {}
            for name, *dims in fields:
                n = int(np.prod(dims))
                v = arena[:, at:at + n]
                if len(dims) == 2:
                    v = v.rearrange("p (a b) -> p a b", a=dims[0])
                elif len(dims) == 3:
                    v = v.rearrange("p (a b c) -> p a b c", a=dims[0], b=dims[1])
                elif len(dims) == 4:
                    v = v.rearrange("p (a b c d) -> p a b c d", a=dims[0], b=dims[1], c=dims[2])
                views[name] = v
                at += n
            assert at <= ARENA, at
            return views

        U2 = 2 * KD * L + 5 * D
        TAILS = 2 * KD * L + 10 * D + 2 * L
        round_over("ring", ring_at, HS * SLOT, HS * SLOT)
        round_over("uT", uT_at, 0, KD * L)
        for first, cols in ((0, 2 * DK * L), (U2, KD * L), (TAILS, 2 * KD * P), (UH, ARENA - UH)):
            round_over("arena", arena_at, first, cols)

        def r32(ap, first=None):
            for at, cols, t in rounded[ap.tensor.name]:
                if at == first or first is None and at <= ap.offset < at + cols:
                    return bass.AP(tensor=t, offset=ap.offset - at if at else ap.offset,
                                   ap=((cols, P),) + tuple(ap.ap)[1:])

        def split(ap, first=None):
            return r32(ap, first).bitcast(F32)

        uh = arena[:, UH:UH + KD * L].rearrange("p (k l) -> p k l", k=KD)
        uhs = uh[:, :, 0:S]

        def raw_slot(n):
            return ring[:, n % HS, :]

        def rest_slot(n):
            return ring[:, HS + n % HS, :]

        def high_slot(n):
            return arena[:, HRING + n % HS * SLOT:HRING + (n % HS + 1) * SLOT]

        def width_of(stage):
            return DK * P if stage.startswith("down") else SLOT

        def stage_at(u):
            stage = [n for n, _ in STREAM if U0[n] <= u][-1]
            return stage, u - U0[stage]

        ident, ones = prm("ident"), prm("ones")
        V0 = BANK - LH

        def wide(M):
            return PS[M % 2][:, V0:V0 + L]

        loaded = sem("loaded")
        w_ready = [sem(f"w_ready{r}") for r in range(R)]
        raw_ready = [sem(f"raw_ready{r}") for r in range(HS)]
        ps_full = sem("ps_full")
        ps_free = [sem(f"ps_free{b}") for b in range(2)]
        sq_full, sq_free = sem("sq_full"), sem("sq_free")
        sd_full = sem("sd_full")
        u_full = sem("u_full")
        h_upd = sem("h_upd")
        raw_full, conv_full = sem("raw_full"), sem("conv_full")
        stored = sem("stored")

        def steps(eng, n, per, body):
            full = n // per
            if full > 1:
                with eng.Fori(0, full) as it:
                    body(it, per)
            elif full:
                body(0, per)
            if n % per:
                body(full, n % per)

        def source_of(stage):
            downs = [n for n, _ in STREAM if n.startswith("down")]
            before = sum(n for name, n in STREAM if U0[name] < U0[stage] and (name in downs) == (stage in downs))
            return (down, before, DK * P) if stage in downs else (stream, before, SLOT)

        def used_up(u):
            if u < 0:
                return None
            stage = [n for n, _ in STREAM if U0[n] <= u][-1]
            r = u - U0[stage]
            if stage == "grp":
                return M0[stage] + r // R * GT + 2 * (r % R) + 2
            return M0[stage] + (r + 1) * TILES_PER_UNIT.get(stage, 2)

        def signal(eng, *what):
            eng.drain()
            for s in what:
                eng.sem_inc(s, 1)

        def slot_of(stage, r):
            return (N0[stage] + r) % R

        def tile_wait(eng, stage, it, per, j):
            eng.wait_ge(ps_full, it * per + M0[stage] + j + 1)

        def tile_of(stage, j):
            return PS[(M0[stage] + j) % 2]

        def free_of(stage, j):
            return ps_free[(M0[stage] + j) % 2]

        def acquire(eng, stage, it, per, j):
            assert per % 2 == 0 or isinstance(it, int) and it == 0
            eng.wait_ge(free_of(stage, j), it * (per // 2) + (M0[stage] + j) // 2 + 1)

        ssd = carve([("BCt", 8, L), ("Xs", 4, L), ("Zs", 4, L), ("Bs", L), ("Cs", L), ("yT", 16, L),
                     ("dtT", 5, 32), ("acsT", 5, 32), ("w2", 5, 32), ("dC", 5, 32), ("eacs", 5, 32),
                     ("Btok", 5, P), ("Gm", 4, P), ("Gm0", 16),
                     ("S", 4, 512),
                     ("Dm", 2, 512), ("sel", HPG, P), ("L0", HPG, 16), ("raw", CONV - 1 + L), ("cv", L),
                     ("ea", 1), ("acs", L), ("xdt", 5, 512), ("ytok", 5, 512)])
        ssd_dt = carve([("_", 8 * L), ("dtv", L), ("dtt", L), ("dt", L), ("one", L)])
        xdt, ytok = ssd["xdt"], ssd["ytok"]
        xw2 = ytok
        acs_keep = ssd["acs"][0:32, :]

        def decays(e):
            return ssd["Dm"][:, e % 4, :] if e % 4 < 2 else sq[:, e % 4 - 2, 0:512]
        sbm = carve([("kT", 8, L), ("qT", 8, L), ("v", 5, D), ("o", 5, D), ("ks", L), ("qs", L),
                     ("A", 2, 3 * BANK), ("W", 2, 3 * BANK), ("SP", 2, 3 * BANK)])
        u2 = sbm["o"].rearrange("p a b -> p (a b)")[:, 0:KD * L].rearrange("p (k l) -> p k l", k=KD)
        tails = sbm["A"].rearrange("p a b -> p (a b)")[:, 0:2 * KD * P].rearrange("p (w k m) -> p w k m", w=2, k=KD)
        ev = carve([("qf", 4, S), ("kf", 4, S), ("vf", 4, S), ("qr", 4, S), ("kr", 4, S), ("vr", 4, S),
                    ("of", 4, S), ("or", 4, S), ("decay", RETH, S), ("sel", 4, P), ("negc", S),
                    ("nm", 2, 4), ("rs", 4, 4), ("ri", 2, 4), ("mu", 32), ("var", 32),
                    ("qs", 2, S), ("ks", 2, S), ("Pm", 2, 1280), ("PT", 2, 1280)])
        gn_squares = ev["decay"].rearrange("p a b -> p (a b)")[:, 0:4 * S]
        z_even = arena[:, 0:KD * S].rearrange("p (k l) -> p k l", k=KD)
        od = carve([("A2", 2, NG, L), ("q", 8, S), ("ksd", NG, S), ("kwd", NG, S), ("vs", 4, 256), ("vw", 4, 256),
                    ("o", 4, D), ("cmp_bias", NH, P), ("gates", 48, 4),
                    ("hb", 4), ("mxc", 16), ("rsc", 16), ("cfc", 16), ("nm", 2, 4), ("rs", 4, 4), ("ri", 2, 4),
                    ("h1", 2, P), ("h1v", 2, NG, 4, CB), ("kcmp", P), ("Vbd", NG, 256), ("Pm", 2, 1280),
                    ("PT", 2, 1280)])
        odr = {}
        for n, name in enumerate(("kc", "vc", "ks", "kw")):
            at = 2 * NG * L + 8 * S + 2 * NG * S + 2 * 4 * 256 + n * 2 * S
            odr[name] = arena[:, at:at + 2 * S].rearrange("p (k l) -> p k l", k=2)
        ods = carve([("qs", 2, S), ("kss", S), ("kws", S), ("kcs", CB), ("bias", 2, S), ("X", 512), ("P2", 512),
                     ("PTc", 512)])
        z_odd = arena[:, 0:KD * S].rearrange("p (k l) -> p k l", k=KD)
        h2 = hT[:, :, META:L]
        uv = uT[:, :, 0:S]
        ffn = carve([("act", DK, L), ("acth", DK, L), ("rawg", FCONV - 1 + L), ("rawv", FCONV - 1 + L), ("cg", L), ("cvv", L)])

        NORM = {n: i for i, n in enumerate(["ssd", "ffn0", "sb", "ffn1", "final", "even", "odd", "last"])}
        H_BASE = {n: 8 * i for n, i in NORM.items()}
        U_BASE = {"ssd": 0, "ffn0": 8, "sb": 16, "sbq": 24, "ffn1": 32, "even": 40, "ev_z": 48, "odd": 56, "od_z": 64,
                  "last": 72}
        UH_BASE = {n: U_BASE[n] - 8 for n in U_BASE}
        TURNS = [(3,), (2, 0), (1,)]
        OFF = {3: 0, 2: 512, 0: 896, 1: 1024}
        DOFF = {0: 0, 1: 512, 3: 896, 2: 1024}

        def scores_at(b, a):
            w = P * (a + 1)
            return PC[:, b, 0:w] if a == 1 else PS[b][:, OFF[a]:OFF[a] + w]

        def decayed_at(b, i):
            w = S - P * i
            return PC[:, b, 0:w] if i == 2 else PS[b][:, DOFF[i]:DOFF[i] + w]

        ev_od = {"fx": ev, "ns": od}


        block = ctx.enter_context(nc.Block())

        @block.sync
        def _(sp):
            def load_stage(stage, n):
                src, src0, width = source_of(stage)
                per = TILE_STEP.get(stage, (R * TILES_PER_UNIT.get(stage, 2)))
                in_run = stage in RUN_OF
                run_start = in_run and stage == SPLIT_RUNS[RUN_OF[stage]][0] and STREAM[names.index(stage) - 1][0] in N0

                def load(it, r, first):
                    if in_run:
                        h = H0[stage] + r
                        slot, ready = raw_slot(h), raw_ready[h % HS]
                        if run_start and first and r < HS:
                            sp.wait_ge(ps_full, M0[stage])
                        else:
                            sp.wait_ge(sem("rest_full"), it * R + h - 1)
                    else:
                        n_ = N0[stage] + r
                        slot, ready = ring[:, n_ % R, :], w_ready[n_ % R]
                        before = stage_before(stage)
                        if not first:
                            sp.wait_ge(ps_full, it * per + used_up(U0[stage] + r) - per)
                        elif before in RUN_OF:
                            sp.wait_ge(ps_full, M0[stage])
                        elif n_ >= R:
                            sp.wait_ge(ps_full, used_up(U0[stage] + r - R))
                    sp.dma_start(slot[:, 0:width],
                                 src[bass.ds(it * R + src0 + r, 1), :, :].rearrange("a p n -> (a p) n")
                                 ).then_inc(ready, 16)

                for r in range(min(R, n)):
                    load(0, r, True)
                full = n // R
                if full > 1:
                    with sp.Fori(1, full) as it:
                        for r in range(R):
                            load(it, r, False)
                if full:
                    for r in range(n % R):
                        load(full, r, False)

            names = [name for name, _ in STREAM]

            def stage_before(stage):
                at = names.index(stage)
                return names[at - 1] if at else stage

            sp.dma_start(hT[:, :, :].rearrange("p k l -> p (k l)"), x_in).then_inc(loaded, 16)
            sp.dma_start(par[:, :], params_in).then_inc(loaded, 16)
            for stage, n in STREAM:
                load_stage(stage, n)
                if stage == "ev_vr":
                    at, n = TABLES["decay"]
                    sp.wait_ge(h_upd, 40)
                    sp.dma_start(ev["decay"].rearrange("p a b -> p (a b)"), tables_in[:, at:at + n]
                                 ).then_inc(sem("decay_in"), 16)
                if stage == "od_vw":
                    sp.wait_ge(sem("pad2"), 1)
                    for which, (raw, moved) in enumerate((("kc", 1), ("vc", 1), ("ks", 0), ("kw", 0))):
                        sp.wait_ge(sem("odk_full"), 2 * which + 2)
                        for gg in range(NG):
                            src = odr[raw][DH * (gg % 2):DH * (gg % 2) + DH, gg // 2, :]
                            dst = od["A2"][:, which, gg, :] if moved else od["ksd" if raw == "ks" else "kwd"][:, gg, :]
                            sp.dma_start(dst[0:DH, 0:S], src).then_inc(sem("dup"), 16)
                            sp.dma_start(dst[DH:P, 0:S - moved], src[:, moved:S]).then_inc(sem("dup"), 16)
                    at, n = TABLES["cmp_bias"]
                    sp.dma_start(od["cmp_bias"].rearrange("p a b -> p (a b)"), tables_in[:, at:at + n]
                                 ).then_inc(sem("cmp_in"), 16)
            sp.wait_ge(u_full, U_BASE["last"] + KD)
            sp.dma_start(out.rearrange("p (k l) -> p k l", k=KD), uv).then_inc(stored, 16)
            sp.wait_ge(stored, 16)


        @block.tensor
        def _(pe):
            mm = nc.tensor.matmul
            pe.wait_ge(loaded, 32)

            def norm_stats(name, width, v0):
                pc = PC[:, :, :].rearrange("p a b -> p (a b)")
                halves = [(0, LH), (LH, L)] if width == L else [(0, width)]
                for k in range(KD):
                    pe.wait_ge(sq_full, NORM[name] * KD + k + 1)
                    for a, b in halves:
                        last = mm(pc[:, v0 + a:v0 + b], ones, sq[:, k % 2, a:b], start=k == 0, stop=k == KD - 1)
                    last.then_inc(sq_free, 1)

            def three(out_, a, ah, b, bh, start, stop):
                mm(out_, r32(ah), r32(bh), start=start, stop=False)
                mm(out_, r32(ah), r32(b), start=False, stop=False)
                return mm(out_, r32(a), r32(bh), start=False, stop=stop)

            def project(stage, it, per, j, r, k_n, mcol, moving, high=None, ready=None):
                tile = tile_of(stage, j)
                width = moving.shape[2]
                v0 = V0 if width == L else 0
                cut = lambda w: w[:, 0:k_n * (DK * P if k_n == DK else SLOT) // k_n].rearrange("p (k m) -> p k m", k=k_n)
                w = cut(rest_slot(H0[stage] + r) if high is not None else ring[:, slot_of(stage, r), :])
                for k in range(k_n):
                    if ready and j == 0:
                        pe.wait_ge(ready[0], ready[1] + k + 1)
                    for a, b in ([(0, LH), (LH, L)] if width == L else [(0, width)]):
                        out_, first, last_ = tile[:, v0 + a:v0 + b], k == 0, k == k_n - 1
                        if high is None:
                            last = mm(out_, w[:, k, mcol:mcol + P], moving[:, k, a:b], start=first, stop=last_)
                        else:
                            wh = cut(high_slot(H0[stage] + r))
                            last = three(out_, w[:, k, mcol:mcol + P], wh[:, k, mcol:mcol + P], moving[:, k, a:b],
                                         high[:, k, a:b], first, last_)
                return last

            def unit_ready(stage, it, r):
                if stage in RUN_OF:
                    pe.wait_ge(sem("rest_full"), it * R + H0[stage] + r + 1)
                else:
                    pe.wait_ge(w_ready[slot_of(stage, r)], 16 * it + 16 * ((N0[stage] + r) // R + 1))

            def project_units(stage, n_units, moving, high=None, ready=None):
                def body(it, count):
                    for r in range(count):
                        unit_ready(stage, it, r)
                        for m in range(2):
                            acquire(pe, stage, it, 2 * R, 2 * r + m)
                            last = project(stage, it, 2 * R, 2 * r + m, r, KD, m * P, moving, high, ready)
                            last.then_inc(ps_full, 1)
                steps(pe, n_units, R, body)

            norm_stats("ssd", L, V0)
            pe.wait_ge(u_full, 8)
            acquire(pe, "dt", 0, 2, 0)
            w_dt = prm("w_dt").rearrange("p (k m) -> p k m", k=KD)
            for a, b in [(0, LH), (LH, L)]:
                for k in range(KD):
                    last = mm(tile_of("dt", 0)[0:32, V0 + a:V0 + b], w_dt[:, k, :], uT[:, k, a:b],
                              start=k == 0, stop=k == KD - 1)
            last.then_inc(ps_full, 1)
            project_units("bc", 4, uT)
            pe.wait_ge(sem("acs_full"), 1)
            acquire(pe, "dtt", 0, 2, 0)
            t = tile_of("dtt", 0)
            for c, (at, n) in enumerate(CHUNKS):
                nc.tensor.transpose(t[0:n, 32 * c:32 * c + 32], ssd_dt["dt"][0:32, at:at + n], ident[0:32, 0:32])
                last = nc.tensor.transpose(t[0:n, BANK + 32 * c:BANK + 32 * c + 32], acs_keep[0:32, at:at + n],
                                           ident[0:32, 0:32])
            last.then_inc(ps_full, 1)
            pe.wait_ge(sem("acsT_full"), 1)
            acquire(pe, "end", 0, 2, 0)
            t = tile_of("end", 0)
            mm(t[:, 0:32], prm("pick15", META), ssd["acsT"][0:META, 0, :], start=True, stop=True)
            mm(t[:, 32:160], prm("pick127"), ssd["acsT"][:, 1:5, :].rearrange("p a b -> p (a b)"),
               start=True, stop=True).then_inc(ps_full, 1)

            Xs, Bs, Cs, Btok, S_ = ssd["Xs"], ssd["Bs"], ssd["Cs"], ssd["Btok"], ssd["S"]
            with pe.Fori(0, GROUPS) as g:
                for r in range(4):
                    unit_ready("grp", g, r)
                    for m in range(2):
                        acquire(pe, "grp", g, GT, 2 * r + m)
                        last = project("grp", g, GT, 2 * r + m, r, KD, m * P, uT)
                        last.then_inc(ps_full, 1)
                pe.wait_ge(sem("bc_staged"), g + 1)
                acquire(pe, "grp", g, GT, 8)
                t = tile_of("grp", 8)
                nc.tensor.transpose(t[0:META, BANK:BANK + P], Bs[:, 0:META], ident)
                for c in range(1, 5):
                    at, n = CHUNKS[c]
                    last = nc.tensor.transpose(t[:, (c - 1) * P:c * P], Bs[:, at:at + n], ident)
                last.then_inc(ps_full, 1)
                acquire(pe, "grp", g, GT, 9)
                t = tile_of("grp", 9)
                mm(t[0:META, BANK:BANK + META], Bs[:, 0:META], Cs[:, 0:META], start=True, stop=True)
                for c in range(1, 5):
                    at, n = CHUNKS[c]
                    last = mm(t[:, (c - 1) * P:c * P], Bs[:, at:at + n], Cs[:, at:at + n], start=True, stop=True)
                last.then_inc(ps_full, 1)
                acquire(pe, "grp", g, GT, 10)
                t = tile_of("grp", 10)
                for e in range(HPG):
                    last = mm(t[:, e * META:(e + 1) * META], ssd["sel"][0:32, e, :], acs_keep[:, 0:META],
                              start=True, stop=True)
                last.then_inc(ps_full, 1)
                pe.wait_ge(sem("x_full"), 4 * g + 4)
                for j, cs in ((11, [0]), (12, [1, 2]), (13, [3, 4])):
                    acquire(pe, "grp", g, GT, j)
                    for i, c in enumerate(cs):
                        at, n = CHUNKS[c]
                        for q in range(4):
                            last = nc.tensor.transpose(tile_of("grp", j)[0:n, i * BANK + q * P:i * BANK + (q + 1) * P],
                                                       Xs[:, q, at:at + n], ident)
                    last.then_inc(ps_full, 1)
                pe.wait_ge(sem("btok_full"), g + 1)
                for c in range(4):
                    n = CHUNKS[c][1]
                    pe.wait_ge(sem("xw_full"), 5 * g + c + 1)
                    acquire(pe, "grp", g, GT, 14 + c)
                    mm(tile_of("grp", 14 + c)[:, 0:BANK], Btok[0:n, c, :], xw2[0:n, c, :],
                       start=True, stop=True).then_inc(ps_full, 1)
                for j in range(2):
                    acquire(pe, "grp", g, GT, 18 + j)
                    for i in range(2):
                        c = 1 + 2 * j + i
                        pe.wait_ge(sem("state_full"), 4 * g + c)
                        last = mm(tile_of("grp", 18 + j)[:, i * BANK:(i + 1) * BANK],
                                  Cs[:, CHUNKS[c][0]:CHUNKS[c][0] + P], S_[:, c - 1, :], start=True, stop=True)
                    last.then_inc(ps_full, 1)

                def spread(e):
                    if e >= 2:
                        pe.wait_ge(sem("dm_full"), HPG * g + e - 1)
                    mm(PC[:, e % 2, :], ssd["sel"][0:32, e, :], acs_keep[:, META:L], start=True, stop=True
                       ).then_inc(sem("pc_full"), 1)

                spread(0)
                spread(1)
                for e in range(HPG):
                    if e + 2 < HPG:
                        spread(e + 2)
                    pe.wait_ge(sem("mt_full"), HPG * g + e + 1)
                    pe.wait_ge(sem("pd_free"), HPG * g + e + 1)
                    if e == HPG - 1:
                        acquire(pe, "grp", g, GT, 20)
                        pe.wait_ge(sem("m0_full"), g + 1)
                    for c in range(4):
                        last = mm(PD[:, e % 2, c * DH:(c + 1) * DH], decays(e)[:, c * P:(c + 1) * P],
                                  xdt[:, c + 1, e * DH:(e + 1) * DH], start=True, stop=True)
                    last.then_inc(sem("pd_full"), 1)
                for e in range(HPG):
                    last = mm(tile_of("grp", 20)[0:META, e * DH:(e + 1) * DH], ssd["L0"][0:META, e, :],
                              xdt[0:META, 0, e * DH:(e + 1) * DH], start=True, stop=True)
                last.then_inc(ps_full, 1)
                pe.wait_ge(sem("ytok_full"), g + 1)
                for q in range(4):
                    acquire(pe, "grp", g, GT, 21 + q)
                    t = tile_of("grp", 21 + q)
                    for c in range(1, 5):
                        nc.tensor.transpose(t[:, BANK + (c - 1) * P:BANK + c * P],
                                            ytok[:, c, q * P:(q + 1) * P], ident)
                    last = nc.tensor.transpose(t[:, BANK - META:BANK], ytok[0:META, 0, q * P:(q + 1) * P],
                                               ident[0:META, 0:META])
                    last.then_inc(ps_full, 1)
                acquire(pe, "grp", g, GT, 25)
                for q in range(4):
                    pe.wait_ge(sem("gsq_full"), 4 * g + q + 1)
                    for a, b in [(0, LH), (LH, L)]:
                        last = mm(tile_of("grp", 25)[:, V0 + a:V0 + b], ones, sq[:, q % 2, a:b],
                                  start=q == 0, stop=q == 3)
                    last.then_inc(sem("gsq_free") if q < 3 else ps_full, 1)

            pe.wait_ge(sem("yT_full"), 4 * GROUPS)

            def sout(it, count):
                for r in range(count):
                    unit_ready("sout", it, r)
                    acquire(pe, "sout", it, R, r)
                    project("sout", it, R, r, r, 16, 0, ssd["yT"]).then_inc(ps_full, 1)
            steps(pe, 8, R, sout)

            def ffn_pe(i):
                norm_stats(f"ffn{i}", L, V0)
                for half, part in enumerate("ab"):
                    project_units(f"ffn{i}{part}", DK, uT, uh, (u_full, U_BASE[f"ffn{i}"]) if half == 0 else None)
                    stage = f"down{i}{part}"
                    acts_ready = (sem("act_full"), DK * (2 * i + half))

                    def body(it, count):
                        for r in range(count):
                            unit_ready(stage, it, r)
                            acquire(pe, stage, it, R, r)
                            project(stage, it, R, r, r, DK, 0, ffn["act"], ffn["acth"], acts_ready).then_inc(ps_full, 1)
                    steps(pe, 8, R, body)

            ffn_pe(0)

            def tokens_major(stage, n_units, moving, high, tokens):
                for r in range(n_units):
                    unit_ready(stage, 0, r)
                    w = rest_slot(H0[stage] + r).rearrange("p (k m) -> p k m", k=KD)
                    for t, at in enumerate(range(0, tokens, P)):
                        n = min(P, tokens - at)
                        j = r * -(-tokens // P) + t
                        acquire(pe, stage, 0, 2, j)
                        wh = high_slot(H0[stage] + r).rearrange("p (k m) -> p k m", k=KD)

                        for k in range(KD):
                            u_, uh_ = ((x[:, k, at:at + P] for x in (moving, high)) if n == P else
                                       (tails[:, which, k, :] for which in range(2)))
                            last = three(tile_of(stage, j)[:, 0:256], u_, uh_, w[:, k, :], wh[:, k, :],
                                         k == 0, k == KD - 1)
                        last.then_inc(ps_full, 1)

            norm_stats("sb", L, V0)
            project_units("sbk", 4, uT, uh, (u_full, U_BASE["sb"]))
            pe.wait_ge(sem("tails_full"), 1)
            tokens_major("sbv", 4, uT, uh, L)
            project_units("sbq", 4, u2, uh, (u_full, U_BASE["sbq"]))
            pe.wait_ge(sem("qkv_full"), 3)
            neg_tri, neg_ones = prm("neg_tri"), prm("neg_ones")

            def zseg(e, seg):
                return PS[e][:, seg * BANK:(seg + 1) * BANK] if seg < 2 else PC[:, e, :]

            def hide(e, seg, at, n):
                return mm(zseg(e, seg)[0:n, at:at + n], ident_b[0:n, 0:n], hidden_b[0:n, 0:n], start=False, stop=True,
                          skip_group_check=True)

            def sb_scores(j, ahead, e):
                pe.wait_ge(sem("staged"), j + ahead + 1)
                ks, qs = sbm["ks"][DH * e:DH * e + DH], sbm["qs"][DH * e:DH * e + DH]
                pe.wait_ge(sem("w_exp"), 6 * j + 6 * ahead + 3 * e + 3)
                mm(zseg(e, 0), ks[:, 0:P], qs[:, 0:S], start=True, stop=True)
                hide(e, 0, 0, P).then_inc(sem("z_full"), 1)
                mm(zseg(e, 1)[:, 0:384], ks[:, P:2 * P], qs[:, P:S], start=True, stop=True)
                mm(zseg(e, 1)[:, 384:512], ks[:, 3 * P:S], qs[:, 3 * P:S], start=False, stop=True,
                   skip_group_check=True)
                hide(e, 1, 0, P)
                hide(e, 1, 384, P).then_inc(sem("z_full"), 1)
                mm(zseg(e, 2)[:, 0:256], ks[:, 2 * P:3 * P], qs[:, 2 * P:S], start=True, stop=True)
                for i in range(5):
                    n = P if i < 4 else META
                    mm(zseg(e, 2)[0:n, 256 + 16 * i:272 + 16 * i], ks[:, P * i:P * i + n], qs[:, S:L],
                       start=False, stop=True, skip_group_check=True)
                hide(e, 2, 0, P)
                hide(e, 2, 320, META).then_inc(sem("z_full"), 1)

            def sb_sums(j, e):
                sp_ = sbm["SP"][:, e, :]

                def add(seg, a, b, w, rhs):
                    out_ = zseg(e, seg)[0:w.shape[1], a:b]
                    if len(rhs.shape) == 3:
                        out_ = out_.rearrange("p (r c) -> p r c", r=rhs.shape[1])
                    return mm(out_, w, rhs, start=False, stop=True, skip_group_check=True)

                pe.wait_ge(sem("sp_full2"), 6 * j + 3 * e + 3)
                add(0, 0, 512, neg_tri, sp_[:, 0:512])
                add(0, 128, 512, neg_ones, sp_[:, 512:896])
                add(0, 256, 512, neg_ones, sp_[:, 1024:1280])
                add(0, 384, 512, neg_ones, sp_[:, 896:1024]).then_inc(sem("c_full"), 1)
                add(1, 0, 384, neg_tri, sp_[:, 512:896])
                add(1, 384, 512, neg_tri, sp_[:, 896:1024])
                add(1, 128, 384, neg_ones, sp_[:, 1024:1280])
                add(1, 256, 384, neg_ones, sp_[:, 896:1024]).then_inc(sem("c_full"), 1)
                add(2, 0, 256, neg_tri, sp_[:, 1024:1280])
                add(2, 128, 256, neg_ones, sp_[:, 896:1024])
                add(2, 256, 320, neg_tri, sp_[:, 1280:1344])
                add(2, 320, 336, neg_tri[0:META, 0:META], sp_[0:META, 1344:1360])
                for i in range(1, 5):
                    n = P if i < 4 else META
                    rhs = sp_[0:n, 1280 + 16 * i:1296 + 16 * i]
                    if i > 1:
                        rhs = rhs.unsqueeze(1).to_broadcast([n, i, META])
                    last = add(2, 256, 256 + 16 * i, neg_ones[0:n, :], rhs)
                last.then_inc(sem("c_full"), 1)

            def sb_outputs(j, e):
                pe.wait_ge(sem("o_free"), 2 * j + e + 1)
                pe.wait_ge(sem("w_exp"), 6 * j + 3 * e + 9)
                W_ = sbm["W"][:, e, :]
                col = [0, 512, 1024, 896]
                first = [0, 1, 2, 3]
                v = lambda i: sbm["v"][:, i, bass.ds((2 * j + e) * DH, DH)]
                for a in range(4):
                    for i in range(a + 1):
                        c = col[i] + P * (a - first[i])
                        mm(PD[:, e, a * DH:(a + 1) * DH], W_[:, c:c + P], v(i), start=i == 0, stop=i == a)
                for i in range(5):
                    last = mm(PD[0:META, e, 256:320], W_[:, 1280 + 16 * i:1296 + 16 * i], v(i),
                              start=i == 0, stop=i == 4)
                last.then_inc(sem("o_full"), 1)

            def sb_pair(j, last):
                for e in range(2):
                    sb_sums(j, e)
                for e in range(2):
                    if not last:
                        sb_scores(j, 1, e)
                    sb_outputs(j, e)

            for e in range(2):
                sb_scores(0, 0, e)
            with pe.Fori(0, SBH // 2 - 1) as j:
                sb_pair(j, False)
            sb_pair(SBH // 2 - 1, True)
            pe.wait_ge(sem("o_free"), SBH + 2)
            for k in range(8):
                acquire(pe, "oT", 0, 2, k)
                t = tile_of("oT", k)
                for a in range(4):
                    nc.tensor.transpose(t[:, a * P:(a + 1) * P], sbm["o"][:, a, k * P:(k + 1) * P], ident)
                nc.tensor.transpose(t[:, S:L], sbm["o"][0:META, 4, k * P:(k + 1) * P], ident[0:META, 0:META]
                                    ).then_inc(ps_full, 1)
            project_units("wo", 4, uT, uh, (sem("oT_full"), 0))
            ffn_pe(1)

            def ret_out(it, h):
                pe.wait_ge(sem("ret_m"), it * 4 + h + 3)
                pe.wait_ge(sem("ret_free"), it * 4 + h + 1)
                v = lambda i: ev["vr"][:, i, bass.ds((it * 4 + h) * DH, DH)]
                for a in range(4):
                    for i in range(a + 1):
                        c = DOFF[i] + P * (a - i)
                        last = mm(PD[:, h % 2, a * DH:(a + 1) * DH], ev["Pm"][:, h % 2, c:c + P], v(i),
                                  start=i == 0, stop=i == a)
                last.then_inc(sem("ret_o"), 1)

            def outputs_T(stage, of):
                for k in range(8):
                    acquire(pe, stage, 0, 2, k)
                    for a in range(4):
                        last = nc.tensor.transpose(tile_of(stage, k)[:, a * P:(a + 1) * P], of(k, a), ident)
                    last.then_inc(ps_full, 1)

            norm_stats("final", S, 0)
            norm_stats("even", S, 0)
            acquire(pe, "ev_f", 0, 2, 0)
            w_f = prm("w_f").rearrange("p (k m) -> p k m", k=KD)
            for k in range(KD):
                pe.wait_ge(u_full, U_BASE["even"] + k + 1)
                mm(tile_of("ev_f", 0)[0:FOXH, 0:S], w_f[:, k, :], split(uhs[:, k, :]), start=k == 0, stop=False)
                last = mm(tile_of("ev_f", 0)[0:FOXH, 0:S], w_f[:, k, :], split(uv[:, k, :]), start=False, stop=k == KD - 1)
            last.then_inc(ps_full, 1)
            for x in "fr":
                project_units(f"ev_q{x}", 2, uv, uhs)
                project_units(f"ev_k{x}", 2, uv, uhs)
                tokens_major(f"ev_v{x}", 2, uv, uhs, S)

            def rows_pe(name, per_it, it, scores, value):
                for s in range(per_it + 2):
                    if s < per_it:
                        pe.wait_ge(sem(name + "_nm"), it * per_it + s + 1)
                        scores(s)
                    if 1 <= s <= per_it:
                        n = s - 1
                        N = it * per_it + n
                        for i, tiles in enumerate(TURNS):
                            pe.wait_ge(sem(name + "_p"), N * 3 + i + 1)
                            if i == 0:
                                pe.wait_ge(sem(name + "_ptd"), N + 1)
                            elif i == 1:
                                pe.wait_ge(sem(name + "_pta"), N * 2 + 1)
                            for a in tiles:
                                for b in range(a + 1):
                                    last = nc.tensor.transpose(
                                        scores_at(1, a)[:, b * P:(b + 1) * P],
                                        ev_od[name]["Pm"][:, n % 2, OFF[a] + b * P:OFF[a] + (b + 1) * P], ident)
                            last.then_inc(sem(name + "_tr"), 1)
                    if s >= 2:
                        n = s - 2
                        N = it * per_it + n
                        pe.wait_ge(sem(name + "_ptd"), N + 2)
                        pe.wait_ge(sem(name + "_pta"), N * 2 + 3)
                        pe.wait_ge(sem(name + "_comb"), N + 1)
                        for a in range(4):
                            for b in range(a + 1):
                                last = mm(PD[:, n % 2, a * DH:(a + 1) * DH],
                                          ev_od[name]["PT"][:, n % 2, OFF[a] + b * P:OFF[a] + (b + 1) * P],
                                          value(n, b), start=b == 0, stop=b == a)
                        last.then_inc(sem(name + "_o"), 1)

            pe.wait_ge(sem("ev_full"), 6)
            pe.wait_ge(sem("negc_full"), 1)
            with pe.Fori(0, 2) as it:
                pe.wait_ge(sem("fstaged"), it + 1)

                def fox_scores(h):
                    rows = slice(DH * (h % 2), DH * (h % 2) + DH)
                    for tiles in TURNS:
                        for a in tiles:
                            w = P * (a + 1)
                            mm(scores_at(0, a), ev["qs"][rows, h // 2, a * P:w], ev["ks"][rows, h // 2, 0:w],
                               start=True, stop=False)
                            last = mm(scores_at(0, a), ev["sel"][0:FOXH, h, :], ev["negc"][0:FOXH, 0:w],
                                      start=False, stop=True)
                        last.then_inc(sem("fx_s"), 1)

                rows_pe("fx", 4, it, fox_scores, lambda h, b: ev["vf"][:, b, bass.ds((it * 4 + h) * DH, DH)])
            with pe.Fori(0, 2) as it:
                pe.wait_ge(sem("fstaged"), it + 3)
                for h in range(4):
                    rows = slice(DH * (h % 2), DH * (h % 2) + DH)
                    pe.wait_ge(sem("ret_m"), it * 4 + h + 1)
                    for i in (0, 1, 3, 2):
                        last = mm(decayed_at(h % 2, i), ev["ks"][rows, h // 2, i * P:(i + 1) * P],
                                  ev["qs"][rows, h // 2, i * P:S], start=True, stop=True)
                    last.then_inc(sem("ret_s"), 1)
                    if h:
                        ret_out(it, h - 1)
                ret_out(it, 3)
            project_units("ev_z", 4, uv, uhs, (u_full, U_BASE["ev_z"]))
            pe.wait_ge(sem("mix_full"), 1)
            outputs_T("ev_y", lambda k, a: (ev["of"] if k < 4 else ev["or"])[:, a, (k % 4) * P:(k % 4 + 1) * P])
            project_units("eout", 4, uv, uhs, (sem("y_full"), 0))
            norm_stats("odd", S, 0)
            acquire(pe, "od_g", 0, 2, 0)
            w_g = prm("w_gate").rearrange("p (k m) -> p k m", k=KD)
            for a in range(4):
                for k in range(KD):
                    if a == 0:
                        pe.wait_ge(u_full, U_BASE["odd"] + k + 1)
                    for n, u_ in enumerate((uhs, uv)):
                        last = mm(tile_of("od_g", 0)[:, a * 48:(a + 1) * 48], split(u_[:, k, a * P:(a + 1) * P]), w_g[:, k, :],
                                  start=k == 0 and n == 0, stop=k == KD - 1 and n == 1)
            last.then_inc(ps_full, 1)
            project_units("od_q", 4, uv, uhs)
            for x in ("kc", "vc", "ks", "kw"):
                project_units(f"od_{x}", 1, uv, uhs)
            tokens_major("od_vs", 1, uv, uhs, S)
            tokens_major("od_vw", 1, uv, uhs, S)
            for which, (stage, pe_) in enumerate((("ck", "pe_k"), ("cv", "pe_v"))):
                pe.wait_ge(sem("dup"), 16 * 2 * NG * 4)
                for hid in range(2):
                    unit_ready(stage, 0, hid)
                    acquire(pe, stage, 0, 2, hid)
                    t = tile_of(stage, hid)
                    w = ring[:, slot_of(stage, hid), :].rearrange("p (k m) -> p k m", k=16)
                    for l2 in range(16):
                        mm(t[:, 0:P].rearrange("p (g c) -> p g c", g=NG), w[:, l2, :],
                           od["A2"][:, which, :, 2 * l2:2 * l2 + 16 * (CB - 1) + 1:16], start=l2 == 0, stop=l2 == 15)
                    for l2 in range(16):
                        last = mm(t[:, BANK:BANK + 1], w[:, l2, :], prm(pe_)[:, l2:l2 + 1], start=l2 == 0, stop=l2 == 15)
                    last.then_inc(ps_full, 1)
                pe.wait_ge(sem("h1_full"), 2 * which + 2)
                acquire(pe, stage + "2", 0, 2, 0)
                t = tile_of(stage + "2", 0)
                if which == 0:
                    for hid in range(2):
                        last = mm(t[:, 0:P], prm("wk2").rearrange("p (a m) -> p a m", a=2)[:, hid, :], od["h1"][:, hid, :],
                                  start=hid == 0, stop=hid == 1)
                else:
                    for g in range(NG):
                        for hid in range(2):
                            last = mm(t[:, g * DH:(g + 1) * DH], od["h1v"][:, hid, g, :, :].rearrange("p a b -> p (a b)"),
                                      prm("wv2").rearrange("p (a m) -> p a m", a=2)[:, hid, :], start=hid == 0, stop=hid == 1)
                last.then_inc(ps_full, 1)
            pe.wait_ge(sem("od_full"), 5)
            with pe.Fori(0, NG) as g:
                pe.wait_ge(sem("gstaged"), g + 1)
                for i in range(4):
                    rows = slice(DH * (i % 2), DH * (i % 2) + DH)
                    for a in range(4):
                        c = i % 2 * BANK + (4 * (i // 2) + a) * CB
                        last = mm(PS[0][:, c:c + CB], ods["qs"][rows, i // 2, a * P:(a + 1) * P],
                                  ods["kcs"][rows, :], start=True, stop=True)
                last.then_inc(sem("cs_full"), 1)
                pe.wait_ge(sem("cp_full"), g + 1)
                for a in range(4):
                    last = nc.tensor.transpose(PS[1][:, a * P:(a + 1) * P], ods["P2"][:, a * P:(a + 1) * P], ident)
                last.then_inc(sem("ct_full"), 1)
                pe.wait_ge(sem("cpt_full"), g + 1)
                for a in range(4):
                    last = mm(PS[0][:, a * 256:(a + 1) * 256], ods["PTc"][:, a * P:(a + 1) * P],
                              od["Vbd"][:, bass.ds(g, 1), :].rearrange("p a b -> p (a b)"), start=True, stop=True)
                last.then_inc(sem("co_full"), 1)
                pe.wait_ge(sem("cc_full"), g + 1)

                def nsa_scores(n):
                    i = n // 2
                    rows = slice(DH * (i % 2), DH * (i % 2) + DH)
                    k_ = ods["kss" if n % 2 == 0 else "kws"]
                    for tiles in TURNS:
                        for a in tiles:
                            last = mm(scores_at(0, a), ods["qs"][rows, i // 2, a * P:(a + 1) * P], k_[rows, 0:P * (a + 1)],
                                      start=True, stop=True)
                        last.then_inc(sem("ns_s"), 1)

                rows_pe("ns", 8, g, nsa_scores,
                        lambda n, b: od["vs" if n % 2 == 0 else "vw"][:, b, bass.ds(g * DH, DH)])
            pe.wait_ge(sem("nsa_full"), 1)
            project_units("od_z", 4, uv, uhs, (u_full, U_BASE["od_z"]))
            outputs_T("od_y", lambda k, a: od["o"][:, a, k * P:(k + 1) * P])
            project_units("oout", 4, uv, uhs, (sem("y_full"), 8))
            norm_stats("last", S, 0)

        @block.scalar
        def _(act):
            A = nc.scalar.activation
            act.wait_ge(loaded, 32)

            def squares(name, h, width):
                for k in range(KD):
                    if name in H_BASE and H_BASE[name]:
                        act.wait_ge(h_upd, H_BASE[name] - 8 + k + 1)
                    n = NORM[name] * KD + k
                    if n >= 2:
                        act.wait_ge(sq_free, n - 1)
                    A(sq[:, k % 2, 0:width], h[:, k, 0:width], ACT.Square).then_inc(sq_full, 1)

            def deviation(name, width, v0):
                pc = PC[:, :, :].rearrange("p a b -> p (a b)")
                act.wait_ge(sq_free, (NORM[name] + 1) * KD)
                A(sd[:, 0:width], pc[:, v0:v0 + width], ACT.Sqrt, bias=prm("eps"), scale=1.0 / D
                  ).then_inc(sd_full, 1)

            def high_part(stage, it, r):
                u = U0[stage] + r
                real, n = stage_at(u)
                if u >= N_UNITS or RUN_OF.get(real) != RUN_OF[stage]:
                    return
                width = width_of(real)
                h = H0[stage] + r
                act.wait_ge(raw_ready[h % HS], it * (R // HS) * 16 + 16 * (h // HS + 1))
                A(r32(high_slot(h)[:, 0:width]), raw_slot(h)[:, 0:width], ACT.Copy).then_inc(sem("high_full"), 1)

            def high_first(stage):
                for r in range(HS):
                    high_part(stage, 0, r)

            def high_next(stage, it, r):
                high_part(stage, it, r + HS)

            def high_input(name, width):
                for k in range(KD):
                    act.wait_ge(sem("u_raw"), UH_BASE[name] + k + 1)
                    A(r32(uh[:, k, 0:width]), sq[:, k % 2, 0:width], ACT.Copy).then_inc(sem("uh_full"), 1)

            def watch(stage, n_tiles, per_unit):
                for r in range(n_tiles // per_unit):
                    tile_wait(act, stage, 0, n_tiles, (r + 1) * per_unit - 1)
                    high_next(stage, 0, r)

            squares("ssd", hT, L)
            deviation("ssd", L, V0)
            act.wait_ge(sem("dtv_full"), 1)
            dtt = ssd_dt["dtt"][0:32, :]
            A(dtt, ssd_dt["dtv"][0:32, :], ACT.Abs)
            act.drain()
            A(dtt, dtt, ACT.Exp, scale=-1.0)
            act.drain()
            A(dtt, dtt, ACT.Ln, bias=1.0)
            A(ssd["ea"][0:32, :], prm("a_log", 32), ACT.Exp)
            signal(act, sem("sp_full"))

            def conv_tile(stage, it, per, j, n, dst, wait_dst=None):
                tile_wait(act, stage, it, per, j)
                A(ssd["raw"][:, CONV - 1:], tile_of(stage, j)[:, V0:V0 + L], ACT.Copy)
                signal(act, raw_full, free_of(stage, j))
                act.wait_ge(conv_full, n + 1)
                return A(dst, ssd["cv"], ACT.Silu)

            act.wait_ge(sem("raw_pad"), 1)
            for j in range(8):
                last = conv_tile("bc", 0, 8, j, j, ssd["BCt"][:, j, :])
                last.then_inc(sem("bc_full"), 1)
            act.wait_ge(sem("wdiff_full"), 1)
            A(ssd["w2"][0:META, 0, :], ssd["w2"][0:META, 0, :], ACT.Exp)
            A(ssd["w2"][:, 1:5, :], ssd["w2"][:, 1:5, :], ACT.Exp).then_inc(sem("w2_exp"), 1)
            A(ssd["dC"][:, :, :], tile_of("end", 0)[:, 0:160].rearrange("p (a b) -> p a b", a=5), ACT.Exp
              ).then_inc(free_of("end", 0), 1)
            A(ssd["eacs"][:, 1:5, :], ssd["acsT"][:, 1:5, :], ACT.Exp).then_inc(sem("dc_full"), 1)

            with act.Fori(0, GROUPS) as g:
                act.wait_ge(sem("grp_done"), g + 1)
                for q in range(4):
                    conv_tile("grp", g, GT, q, g * 4 + 8 + q, ssd["Xs"][:, q, :]).then_inc(sem("x_full"), 1)
                for q in range(4):
                    tile_wait(act, "grp", g, GT, 4 + q)
                    A(ssd["Zs"][:, q, :], tile_of("grp", 4 + q)[:, V0:V0 + L], ACT.Silu).then_inc(free_of("grp", 4 + q), 1)
                tile_wait(act, "grp", g, GT, 8)
                t = tile_of("grp", 8)
                A(ssd["Btok"][0:META, 0, :], t[0:META, BANK:BANK + P], ACT.Copy)
                A(ssd["Btok"][:, 1:5, :].rearrange("p a b -> p (a b)"), t[:, 0:BANK], ACT.Copy)
                signal(act, sem("btok_full"), free_of("grp", 8))
                act.wait_ge(sem("l0_full"), g + 1)
                A(ssd["L0"][0:META, :, :], ssd["L0"][0:META, :, :], ACT.Exp).then_inc(sem("l0_exp"), 1)
                for e in range(HPG):
                    act.wait_ge(sem("dm_full"), HPG * g + e + 1)
                    A(decays(e), decays(e), ACT.Exp).then_inc(sem("dm_exp"), 1)
                for q in range(4):
                    act.wait_ge(sem("y2_full"), 4 * g + q + 1)
                    if q >= 2:
                        act.wait_ge(sem("gsq_free"), 3 * g + q - 1)
                    A(sq[:, q % 2, :], ssd["yT"][:, bass.ds(4 * g + q, 1), :].rearrange("p a l -> p (a l)"), ACT.Square
                      ).then_inc(sem("gsq_full"), 1)
                tile_wait(act, "grp", g, GT, 25)
                A(sd[:, :], tile_of("grp", 25)[:, V0:V0 + L], ACT.Sqrt, bias=prm("eps"), scale=1.0 / 512)
                signal(act, sem("gsd_full"), free_of("grp", 25))

            def ffn_act(i):
                squares(f"ffn{i}", hT, L)
                deviation(f"ffn{i}", L, V0)
                high_input(f"ffn{i}", L)
                act.wait_ge(sem("fpad"), i + 1)
                for half, part in enumerate("ab"):
                    stage = f"ffn{i}{part}"
                    n0 = DK * (2 * i + half)

                    def body(it, count):
                        for r in range(count):
                            for m, raw in ((0, "rawg"), (1, "rawv")):
                                tile_wait(act, stage, it, 2 * R, 2 * r + m)
                                A(ffn[raw][:, FCONV - 1:], tile_of(stage, 2 * r + m)[:, V0:V0 + L], ACT.Copy)
                                signal(act, raw_full, free_of(stage, 2 * r + m))
                            high_next(stage, it, r)
                            act.wait_ge(conv_full, it * 2 * R + 24 + 2 * n0 + 2 * r + 2)
                            A(ffn["cg"], ffn["cg"], ACT.Silu).then_inc(sem("glu"), 1)
                    steps(act, DK, R, body)
                    watch(f"down{i}{part}", 8, 1)

            act.wait_ge(sem("yT_full"), 4 * GROUPS)
            high_first("ffn0a")
            ffn_act(0)

            def evacuate(stage, n, per, dst, width, func=ACT.Copy, scale=1.0, done=None):
                def body(it, count):
                    for j in range(count):
                        tile_wait(act, stage, it, per, j)
                        v0 = V0 if width == L else 0
                        A(dst[:, bass.ds(it * per + j, 1), 0:width].rearrange("p a l -> p (a l)"),
                          tile_of(stage, j)[:, v0:v0 + width], func, scale=scale).then_inc(free_of(stage, j), 1)
                        if j % 2:
                            high_next(stage, it, j // 2)
                steps(act, n, per, body)
                if done:
                    signal(act, sem(done))

            def evacuate_v(stage, n_units, tokens, dst, done):
                tt = -(-tokens // P)
                for r in range(n_units):
                    for t in range(tt):
                        n = min(P, tokens - t * P)
                        tile_wait(act, stage, 0, 2, r * tt + t)
                        A(dst[0:n, t, 256 * r:256 * (r + 1)], tile_of(stage, r * tt + t)[0:n, 0:256], ACT.Copy
                          ).then_inc(free_of(stage, r * tt + t), 1)
                    high_next(stage, 0, r)
                signal(act, sem(done))

            squares("sb", hT, L)
            deviation("sb", L, V0)
            high_input("sb", L)
            evacuate("sbk", 8, 8, sbm["kT"], L, done="qkv_full")
            act.wait_ge(sem("v_zero"), 1)
            evacuate_v("sbv", 4, L, sbm["v"], "qkv_full")
            high_input("sbq", L)
            evacuate("sbq", 8, 8, sbm["qT"], L, scale=DH ** -0.5, done="qkv_full")
            act.sem_inc(sem("w_exp"), 6)
            act.wait_ge(sem("w_zero"), 1)
            SEGS = [(0, 512), (512, 1024), (1024, 1344)]
            zs = lambda e, seg: PS[e][:, seg * BANK:(seg + 1) * BANK] if seg < 2 else PC[:, e, :]

            def sb_softplus(j, ahead):
                for e in range(2):
                    A_ = sbm["A"][:, e, :]
                    for i, (a, b) in enumerate(SEGS):
                        act.wait_ge(sem("z_full"), 6 * j + 6 * ahead + 3 * e + i + 2)
                        A(A_[:, a:b], zs(e, i)[:, 0:b - a], ACT.Abs)
                    A(A_[0:META, 1344:1360], PC[0:META, e, 320:336], ACT.Abs)
                    act.drain()
                    for a, b in SEGS:
                        A(A_[:, a:b], A_[:, a:b], ACT.Exp, scale=-1.0)
                    A(A_[0:META, 1344:1360], A_[0:META, 1344:1360], ACT.Exp, scale=-1.0)
                    act.drain()
                    A(A_[0:META, 1344:1360], A_[0:META, 1344:1360], ACT.Ln, bias=1.0)
                    for i, (a, b) in enumerate(SEGS):
                        A(A_[:, a:b], A_[:, a:b], ACT.Ln, bias=1.0).then_inc(sem("l_full"), 1)

            def sb_weights(j):
                for e in range(2):
                    W_ = sbm["W"][:, e, :]
                    for i, (a, b) in enumerate(SEGS):
                        act.wait_ge(sem("c_full"), 6 * j + 3 * e + i + 1)
                        if i == 2:
                            A(W_[0:META, 1344:1360], PC[0:META, e, 320:336], ACT.Exp)
                        A(W_[:, a:b], zs(e, i)[:, 0:b - a], ACT.Exp).then_inc(sem("w_exp"), 1)

            sb_softplus(0, 0)
            with act.Fori(0, SBH // 2 - 1) as j:
                sb_weights(j)
                sb_softplus(j, 1)
            sb_weights(SBH // 2 - 1)
            act.wait_ge(sem("o_full"), SBH)
            high_first("wo")
            for k in range(8):
                tile_wait(act, "oT", 0, 2, k)
                A(r32(uh[:, k, :]), tile_of("oT", k)[:, 0:L], ACT.Copy).then_inc(sem("oT_high"), 1)
            watch("wo", 8, 2)
            ffn_act(1)

            squares("final", h2, S)
            deviation("final", S, 0)
            squares("even", h2, S)
            deviation("even", S, 0)
            high_input("even", S)
            act.wait_ge(sem("fl_v"), 1)
            t1 = ev["of"][0:FOXH, 1, :]
            A(t1, ev["of"][0:FOXH, 0, :], ACT.Abs)
            act.drain()
            A(t1, t1, ACT.Exp, scale=-1.0)
            act.drain()
            A(t1, t1, ACT.Ln, bias=1.0)
            signal(act, sem("fl_l"))
            for x in "fr":
                evacuate(f"ev_q{x}", 4, 4, ev[f"q{x}"], S, scale=DH ** -0.5 if x == "f" else 1.0, done="ev_full")
                evacuate(f"ev_k{x}", 4, 4, ev[f"k{x}"], S, done="ev_full")
                evacuate_v(f"ev_v{x}", 2, S, ev[f"v{x}"], "ev_full")

            def rows_act(name, per_it, it, before=None):
                for s in range(per_it + 1):
                    if s:
                        N = it * per_it + s - 1
                        par_ = (s - 1) % 2
                        PT = ev_od[name]["PT"][:, par_, :]
                        act.wait_ge(sem(name + "_tr"), N * 3 + 2)
                        A(PT[:, 512:1024], PS[1][:, 512:1024], ACT.Copy).then_inc(sem(name + "_pta"), 1)
                        act.wait_ge(sem(name + "_tr"), N * 3 + 3)
                        A(PT[:, 1024:1280], PC[:, 1, 0:256], ACT.Copy).then_inc(sem(name + "_pta"), 1)
                    if s < per_it:
                        if before and s == 0:
                            before(0)
                        act.wait_ge(sem(name + "_nm"), it * per_it + s + 2)
                        par_ = s % 2
                        for i, tiles in enumerate(TURNS):
                            for a in tiles:
                                p_ = ev_od[name]["Pm"][:, par_, OFF[a]:OFF[a] + P * (a + 1)]
                                A(p_, p_, ACT.Exp, bias=ev_od[name]["nm"][:, par_, a:a + 1],
                                  accum_out=ev_od[name]["rs"][:, s % 4, a:a + 1])
                            signal(act, sem(name + "_p"))
                        if before and s % 2 == 0 and s + 2 < per_it:
                            before(s + 2)

            act.sem_inc(sem("fx_pta"), 1)
            act.sem_inc(sem("ns_pta"), 1)
            with act.Fori(0, 2) as it:
                rows_act("fx", 4, it)
            with act.Fori(0, 2) as it:
                for h in range(4):
                    act.wait_ge(sem("ret_o"), it * 4 + h + 1)
                    A(ev["or"].rearrange("p a (h d) -> p a h d", h=RETH)[:, :, bass.ds(it * 4 + h, 1), :].rearrange(
                        "p a h d -> p a (h d)"), PD[:, h % 2, 0:256].rearrange("p (a d) -> p a d", a=4), ACT.Copy
                      ).then_inc(sem("ret_free"), 1)
            high_first("ev_z")
            high_input("ev_z", S)
            act.wait_ge(sem("gn_d"), 1)
            A(gn_squares, ev["or"].rearrange("p a b -> p (a b)"), ACT.Square)
            signal(act, sem("gn_sq"))
            act.wait_ge(sem("gn_var"), 1)
            A(ev["var"], ev["var"], ACT.Sqrt, bias=prm("gn_eps"), scale=1.0 / DH)
            signal(act, sem("gn_sd"))
            evacuate("ev_z", 8, 8, z_even, S, func=ACT.Silu, done="z_full2")
            watch("eout", 8, 2)
            squares("odd", h2, S)
            deviation("odd", S, 0)
            high_input("odd", S)
            act.wait_ge(sem("g_full"), 1)
            A(od["gates"].rearrange("p a b -> p (a b)"), od["gates"].rearrange("p a b -> p (a b)"), ACT.Sigmoid)
            signal(act, sem("gates_full"))
            evacuate("od_q", 8, 8, od["q"], S, scale=DH ** -0.5, done="od_full")
            for x in ("kc", "vc", "ks", "kw"):
                evacuate(f"od_{x}", 2, 2, odr[x], S)
                act.drain()
                act.sem_inc(sem("odk_full"), 2)
            evacuate_v("od_vs", 1, S, od["vs"], "od_full")
            evacuate_v("od_vw", 1, S, od["vw"], "od_full")
            for which, stage in enumerate(("ck", "cv")):
                for hid in range(2):
                    tile_wait(act, stage, 0, 2, hid)
                    t = tile_of(stage, hid)
                    A(od["hb"][:, 2 * which + hid:2 * which + hid + 1], t[:, BANK:BANK + 1], ACT.Copy)
                    act.drain()
                    b_ = od["hb"][:, 2 * which + hid:2 * which + hid + 1]
                    if which == 0:
                        A(od["h1"][:, hid, :], t[:, 0:P], ACT.Silu, bias=b_)
                    else:
                        A(od["h1v"][:, hid, 0, :, :], t[:, 0:CB].unsqueeze(1).to_broadcast([P, 4, CB]), ACT.Silu, bias=b_)
                        for g in range(1, NG):
                            A(od["h1v"][:, hid, g, :, :], t[:, CB * g:CB * (g + 1)].unsqueeze(1).to_broadcast([P, 4, CB]),
                              ACT.Silu, bias=b_)
                    signal(act, free_of(stage, hid), sem("h1_full"))
                tile_wait(act, stage + "2", 0, 2, 0)
                t = tile_of(stage + "2", 0)
                if which == 0:
                    A(od["kcmp"], t[:, 0:P], ACT.Copy)
                else:
                    act.wait_ge(sem("vbd_zero"), 1)
                    for i in range(4):
                        rows = slice(CB * i, CB * (i + 1))
                        A(od["Vbd"][rows, :, i * DH:(i + 1) * DH], t[rows, 0:256].rearrange("p (g d) -> p g d", g=NG), ACT.Copy)
                signal(act, free_of(stage + "2", 0), sem("od_full"))
            with act.Fori(0, NG) as g:
                act.wait_ge(sem("cx_full"), g + 1)
                A(ods["X"], ods["X"], ACT.Exp)
                signal(act, sem("cx_exp"))
                act.wait_ge(sem("ct_full"), g + 1)
                A(ods["PTc"], PS[1][:, 0:512], ACT.Copy)
                signal(act, sem("cpt_full"))

                def bias(n):
                    if n % 2 == 0:
                        i = n // 2
                        if i >= 2:
                            act.wait_ge(sem("ns_nm"), g * 8 + 2 * i - 1)
                        A(ods["bias"][:, i % 2, :], prm("alibi"), ACT.Copy, scale=prm("slopes")[:, bass.ds(4 * g + i, 1)])
                        signal(act, sem("bias_full"))
                rows_act("ns", 8, g, bias)
            act.wait_ge(sem("nsa_full"), 1)
            high_first("od_z")
            high_input("od_z", S)
            evacuate("od_z", 8, 8, z_odd, S, func=ACT.Silu, done="z_full2")
            watch("oout", 8, 2)
            squares("last", h2, S)
            deviation("last", S, 0)

        @block.vector
        def _(dve):
            V = nc.vector
            for b in range(2):
                dve.sem_inc(ps_free[b], 1)
            for name, n in (("pd_free", 2), ("grp_done", 1)):
                dve.sem_inc(sem(name), n)
            dve.wait_ge(loaded, 32)

            def normalise(name, h, width, outs, h0=0):
                dve.wait_ge(sd_full, NORM[name] + 1)
                V.reciprocal(rstd[:, 0:width], sd[:, 0:width])
                dve.drain()
                for dst, gain in outs:
                    for k in range(KD):
                        V.scalar_tensor_tensor(dst[:, k, 0:width], h[:, k, h0:h0 + width], prm(gain)[:, k:k + 1],
                                               rstd[:, 0:width], ALU.mult, ALU.mult).then_inc(u_full, 1)

            def normalise_split(name, h, width, dst, gain, fresh=True):
                if fresh:
                    dve.wait_ge(sd_full, NORM[name] + 1)
                    V.reciprocal(rstd[:, 0:width], sd[:, 0:width])
                    dve.drain()
                for k in range(KD + 1):
                    if k < KD:
                        V.scalar_tensor_tensor(sq[:, k % 2, 0:width], h[:, k, 0:width], prm(gain)[:, k:k + 1],
                                               rstd[:, 0:width], ALU.mult, ALU.mult).then_inc(sem("u_raw"), 1)
                    if k:
                        j = k - 1
                        dve.wait_ge(sem("uh_full"), UH_BASE[name] + j + 1)
                        V.tensor_tensor(r32(dst[:, j, 0:width]), sq[:, j % 2, 0:width], split(uh[:, j, 0:width]),
                                        ALU.subtract).then_inc(u_full, 1)
                        dve.drain()

            V.memset(ssd["raw"][:, 0:CONV - 1], 0.0).then_inc(sem("raw_pad"), 1)
            V.memset(ssd_dt["one"][0:32, :], 1.0)
            normalise("ssd", hT, L, [(uT, "ssd_norm")])
            tile_wait(dve, "dt", 0, 2, 0)
            dtv, dtt, dt = (ssd_dt[n][0:32, :] for n in ("dtv", "dtt", "dt"))
            V.tensor_scalar(dtv, tile_of("dt", 0)[0:32, V0:V0 + L], prm("dt_bias", 32), None, ALU.add)
            signal(dve, sem("dtv_full"), free_of("dt", 0))
            dve.wait_ge(sem("sp_full"), 1)
            V.scalar_tensor_tensor(dt, dtv, 0.0, dtt, ALU.max, ALU.add)
            dve.drain()
            V.tensor_scalar(dtv, dt, ssd["ea"][0:32, :], -1.0, ALU.mult, ALU.mult)
            dve.drain()
            for at, n in CHUNKS:
                last = V.tensor_tensor_scan(acs_keep[:, at:at + n], ssd_dt["one"][0:32, at:at + n],
                                            dtv[:, at:at + n], 0.0, ALU.mult, ALU.add)
            last.then_inc(sem("acs_full"), 1)

            def conv_tile(n, tile, slot=None):
                raw, cv = ssd["raw"], ssd["cv"]
                w = lambda k: prm("conv_w")[:, bass.ds(tile * CONV + k, 1)]
                dve.wait_ge(raw_full, n + 1)
                V.tensor_scalar(cv, raw[:, 0:L], w(0), prm("conv_b")[:, bass.ds(tile, 1)], ALU.mult, ALU.add)
                for k in range(1, CONV):
                    dve.drain()
                    last = V.scalar_tensor_tensor(cv, raw[:, k:k + L], w(k), cv, ALU.mult, ALU.add)
                last.then_inc(conv_full, 1)

            for j in range(8):
                conv_tile(j, j)
            tile_wait(dve, "dtt", 0, 2, 0)
            t = tile_of("dtt", 0)
            V.tensor_copy(ssd["dtT"][0:META, 0, :], t[0:META, 0:32])
            V.tensor_copy(ssd["dtT"][:, 1:5, :], t[:, 32:160].rearrange("p (a b) -> p a b", a=4))
            V.tensor_copy(ssd["acsT"][0:META, 0, :], t[0:META, BANK:BANK + 32])
            V.tensor_copy(ssd["acsT"][:, 1:5, :], t[:, BANK + 32:BANK + 160].rearrange("p (a b) -> p a b", a=4))
            signal(dve, sem("acsT_full"), free_of("dtt", 0))
            tile_wait(dve, "end", 0, 2, 0)
            t = tile_of("end", 0)
            V.tensor_tensor(ssd["w2"][0:META, 0, :], t[0:META, 0:32], ssd["acsT"][0:META, 0, :], ALU.subtract)
            V.tensor_tensor(ssd["w2"][:, 1:5, :], t[:, 32:160].rearrange("p (a b) -> p a b", a=4),
                            ssd["acsT"][:, 1:5, :], ALU.subtract).then_inc(sem("wdiff_full"), 1)
            dve.wait_ge(sem("w2_exp"), 1)
            V.tensor_tensor(ssd["w2"][0:META, 0, :], ssd["w2"][0:META, 0, :], ssd["dtT"][0:META, 0, :], ALU.mult)
            V.tensor_tensor(ssd["w2"][:, 1:5, :], ssd["w2"][:, 1:5, :], ssd["dtT"][:, 1:5, :], ALU.mult)
            dve.drain()
            dve.wait_ge(sem("dc_full"), 1)

            Xs, Zs, S_, Dm, L0, yT = (ssd[n] for n in ("Xs", "Zs", "S", "Dm", "L0", "yT"))

            def per_head(a, n):
                return a.rearrange("p (h d) -> p h d", h=HPG)

            def of_heads(a, n, c, g):
                return a[0:n, c, bass.ds(g * HPG, HPG)].unsqueeze(2).to_broadcast([n, HPG, DH])

            with dve.Fori(0, GROUPS) as g:
                for q in range(4):
                    conv_tile(g * 4 + 8 + q, g * 4 + 8 + q)
                tile_wait(dve, "grp", g, GT, 9)
                t = tile_of("grp", 9)
                V.tensor_tensor(ssd["Gm0"][0:META, :], t[0:META, BANK:BANK + META], prm("mask_sl", META)[:, 0:META],
                                ALU.mult)
                V.tensor_tensor(ssd["Gm"][:, :, :], t[:, 0:BANK].rearrange("p (a b) -> p a b", a=4),
                                prm("mask_sl").unsqueeze(1).to_broadcast([P, 4, P]), ALU.mult
                                ).then_inc(free_of("grp", 9), 1)
                tile_wait(dve, "grp", g, GT, 10)
                V.tensor_tensor(L0[0:META, :, :],
                                tile_of("grp", 10)[0:META, 0:HPG * META].rearrange("p (h l) -> p h l", h=HPG),
                                ssd["acsT"][0:META, 0, bass.ds(g * HPG, HPG)].unsqueeze(2).to_broadcast(
                                    [META, HPG, META]), ALU.subtract).then_inc(free_of("grp", 10), 1)
                dve.drain()
                V.tensor_scalar(L0[0:META, :, :], L0[0:META, :, :], 0.0, None, ALU.min).then_inc(sem("l0_full"), 1)
                for j, cs in ((11, [0]), (12, [1, 2]), (13, [3, 4])):
                    tile_wait(dve, "grp", g, GT, j)
                    for i, c in enumerate(cs):
                        n = CHUNKS[c][1]
                        x = per_head(tile_of("grp", j)[0:n, i * BANK:(i + 1) * BANK], n)
                        V.tensor_tensor(per_head(xw2[0:n, c, :], n), x, of_heads(ssd["w2"], n, c, g), ALU.mult
                                        ).then_inc(sem("xw_full"), 1)
                        last = V.tensor_tensor(per_head(xdt[0:n, c, :], n), x, of_heads(ssd["dtT"], n, c, g), ALU.mult)
                    last.then_inc(free_of("grp", j), 1)
                for c in range(4):
                    tile_wait(dve, "grp", g, GT, 14 + c)
                    add = tile_of("grp", 14 + c)[:, 0:BANK]
                    if c == 0:
                        V.tensor_copy(S_[:, 0, :], add).then_inc(free_of("grp", 14), 1)
                    else:
                        V.tensor_tensor(per_head(S_[:, c, :], P), per_head(S_[:, c - 1, :], P),
                                        of_heads(ssd["dC"], P, c, g), ALU.mult)
                        dve.drain()
                        V.tensor_tensor(S_[:, c, :], S_[:, c, :], add, ALU.add).then_inc(free_of("grp", 14 + c), 1)
                    dve.drain()
                    dve.sem_inc(sem("state_full"), 1)
                for j in range(2):
                    tile_wait(dve, "grp", g, GT, 18 + j)
                    for i in range(2):
                        c = 1 + 2 * j + i
                        last = V.tensor_tensor(per_head(ytok[:, c, :], P),
                                               per_head(tile_of("grp", 18 + j)[:, i * BANK:(i + 1) * BANK], P),
                                               of_heads(ssd["eacs"], P, c, g), ALU.mult)
                    last.then_inc(free_of("grp", 18 + j), 1)
                dve.wait_ge(sem("l0_exp"), g + 1)
                V.tensor_tensor(L0[0:META, :, :], L0[0:META, :, :],
                                ssd["Gm0"][0:META, :].unsqueeze(1).to_broadcast([META, HPG, META]), ALU.mult
                                ).then_inc(sem("m0_full"), 1)

                def decay(e):
                    dve.wait_ge(sem("pc_full"), HPG * g + e + 1)
                    for c in range(4):
                        last = V.tensor_scalar(decays(e)[:, c * P:(c + 1) * P], PC[:, e % 2, c * P:(c + 1) * P],
                                               ssd["acsT"][:, c + 1, bass.ds(g * HPG + e, 1)], 0.0,
                                               ALU.subtract, ALU.min)
                    last.then_inc(sem("dm_full"), 1)

                def weigh(e):
                    dve.wait_ge(sem("dm_exp"), HPG * g + e + 1)
                    V.tensor_tensor(decays(e), decays(e), ssd["Gm"].rearrange("p a b -> p (a b)"),
                                    ALU.mult).then_inc(sem("mt_full"), 1)

                def gather(e):
                    dve.wait_ge(sem("pd_full"), HPG * g + e + 1)
                    y = ytok[:, 1:5, e * DH:(e + 1) * DH]
                    V.tensor_tensor(y, y, PD[:, e % 2, 0:4 * DH].rearrange("p (c d) -> p c d", c=4), ALU.add
                                    ).then_inc(sem("pd_free"), 1)

                dve.drain()
                for e in range(HPG + 2):
                    if e < HPG:
                        decay(e)
                    if 1 <= e <= HPG:
                        weigh(e - 1)
                    if e >= 2:
                        gather(e - 2)
                tile_wait(dve, "grp", g, GT, 20)
                V.tensor_copy(ytok[0:META, 0, :], tile_of("grp", 20)[0:META, 0:BANK]).then_inc(free_of("grp", 20), 1)
                dve.drain()
                dve.sem_inc(sem("ytok_full"), 1)
                for q in range(4):
                    tile_wait(dve, "grp", g, GT, 21 + q)
                    V.scalar_tensor_tensor(Xs[:, q, :], Xs[:, q, :], prm("d_skip")[:, bass.ds(4 * g + q, 1)],
                                           tile_of("grp", 21 + q)[:, BANK - META:BANK - META + L],
                                           ALU.mult, ALU.add).then_inc(free_of("grp", 21 + q), 1)
                    dve.drain()
                    V.tensor_tensor(yT[:, bass.ds(4 * g + q, 1), :].rearrange("p a l -> p (a l)"), Xs[:, q, :],
                                    Zs[:, q, :], ALU.mult).then_inc(sem("y2_full"), 1)
                dve.wait_ge(sem("gsd_full"), g + 1)
                V.reciprocal(rstd[:, :], sd[:, :])
                dve.drain()
                for q in range(4):
                    y = yT[:, bass.ds(4 * g + q, 1), :].rearrange("p a l -> p (a l)")
                    V.scalar_tensor_tensor(y, y, prm("gate_norm")[:, bass.ds(4 * g + q, 1)], rstd[:, :],
                                           ALU.mult, ALU.mult).then_inc(sem("yT_full"), 1)
                dve.sem_inc(sem("grp_done"), 1)
            dve.drain()

            def residual(stage, n, per, final=True):
                def body(it, count):
                    for j in range(count):
                        tile_wait(dve, stage, it, per, j)
                        h = hT[:, bass.ds(it * per + j, 1), :].rearrange("p a l -> p (a l)")
                        V.tensor_tensor(h, h, tile_of(stage, j)[:, V0:V0 + L], ALU.add).then_inc(free_of(stage, j), 1)
                        dve.drain()
                        if final:
                            dve.sem_inc(h_upd, 1)
                steps(dve, n, per, body)

            residual("sout", 8, R)

            def ffn_dve(i):
                for raw in ("rawg", "rawv"):
                    last = V.memset(ffn[raw][:, 0:FCONV - 1], 0.0)
                last.then_inc(sem("fpad"), 1)
                normalise_split(f"ffn{i}", hT, L, uT, f"ffn_norm{i}")
                for half, part in enumerate("ab"):
                    stage = f"ffn{i}{part}"
                    n0 = DK * (2 * i + half)

                    def body(it, count):
                        for r in range(count):
                            for m, (raw, cv) in enumerate((("rawg", "cg"), ("rawv", "cvv"))):
                                t = 2 * (DK * half + r) + m
                                w = lambda k: prm(f"fconv_w{i}")[:, bass.ds(it * 2 * R * FCONV + t * FCONV + k, 1)]
                                b = prm(f"fconv_b{i}")[:, bass.ds(it * 2 * R + t, 1)]
                                dve.wait_ge(raw_full, it * 2 * R + 24 + 2 * (n0 + r) + m + 1)
                                V.tensor_scalar(ffn[cv], ffn[raw][:, 0:L], w(0), b, ALU.mult, ALU.add)
                                for k in range(1, FCONV):
                                    dve.drain()
                                    last = V.scalar_tensor_tensor(ffn[cv], ffn[raw][:, k:k + L], w(k), ffn[cv],
                                                                  ALU.mult, ALU.add)
                                last.then_inc(conv_full, 1)
                            dve.wait_ge(sem("glu"), it * R + n0 + r + 1)
                            V.tensor_tensor(ffn["cg"], ffn["cg"], ffn["cvv"], ALU.mult)
                            dve.drain()
                            hi, rest = (ffn[n][:, bass.ds(it * R + r, 1), :].rearrange("p a l -> p (a l)")
                                        for n in ("acth", "act"))
                            V.tensor_copy(r32(hi, 0), ffn["cg"])
                            dve.drain()
                            V.tensor_tensor(r32(rest, 0), ffn["cg"], split(hi, 0), ALU.subtract).then_inc(sem("act_full"), 1)
                            dve.drain()
                    steps(dve, DK, R, body)
                    residual(f"down{i}{part}", 8, R, final=half == 1)

            ffn_dve(0)


            V.memset(sbm["v"][:, 4, :], 0.0)
            V.tensor_copy(ident_b[:, :], ident)
            V.tensor_copy(hidden_b[:, :], prm("hidden"))
            signal(dve, sem("v_zero"))
            normalise_split("sb", hT, L, uT, "kv_norm")
            dve.drain()
            for which, u_ in enumerate((uT, uh)):
                V.tensor_copy(r32(tails[:, which, :, :]).rearrange("p k (c t) -> p k c t", c=P // META),
                              split(u_[:, :, S:L]).unsqueeze(2).to_broadcast([P, KD, P // META, META]))
            signal(dve, sem("tails_full"))
            normalise_split("sbq", hT, L, u2, "sb_norm", fresh=False)
            tile_wait(dve, "sbq", 0, 8, 7)
            V.memset(sbm["W"][:, :, 1344:1360], 0.0)
            signal(dve, sem("w_zero"))
            dve.sem_inc(sem("o_free"), 2)
            SEGS = [(0, 512), (512, 1024), (1024, 1344)]
            TAIL = slice(1344, 1360)
            zs = lambda e, seg: PS[e][:, seg * BANK:(seg + 1) * BANK] if seg < 2 else PC[:, e, :]

            def sb_softplus(j, ahead, e):
                for i, (a, b) in enumerate(SEGS):
                    dve.wait_ge(sem("l_full"), 6 * j + 6 * ahead + 3 * e + i + 1)
                    if i == 2:
                        V.scalar_tensor_tensor(sbm["SP"][0:META, e, TAIL], PC[0:META, e, 320:336], 0.0,
                                               sbm["A"][0:META, e, TAIL], ALU.max, ALU.add)
                    V.scalar_tensor_tensor(sbm["SP"][:, e, a:b], zs(e, i)[:, 0:b - a], 0.0, sbm["A"][:, e, a:b],
                                           ALU.max, ALU.add).then_inc(sem("sp_full2"), 1)

            def sb_out(j, e):
                dve.wait_ge(sem("o_full"), 2 * j + e + 1)
                V.tensor_copy(sbm["o"][0:META, 4, bass.ds((2 * j + e) * DH, DH)], PD[0:META, e, 256:320])
                V.tensor_copy(sbm["o"][:, 0:4, bass.ds((2 * j + e) * DH, DH)],
                              PD[:, e, 0:256].rearrange("p (a d) -> p a d", a=4)).then_inc(sem("o_free"), 1)

            for e in range(2):
                sb_softplus(0, 0, e)
            with dve.Fori(0, SBH // 2 - 1) as j:
                for e in range(2):
                    sb_out(j, e)
                    sb_softplus(j, 1, e)
            for e in range(2):
                sb_out(SBH // 2 - 1, e)
            for k in range(8):
                dve.wait_ge(sem("oT_high"), k + 1)
                V.tensor_tensor(r32(uT[:, k, :]), tile_of("oT", k)[:, 0:L], split(uh[:, k, :]), ALU.subtract)
                signal(dve, free_of("oT", k), sem("oT_full"))
            residual("wo", 8, R)
            ffn_dve(1)

            def residual2(stage):
                for j in range(8):
                    tile_wait(dve, stage, 0, 8, j)
                    V.tensor_tensor(h2[:, j, :], h2[:, j, :], tile_of(stage, j)[:, 0:S], ALU.add)
                    signal(dve, free_of(stage, j), h_upd)

            dve.wait_ge(sd_full, NORM["final"] + 1)
            V.reciprocal(rstd[:, 0:S], sd[:, 0:S])
            dve.drain()
            for k in range(KD):
                V.scalar_tensor_tensor(h2[:, k, :], h2[:, k, :], prm("final_norm")[:, k:k + 1], rstd[:, 0:S],
                                       ALU.mult, ALU.mult).then_inc(h_upd, 1)
            dve.drain()
            normalise_split("even", h2, S, uv, "even_norm")
            fv, fl, fone = (ev["of"][0:FOXH, n, :] for n in range(3))
            tile_wait(dve, "ev_f", 0, 2, 0)
            V.tensor_scalar(fv, tile_of("ev_f", 0)[0:FOXH, 0:S], prm("b_f", FOXH), None, ALU.add)
            V.memset(fone, 1.0)
            signal(dve, sem("fl_v"), free_of("ev_f", 0))
            dve.wait_ge(sem("fl_l"), 1)
            V.tensor_scalar(fv, fv, 0.0, None, ALU.min)
            dve.drain()
            V.tensor_tensor(fl, fl, fv, ALU.subtract)
            dve.drain()
            V.tensor_tensor_scan(ev["negc"][0:FOXH, :], fone, fl, 0.0, ALU.mult, ALU.add)
            signal(dve, sem("negc_full"))

            def rows_dve(name, per_it, it, table, finish):
                m = ev_od[name]
                for s in range(per_it + 2):
                    par_ = s % 2
                    if s < per_it:
                        N = it * per_it + s
                        t_ = table(s)
                        for i, tiles in enumerate(TURNS):
                            dve.wait_ge(sem(name + "_s"), N * 3 + i + 1)
                            dve.sem_inc(sem(name + "_seen"), 1)
                            for a in tiles:
                                w = P * (a + 1)
                                V.tensor_tensor_reduce(out=m["Pm"][:, par_, OFF[a]:OFF[a] + w], in0=scores_at(0, a),
                                                       in1=t_[:, 512 - w:512], scale=1.0, scalar=-3e38, op0=ALU.add,
                                                       op1=ALU.max, accum_out=m["nm"][:, par_, a:a + 1])
                        dve.drain()
                        V.tensor_scalar(m["nm"][:, par_, :], m["nm"][:, par_, :], -1.0, None, ALU.mult
                                        ).then_inc(sem(name + "_nm"), 1)
                    if 1 <= s <= per_it:
                        n = s - 1
                        dve.wait_ge(sem(name + "_tr"), (it * per_it + n) * 3 + 1)
                        V.tensor_copy(m["PT"][:, n % 2, 0:512], PS[1][:, 0:512]).then_inc(sem(name + "_ptd"), 1)
                    if s >= 2:
                        n = s - 2
                        q = n % 2
                        dve.wait_ge(sem(name + "_o"), it * per_it + n + 1)
                        V.reciprocal(m["ri"][:, q, :], m["rs"][:, n % 4, :])
                        dve.drain()
                        finish(n, q)
                        signal(dve, sem(name + "_comb"))

            for name in ("fx", "ns"):
                dve.sem_inc(sem(name + "_nm"), 1)
                dve.sem_inc(sem(name + "_ptd"), 1)
                dve.sem_inc(sem(name + "_comb"), 2)
            dve.sem_inc(sem("ret_m"), 2)
            dve.sem_inc(sem("ret_free"), 2)
            with dve.Fori(0, 2) as it:
                def fox_out(h, q):
                    V.tensor_tensor(ev["of"][:, :, bass.ds((it * 4 + h) * DH, DH)],
                                    PD[:, q, 0:256].rearrange("p (a d) -> p a d", a=4),
                                    ev["ri"][:, q, :].unsqueeze(2).to_broadcast([P, 4, DH]), ALU.mult)
                rows_dve("fx", 4, it, lambda s: prm("causal"), fox_out)
            dve.wait_ge(sem("decay_in"), 16)
            with dve.Fori(0, 2) as it:
                for h in range(4):
                    dve.drain()
                    dve.wait_ge(sem("ret_s"), it * 4 + h + 1)
                    for i in (0, 1, 3, 2):
                        w = S - P * i
                        last = V.tensor_tensor(ev["Pm"][:, h % 2, DOFF[i]:DOFF[i] + w], decayed_at(h % 2, i),
                                               ev["decay"][:, bass.ds(it * 4 + h, 1), 0:w].rearrange("p a b -> p (a b)"),
                                               ALU.mult)
                    last.then_inc(sem("ret_m"), 1)
            normalise_split("ev_z", h2, S, uv, "even_norm", fresh=False)
            rt = ev["or"].rearrange("p a (h d) -> p (a h) d", h=RETH)
            dve.wait_ge(sem("ret_free"), 10)
            V.tensor_reduce(ev["mu"], rt, AX.X, ALU.add)
            dve.drain()
            V.tensor_scalar(ev["mu"], ev["mu"], 1.0 / DH, None, ALU.mult)
            dve.drain()
            V.tensor_tensor(rt, rt, ev["mu"].unsqueeze(2).to_broadcast([P, 32, DH]), ALU.subtract)
            signal(dve, sem("gn_d"))
            dve.wait_ge(sem("gn_sq"), 1)
            V.tensor_reduce(ev["var"], gn_squares.rearrange("p (a d) -> p a d", a=32), AX.X, ALU.add)
            signal(dve, sem("gn_var"))
            dve.wait_ge(sem("gn_sd"), 1)
            V.reciprocal(ev["mu"], ev["var"])
            dve.drain()
            V.tensor_tensor(rt, rt, ev["mu"].unsqueeze(2).to_broadcast([P, 32, DH]), ALU.mult)
            signal(dve, sem("mix_full"))

            def gated(stage, z, gn):
                dve.wait_ge(sem("z_full2"), 1 if gn else 2)
                for k in range(8):
                    tile_wait(dve, stage, 0, 2, k)
                    t, y = tile_of(stage, k)[:, 0:S], sq[:, k % 2, 0:S]
                    if gn and k >= 4:
                        V.scalar_tensor_tensor(y, t, prm("gn_g")[:, k - 4:k - 3], z[:, k, :], ALU.mult, ALU.mult)
                    else:
                        V.tensor_tensor(y, t, z[:, k, :], ALU.mult)
                    signal(dve, free_of(stage, k))
                    V.tensor_copy(r32(uhs[:, k, :]), y)
                    dve.drain()
                    V.tensor_tensor(r32(uv[:, k, :]), y, split(uhs[:, k, :]), ALU.subtract).then_inc(sem("y_full"), 1)

            gated("ev_y", z_even, True)
            residual2("eout")
            V.memset(od["A2"].rearrange("p a b c -> p (a b c)"), 0.0)
            signal(dve, sem("pad2"))
            normalise_split("odd", h2, S, uv, "odd_norm")
            tile_wait(dve, "od_g", 0, 2, 0)
            V.tensor_tensor(od["gates"][:, :, :].rearrange("p c a -> p a c"),
                            tile_of("od_g", 0)[:, 0:192].rearrange("p (a c) -> p a c", a=4),
                            prm("b_gate").unsqueeze(1).to_broadcast([P, 4, 48]), ALU.add)
            signal(dve, sem("g_full"), free_of("od_g", 0))
            tile_wait(dve, "od_vw", 0, 4, 3)
            V.memset(od["Vbd"][:, :, :], 0.0)
            signal(dve, sem("vbd_zero"))
            dve.wait_ge(sem("gates_full"), 1)
            dve.wait_ge(sem("cmp_in"), 16)
            with dve.Fori(0, NG) as g:
                def gate(b):
                    v = od["gates"].rearrange("p (h b) a -> p h b a", b=3)
                    return v[:, bass.ds(4 * g, 4), b, :]

                X, P2 = ods["X"], ods["P2"]
                dve.wait_ge(sem("cs_full"), g + 1)
                V.tensor_tensor(X.rearrange("p (j e c) -> p e j c", j=2, e=2),
                                PS[0].rearrange("p (e k) -> p e k", e=2)[:, :, 0:256].rearrange("p e (j c) -> p e j c", j=2),
                                od["cmp_bias"][:, bass.ds(4 * g, 4), :].rearrange("p (j e) c -> p e j c", j=2), ALU.add)
                dve.drain()
                X3 = X.rearrange("p (a c) -> p a c", a=16)
                V.tensor_reduce(od["mxc"], X3, AX.X, ALU.max)
                dve.drain()
                V.tensor_tensor(X3, X3, od["mxc"].unsqueeze(2).to_broadcast([P, 16, CB]), ALU.subtract)
                signal(dve, sem("cx_full"))
                dve.wait_ge(sem("cx_exp"), g + 1)
                V.tensor_reduce(od["rsc"], X3, AX.X, ALU.add)
                V.tensor_tensor(P2.rearrange("p (a i c) -> p i a c", a=4, i=4), X.rearrange("p (i a c) -> p i a c", i=4, a=4),
                                prm("cmp_seen").rearrange("p (a c) -> p a c", a=4).unsqueeze(1).to_broadcast([P, 4, 4, CB]),
                                ALU.mult)
                signal(dve, sem("cp_full"))
                V.reciprocal(od["rsc"], od["rsc"])
                dve.drain()
                V.tensor_tensor(od["cfc"].rearrange("p (i a) -> p i a", i=4), od["rsc"].rearrange("p (i a) -> p i a", i=4),
                                gate(0), ALU.mult)
                dve.drain()
                dve.wait_ge(sem("co_full"), g + 1)
                V.tensor_tensor(od["o"].rearrange("p a (h d) -> p a h d", d=DH)[:, :, bass.ds(4 * g, 4), :],
                                PS[0][:, :].rearrange("p (a i d) -> p a i d", a=4, i=4),
                                od["cfc"].rearrange("p (i a) -> p a i", i=4).unsqueeze(3).to_broadcast([P, 4, 4, DH]),
                                ALU.mult)
                signal(dve, sem("cc_full"))

                def table(n):
                    if n % 2 == 0:
                        dve.wait_ge(sem("bias_full"), 4 * g + n // 2 + 1)
                    return ods["bias"][:, n // 2 % 2, :]

                def add_out(n, q):
                    i, b = n // 2, 1 + n % 2
                    gt = od["gates"].rearrange("p (h b) a -> p h b a", b=3)[:, bass.ds(4 * g + i, 1), b, :]
                    V.tensor_tensor(od["ri"][:, q, :], od["ri"][:, q, :], gt.rearrange("p h a -> p (h a)"), ALU.mult)
                    dve.drain()
                    t_ = ods["X"][:, 0:256].rearrange("p (a d) -> p a d", a=4)
                    V.tensor_tensor(t_, PD[:, q, 0:256].rearrange("p (a d) -> p a d", a=4),
                                    od["ri"][:, q, :].unsqueeze(2).to_broadcast([P, 4, DH]), ALU.mult)
                    dve.drain()
                    o_ = od["o"][:, :, bass.ds((4 * g + i) * DH, DH)]
                    V.tensor_tensor(o_, o_, t_, ALU.add)
                rows_dve("ns", 8, g, table, add_out)
            signal(dve, sem("nsa_full"))
            normalise_split("od_z", h2, S, uv, "odd_norm", fresh=False)
            gated("od_y", z_odd, False)
            residual2("oout")
            normalise("last", h2, S, [(uv, "final_g")])

        @block.gpsimd
        def _(pool):
            G = nc.gpsimd
            pool.wait_ge(loaded, 32)
            pool.wait_ge(sem("bc_full"), 8)
            with pool.Fori(0, GROUPS) as g:
                pool.wait_ge(sem("grp_done"), g + 1)
                G.tensor_copy(ssd["Bs"], ssd["BCt"][:, bass.ds(g, 1), :].rearrange("p a l -> p (a l)"))
                G.tensor_copy(ssd["Cs"], ssd["BCt"][:, bass.ds(g + GROUPS, 1), :].rearrange("p a l -> p (a l)"))
                G.tensor_copy(ssd["sel"][0:32, :, :], ident[0:32, bass.ds(g * HPG, HPG)].unsqueeze(2).to_broadcast(
                    [32, HPG, P])).then_inc(sem("bc_staged"), 1)

            def rests(run):
                for stage, n in STREAM:
                    if RUN_OF.get(stage) != run:
                        continue
                    width = width_of(stage)

                    def body(it, count):
                        for r in range(count):
                            pool.wait_ge(sem("high_full"), it * R + H0[stage] + r + 1)
                            G.tensor_tensor(r32(rest_slot(H0[stage] + r)[:, 0:width]),
                                            raw_slot(H0[stage] + r)[:, 0:width], split(high_slot(H0[stage] + r)[:, 0:width]), ALU.subtract
                                            ).then_inc(sem("rest_full"), 1)
                    steps(pool, n, R, body)

            rests(0)

            pool.sem_inc(sem("z_full"), 1)
            pool.wait_ge(sem("qkv_full"), 3)

            with pool.Fori(0, SBH // 2) as j:
                pool.wait_ge(sem("z_full"), 6 * j + 1)
                G.tensor_copy(sbm["ks"], sbm["kT"][:, bass.ds(j, 1), :].rearrange("p a l -> p (a l)"))
                G.tensor_copy(sbm["qs"], sbm["qT"][:, bass.ds(j, 1), :].rearrange("p a l -> p (a l)")
                              ).then_inc(sem("staged"), 1)
            rests(1)

            pool.wait_ge(sem("ev_full"), 6)
            with pool.Fori(0, 2) as it:
                pool.wait_ge(sem("fx_nm"), it * 4 + 1)
                G.tensor_copy(ev["qs"], ev["qf"][:, bass.ds(2 * it, 2), :])
                G.tensor_copy(ev["ks"], ev["kf"][:, bass.ds(2 * it, 2), :])
                G.tensor_copy(ev["sel"][0:FOXH, :, :], ident[0:FOXH, bass.ds(4 * it, 4)].unsqueeze(2).to_broadcast(
                    [FOXH, 4, P])).then_inc(sem("fstaged"), 1)
            pool.wait_ge(sem("fx_nm"), 9)
            with pool.Fori(0, 2) as it:
                pool.wait_ge(sem("ret_m"), it * 4 + 2)
                G.tensor_copy(ev["qs"], ev["qr"][:, bass.ds(2 * it, 2), :])
                G.tensor_copy(ev["ks"], ev["kr"][:, bass.ds(2 * it, 2), :]).then_inc(sem("fstaged"), 1)
            rests(2)
            pool.wait_ge(sem("od_full"), 5)
            pool.wait_ge(sem("dup"), 16 * 8 * NG)
            with pool.Fori(0, NG) as g:
                pool.wait_ge(sem("ns_nm"), g * 8 + 1)
                G.tensor_copy(ods["qs"], od["q"][:, bass.ds(2 * g, 2), :])
                G.tensor_copy(ods["kss"], od["ksd"][:, bass.ds(g, 1), :].rearrange("p a b -> p (a b)"))
                G.tensor_copy(ods["kws"], od["kwd"][:, bass.ds(g, 1), :].rearrange("p a b -> p (a b)"))
                G.tensor_copy(ods["kcs"], od["kcmp"][:, bass.ds(g * CB, CB)]).then_inc(sem("gstaged"), 1)
            rests(3)


TILES_PER_UNIT = {"sout": 1, "sbv": 5, "down0a": 1, "down0b": 1, "down1a": 1, "down1b": 1, "ev_vf": 4, "ev_vr": 4, "od_vs": 4,
                  "od_vw": 4, "ck": 1, "cv": 1}
TILE_STEP = {"grp": GT}


def tile_w(w, kt, m0, m1):
    return w[:, m0:m1].reshape(kt, P, m1 - m0).transpose(1, 0, 2).reshape(P, -1)


def pack(i):
    f = np.float32
    W = i["ssd_w_in"][0]
    cols = lambda w, a, n, step=256: [tile_w(w, KD, a + step * u, a + step * (u + 1)) for u in range(n)]
    units = cols(W, 2 * DI, 4)
    for g in range(GROUPS):
        units += cols(W, DI + 512 * g, 2) + cols(W, 512 * g, 2)
    units += [tile_w(i["ssd_w_out"][0], 16, P * m, P * (m + 1)) for m in range(8)]

    def up(l):
        w = i["ffn_w_up"][l]
        F = FT * P
        return [tile_w(np.concatenate([w[:, P * j:P * j + P], w[:, F + P * j:F + P * j + P]], 1), KD, 0, 256)
                for j in range(FT)]
    units += up(0)
    kv = i["w_kv"]
    units += cols(kv, 0, 4) + cols(kv, D, 4) + cols(i["sb_w_q"][0], 0, 4) + cols(i["sb_w_o"][0], 0, 4) + up(1)
    ev = i["even_w_in_2"][0]
    for a in (0, 512, 1024, 1544, 2056, 2568):
        units += cols(ev, a, 2)
    units += cols(ev, 3080, 4) + cols(i["even_w_out_2"][0], 0, 4)
    od = i["odd_w_in_2"][0]
    units += cols(od, 0, 4)
    for n in (0, 1, 2, 4, 3, 5):
        units += cols(od, 1024 + 256 * n, 1)
    for w in (i["odd_wk1_2"][0], i["odd_wv1_2"][0]):
        units += [tile_w(w, 16, P * m, P * (m + 1)) for m in range(2)]
    units += cols(od, 2608, 4) + cols(i["odd_w_out_2"][0], 0, 4)
    stream = np.stack(units)
    down = np.stack([tile_w(i["ffn_w_down"][l][DK * P * half:DK * P * (half + 1)], DK, P * m, P * (m + 1))
                     for l in range(2) for half in range(2) for m in range(8)])

    par = np.zeros((P, N_PARAMS), f)

    def put(name, a, rows=P):
        at, n = PARAMS[name]
        par[0:rows, at:at + n] = np.asarray(a).reshape(rows, n)

    col = lambda v: v.reshape(-1, P).T
    for name, v in (("ssd_norm", i["ssd_norm"][0]), ("kv_norm", i["kv_norm"]), ("sb_norm", i["sb_norm"][0]),
                    ("ffn_norm0", i["ffn_norm"][0]), ("ffn_norm1", i["ffn_norm"][1]),
                    ("final_norm", i["final_norm"]), ("even_norm", i["even_norm_g_2"][0]),
                    ("odd_norm", i["odd_norm_g_2"][0]), ("final_g", i["final_g_2"]),
                    ("gate_norm", i["ssd_gate_norm"][0]), ("gn_g", i["even_gn_g_2"][0])):
        put(name, col(v))
    order = np.concatenate([np.arange(DI, DI + 1024), np.arange(DI)])
    put("conv_w", i["ssd_conv_w"][0][:, order].reshape(CONV, 24, P).transpose(2, 1, 0))
    put("conv_b", col(i["ssd_conv_b"][0][order]))
    for l in range(2):
        w = i["ffn_conv_w"][l].reshape(FCONV, 2, FT, P)
        put(f"fconv_w{l}", w.transpose(3, 2, 1, 0))
        put(f"fconv_b{l}", i["ffn_conv_b"][l].reshape(2, FT, P).transpose(2, 1, 0))
    put("d_skip", np.repeat(i["ssd_d_skip"][0], DH).reshape(16, P).T)
    put("dt_bias", i["ssd_dt_bias"][0], 32)
    put("a_log", i["ssd_a_log"][0], 32)
    put("w_dt", tile_w(W, KD, 2 * DI + 1024, 2 * DI + 1056))
    put("w_f", tile_w(ev, KD, 1536, 1544))
    put("w_gate", tile_w(od, KD, 2560, 2608))
    put("b_f", i["even_b_f_2"][0], 8)
    put("b_gate", np.broadcast_to(i["odd_b_gate_2"][0], (P, 48)))
    for name, v in (("pe_k", i["odd_pe_k_2"][0]), ("pe_v", i["odd_pe_v_2"][0])):
        put(name, v.reshape(16, P).T)
    wk2 = i["odd_wk2_2"][0].reshape(2, P, DH).transpose(1, 0, 2)
    put("wk2", np.concatenate([wk2, wk2], 2))
    put("wv2", i["odd_wv2_2"][0].reshape(2, P, DH).transpose(1, 0, 2))
    r = np.arange(P)
    put("ident", np.eye(P, dtype=f))
    put("ones", np.ones((P, P), f))
    put("neg_tri", np.where(r[:, None] >= r[None, :], -1.0, 0.0))
    put("neg_ones", -np.ones((P, P), f))
    put("pick127", np.repeat((r == 127)[:, None], P, 1))
    put("pick15", np.repeat((r == 15)[:, None], P, 1))
    put("mask_sl", r[:, None] <= r[None, :])
    put("hidden", np.where(r[None, :] <= r[:, None], -BIG, 0.0))
    put("eps", np.full((P, 1), EPS))
    put("gn_eps", np.full((P, 1), GN_EPS))
    slopes = (2.0 ** (-8.0 * (np.arange(NH) + 1) / NH)).astype(f)
    put("slopes", np.broadcast_to(slopes, (P, NH)))
    sigma = np.arange(512) - 384
    seen = sigma[None, :] <= r[:, None]
    put("alibi", np.where(seen, sigma[None, :] - r[:, None], -BIG))
    put("causal", np.where(seen, 0.0, -BIG))
    t = r[:, None, None] + P * np.arange(4)[None, :, None]
    c_end = 16 * np.arange(CB)[None, None, :] + 31
    ok = (c_end <= t) & (np.arange(CB) < N_CMP)[None, None, :]
    put("cmp_seen", ok.astype(f))
    tab = np.zeros((P, N_TABLES), f)
    lg = np.log(1.0 - 2.0 ** (-5.0 - np.arange(RETH)))
    tau = np.arange(512)[None, None, :] - r[:, None, None]
    dec = np.where(tau >= 0, np.exp(lg[None, :, None] * np.maximum(tau, 0)), 0.0).astype(f) * f(DH ** -0.5)
    tab[:, 0:RETH * 512] = dec.reshape(P, -1)
    bias = np.where(ok[:, None], -slopes[None, :, None, None] * (t - c_end).astype(f)[:, None], f(-BIG))
    tab[:, RETH * 512:] = bias.reshape(P, -1)
    x = np.concatenate([i["meta_tokens"], i["x"][0]], 0)
    xT = x.T.reshape(KD, P, L).transpose(1, 0, 2).reshape(P, KD * L)
    c = np.ascontiguousarray
    return {"x_in": c(xT), "stream": c(stream), "down": c(down), "params": par, "tables": tab}


def kernel(**inputs):
    import concourse.bacc as bacc
    from concourse.bass_utils import run_bass_kernel_spmd

    nc = bacc.Bacc("TRN2", target_bir_lowering=False, num_devices=1)
    arrays = pack({k: np.asarray(v) for k, v in inputs.items()})
    aps = [nc.dram_tensor(n, arrays[n].shape, F32, kind="ExternalInput").ap()
           for n in ("x_in", "stream", "down", "params", "tables")]
    out = nc.dram_tensor("out", (P, KD * S), F32, kind="ExternalOutput").ap()
    build(nc, *aps, out)
    got = run_bass_kernel_spmd(nc, [arrays], core_ids=[0]).results[0]["out"]
    return got.reshape(P, KD, S).transpose(2, 1, 0).reshape(1, S, D)
```
